# Optimizing a Trainium2 kernel written in Bass

```python
import jax, jax.numpy as jnp
from jax import lax
import numpy as np

D_MODEL = 1024
BATCH = 1
SEQ = 512
DEPTH = 1
DEC_BATCH = 1
DEC_SEQ = 32
PAST_LEN = 1024

CHUNK = 64
EPS = 1e-6
N_MOD = 6
RWKV_HEAD_DIM = 64
RWKV_DIM = D_MODEL
RWKV_HEADS = RWKV_DIM // RWKV_HEAD_DIM
DECAY_LORA = 64
AAA_LORA = 64
GATE_LORA = 128
RWKV_PROJ = 3 * RWKV_DIM + DECAY_LORA + AAA_LORA + GATE_LORA
LN_X_EPS = 64e-5
GLA_HEADS = 4
GLA_DK_TOTAL = D_MODEL // 2
GLA_DV_TOTAL = D_MODEL
GLA_DK = GLA_DK_TOTAL // GLA_HEADS
GLA_DV = GLA_DV_TOTAL // GLA_HEADS
GLA_GATE_RANK = 16
GLA_GATE_NORM = 16.0
GLA_PROJ = 2 * GLA_DK_TOTAL + 2 * GLA_DV_TOTAL + GLA_GATE_RANK
GATE_PROJ = 2 * D_MODEL
IN_PROJ = RWKV_PROJ + GLA_PROJ + GATE_PROJ
N_GROUPS = 4
EXPERTS_PER_GROUP = 8
N_EXPERTS = N_GROUPS * EXPERTS_PER_GROUP
TOP_K = 2
EXPERT_FF = 512

kernel_name = 'hybrid_rwkv7_gla_hmoe_stream_step'

def _rmsnorm(x, g):
    x32 = x.astype(jnp.float32)
    y = x32 * lax.rsqrt(jnp.mean(x32 * x32, axis=-1, keepdims=True) + EPS)
    return (y * g.astype(jnp.float32)).astype(x.dtype)

def _rwkv7(xr, s0, w0, decay_up, a0, aaa_up, gate_up, k_k, k_a, r_k, ln_g, ln_b):
    B, T, _ = xr.shape
    f32 = jnp.float32
    o1, o2, o3 = RWKV_DIM, 2 * RWKV_DIM, 3 * RWKV_DIM
    o4, o5 = o3 + DECAY_LORA, o3 + DECAY_LORA + AAA_LORA
    x32 = xr.astype(f32)
    r, k, v = x32[..., :o1], x32[..., o1:o2], x32[..., o2:o3]
    xw, xa, xg = x32[..., o3:o4], x32[..., o4:o5], x32[..., o5:]
    w_log = -jax.nn.softplus(-(w0.astype(f32) + jnp.tanh(xw) @ decay_up.astype(f32))) - 0.5
    decay = jnp.exp(-jnp.exp(w_log))
    a = jax.nn.sigmoid(a0.astype(f32) + xa @ aaa_up.astype(f32))
    g = jax.nn.sigmoid(xg) @ gate_up.astype(f32)
    hd = lambda t: t.reshape(B, T, RWKV_HEADS, RWKV_HEAD_DIM)
    kk = hd(k * k_k.astype(f32))
    kk = kk * lax.rsqrt(jnp.maximum(jnp.sum(kk * kk, axis=-1, keepdims=True), 1e-24))
    k = k * (1.0 + (a - 1.0) * k_a.astype(f32))
    r_h, k_h, v_h, w_h, a_h = hd(r), hd(k), hd(v), hd(decay), hd(a)
    tm = lambda t: jnp.transpose(t, (1, 0, 2, 3))

    def step(S, inp):
        r_t, k_t, v_t, w_t, kk_t, a_t = inp
        sa = jnp.einsum('bhij,bhj->bhi', S, -kk_t)
        S = S * w_t[:, :, None, :] + sa[..., None] * (kk_t * a_t)[:, :, None, :] + v_t[..., None] * k_t[:, :, None, :]
        return S, jnp.einsum('bhij,bhj->bhi', S, r_t)

    s_new, ys = lax.scan(step, s0.astype(f32), (tm(r_h), tm(k_h), tm(v_h), tm(w_h), tm(kk), tm(a_h)))
    y = jnp.transpose(ys, (1, 0, 2, 3))
    mu = jnp.mean(y, axis=-1, keepdims=True)
    var = jnp.mean(jnp.square(y - mu), axis=-1, keepdims=True)
    yn = ((y - mu) * lax.rsqrt(var + LN_X_EPS)).reshape(B, T, RWKV_DIM) * ln_g.astype(f32) + ln_b.astype(f32)
    bonus = (jnp.sum(r_h * k_h * r_k.astype(f32), axis=-1, keepdims=True) * v_h).reshape(B, T, RWKV_DIM)
    out = (yn + bonus) * g
    return out.astype(xr.dtype), s_new.astype(s0.dtype)

def _gla(xg, s0, alpha_up, alpha_b, norm_g):
    B, T, _ = xg.shape
    f32 = jnp.float32
    o1, o2, o3, o4 = GLA_DK_TOTAL, 2 * GLA_DK_TOTAL, 2 * GLA_DK_TOTAL + GLA_DV_TOTAL, 2 * GLA_DK_TOTAL + GLA_DV_TOTAL + GLA_GATE_RANK
    x32 = xg.astype(f32)
    q = x32[..., :o1] * GLA_DK ** -0.5
    k, v, xa, r = x32[..., o1:o2], x32[..., o2:o3], x32[..., o3:o4], x32[..., o4:]
    log_alpha = jax.nn.log_sigmoid(xa @ alpha_up.astype(f32) + alpha_b.astype(f32)) / GLA_GATE_NORM
    C = min(CHUNK, T)
    n = T // C

    def to_chunks(t):
        return t.reshape(B, n, C, GLA_HEADS, -1).transpose(1, 0, 3, 2, 4)

    mask = jnp.tril(jnp.ones((C, C), dtype=bool))[None, None, :, :, None]

    def chunk_step(S, inp):
        q_c, k_c, v_c, g_c = inp
        b = jnp.cumsum(g_c, axis=2)
        dmat = jnp.exp(jnp.where(mask, b[:, :, :, None, :] - b[:, :, None, :, :], -jnp.inf))
        att = jnp.einsum('bhtd,bhtsd,bhsd->bhts', q_c, dmat, k_c)
        o = jnp.einsum('bhts,bhsv->bhtv', att, v_c) + jnp.einsum('bhtd,bhdv->bhtv', q_c * jnp.exp(b), S)
        b_last = b[:, :, -1:, :]
        S = jnp.exp(b_last[:, :, 0, :])[..., None] * S + jnp.einsum('bhsd,bhsv->bhdv', k_c * jnp.exp(b_last - b), v_c)
        return S, o

    s_new, o = lax.scan(chunk_step, s0.astype(f32), (to_chunks(q), to_chunks(k), to_chunks(v), to_chunks(log_alpha)))
    o = o.transpose(1, 0, 3, 2, 4).reshape(B, T, GLA_HEADS, GLA_DV)
    o = o * lax.rsqrt(jnp.mean(o * o, axis=-1, keepdims=True) + EPS) * norm_g.astype(f32)
    out = o.reshape(B, T, GLA_DV_TOTAL) * jax.nn.silu(r)
    return out.astype(xg.dtype), s_new.astype(s0.dtype)

def _hier_moe(h, router_group, router_expert, e_gate, e_up, e_down):
    B, T, D = h.shape
    ht = h.reshape(B * T, D)
    f32 = jnp.float32
    group_logits = (ht @ router_group).astype(f32)
    p_group = jax.nn.softmax(group_logits, axis=-1)
    _, g_idx = lax.top_k(group_logits, 1)
    p_g = jnp.take_along_axis(p_group, g_idx, axis=-1)
    expert_logits = (ht @ router_expert).astype(f32).reshape(-1, N_GROUPS, EXPERTS_PER_GROUP)
    within = jnp.take_along_axis(expert_logits, g_idx[:, :, None], axis=1)[:, 0]
    top_vals, top_idx = lax.top_k(within, TOP_K)
    w_top = jax.nn.softmax(top_vals, axis=-1) * p_g
    expert_ids = g_idx * EXPERTS_PER_GROUP + top_idx
    combine = jnp.sum(jax.nn.one_hot(expert_ids, N_EXPERTS, dtype=f32) * w_top[..., None], axis=1).astype(h.dtype)
    out = jnp.zeros_like(ht)
    for e in range(N_EXPERTS):
        hid = jax.nn.silu(ht @ e_gate[e]) * (ht @ e_up[e])
        out = out + combine[:, e:e + 1] * (hid @ e_down[e])
    return out.reshape(B, T, D)

def _layer(x, c, shift_prev, s_rwkv, s_gla, lw):
    (w_ada, b_ada, norm1_g, w_in, rwkv_mu, rwkv_w0, rwkv_decay_up, rwkv_a0, rwkv_aaa_up, rwkv_gate_up,
     rwkv_k_k, rwkv_k_a, rwkv_r_k, rwkv_ln_g, rwkv_ln_b, gla_alpha_up, gla_alpha_b, gla_norm_g,
     w_branch_rwkv, w_branch_gla, w_out, norm2_g, router_group, router_expert,
     expert_w_gate, expert_w_up, expert_w_down) = lw
    mod = (jax.nn.silu(c) @ w_ada + b_ada)[:, None, :]
    sh1, sc1, gt1, sh2, sc2, gt2 = jnp.split(mod, N_MOD, axis=-1)
    h = _rmsnorm(x, norm1_g) * (1.0 + sc1) + sh1
    proj = h @ w_in
    p_rwkv = proj[..., :RWKV_PROJ]
    p_gla = proj[..., RWKV_PROJ:RWKV_PROJ + GLA_PROJ]
    gate_r, gate_g = jnp.split(jax.nn.sigmoid(proj[..., RWKV_PROJ + GLA_PROJ:]), 2, axis=-1)
    prev = jnp.concatenate([shift_prev, p_rwkv[:, :-1]], axis=1)
    x_rwkv = p_rwkv + (prev - p_rwkv) * rwkv_mu
    y_r, s_rwkv_new = _rwkv7(x_rwkv, s_rwkv, rwkv_w0, rwkv_decay_up, rwkv_a0, rwkv_aaa_up, rwkv_gate_up,
                             rwkv_k_k, rwkv_k_a, rwkv_r_k, rwkv_ln_g, rwkv_ln_b)
    y_g, s_gla_new = _gla(p_gla, s_gla, gla_alpha_up, gla_alpha_b, gla_norm_g)
    merged = gate_r * (y_r @ w_branch_rwkv) + gate_g * (y_g @ w_branch_gla)
    x = x + gt1 * (merged @ w_out)
    h2 = _rmsnorm(x, norm2_g) * (1.0 + sc2) + sh2
    x = x + gt2 * _hier_moe(h2, router_group, router_expert, expert_w_gate, expert_w_up, expert_w_down)
    return x, p_rwkv[:, -1:], s_rwkv_new, s_gla_new

def _trunk(x, c, shift0, srwkv0, sgla0, weights, final_norm_g):
    shifts, srs, sgs = [], [], []
    for l in range(DEPTH):
        lw = tuple(w[l] for w in weights)
        x, sh, sr, sg = _layer(x, c, shift0[l], srwkv0[l], sgla0[l], lw)
        shifts.append(sh)
        srs.append(sr)
        sgs.append(sg)
    return _rmsnorm(x, final_norm_g), jnp.stack(shifts), jnp.stack(srs), jnp.stack(sgs)

def setup_inputs(seed: int = 0) -> dict:
    key = jax.random.key(seed)
    ks = iter(jax.random.split(key, 40))
    nrm = lambda shape, s: jax.random.normal(next(ks), shape, jnp.float32) * s
    L = DEPTH
    d = {}
    d['x_prompt'] = nrm((BATCH, SEQ, D_MODEL), 1.0)
    d['x_sample'] = nrm((DEC_BATCH, DEC_SEQ, D_MODEL), 1.0)
    d['c_prompt'] = nrm((BATCH, D_MODEL), 1.0)
    d['c_sample'] = nrm((DEC_BATCH, D_MODEL), 1.0)
    d['state_rwkv_shift'] = nrm((L, DEC_BATCH, 1, RWKV_PROJ), 1.0)
    d['state_rwkv'] = nrm((L, DEC_BATCH, RWKV_HEADS, RWKV_HEAD_DIM, RWKV_HEAD_DIM), 0.5)
    d['state_gla'] = nrm((L, DEC_BATCH, GLA_HEADS, GLA_DK, GLA_DV), 0.5)
    d['w_ada'] = nrm((L, D_MODEL, N_MOD * D_MODEL), 0.5 * D_MODEL ** -0.5)
    d['b_ada'] = nrm((L, N_MOD * D_MODEL), 0.01)
    d['norm1_g'] = 1.0 + nrm((L, D_MODEL), 0.02)
    d['w_in'] = nrm((L, D_MODEL, IN_PROJ), D_MODEL ** -0.5)
    d['rwkv_mu'] = jax.random.uniform(next(ks), (L, RWKV_PROJ), jnp.float32)
    d['rwkv_w0'] = nrm((L, RWKV_DIM), 0.5)
    d['rwkv_decay_up'] = nrm((L, DECAY_LORA, RWKV_DIM), 0.3 * DECAY_LORA ** -0.5)
    d['rwkv_a0'] = nrm((L, RWKV_DIM), 0.1)
    d['rwkv_aaa_up'] = nrm((L, AAA_LORA, RWKV_DIM), 0.3 * AAA_LORA ** -0.5)
    d['rwkv_gate_up'] = nrm((L, GATE_LORA, RWKV_DIM), GATE_LORA ** -0.5)
    d['rwkv_k_k'] = 0.85 + nrm((L, RWKV_DIM), 0.02)
    d['rwkv_k_a'] = 1.0 + nrm((L, RWKV_DIM), 0.02)
    d['rwkv_r_k'] = nrm((L, RWKV_HEADS, RWKV_HEAD_DIM), 0.1)
    d['rwkv_ln_g'] = 1.0 + nrm((L, RWKV_DIM), 0.02)
    d['rwkv_ln_b'] = nrm((L, RWKV_DIM), 0.01)
    d['gla_alpha_up'] = nrm((L, GLA_GATE_RANK, GLA_DK_TOTAL), GLA_GATE_RANK ** -0.5)
    d['gla_alpha_b'] = nrm((L, GLA_DK_TOTAL), 0.1)
    d['gla_norm_g'] = 1.0 + nrm((L, GLA_DV), 0.02)
    d['w_branch_rwkv'] = nrm((L, RWKV_DIM, D_MODEL), RWKV_DIM ** -0.5)
    d['w_branch_gla'] = nrm((L, GLA_DV_TOTAL, D_MODEL), GLA_DV_TOTAL ** -0.5)
    d['w_out'] = nrm((L, D_MODEL, D_MODEL), D_MODEL ** -0.5)
    d['norm2_g'] = 1.0 + nrm((L, D_MODEL), 0.02)
    d['router_group'] = nrm((L, D_MODEL, N_GROUPS), D_MODEL ** -0.5)
    d['router_expert'] = nrm((L, D_MODEL, N_EXPERTS), D_MODEL ** -0.5)
    d['expert_w_gate'] = nrm((L, N_EXPERTS, D_MODEL, EXPERT_FF), D_MODEL ** -0.5)
    d['expert_w_up'] = nrm((L, N_EXPERTS, D_MODEL, EXPERT_FF), D_MODEL ** -0.5)
    d['expert_w_down'] = nrm((L, N_EXPERTS, EXPERT_FF, D_MODEL), EXPERT_FF ** -0.5)
    d['final_norm_g'] = 1.0 + nrm((D_MODEL,), 0.02)
    return d

def reference(x_prompt, x_sample, c_prompt, c_sample, state_rwkv_shift, state_rwkv, state_gla,
              w_ada, b_ada, norm1_g, w_in, rwkv_mu, rwkv_w0, rwkv_decay_up, rwkv_a0, rwkv_aaa_up,
              rwkv_gate_up, rwkv_k_k, rwkv_k_a, rwkv_r_k, rwkv_ln_g, rwkv_ln_b, gla_alpha_up, gla_alpha_b,
              gla_norm_g, w_branch_rwkv, w_branch_gla, w_out, norm2_g, router_group, router_expert,
              expert_w_gate, expert_w_up, expert_w_down, final_norm_g):
    weights = (w_ada, b_ada, norm1_g, w_in, rwkv_mu, rwkv_w0, rwkv_decay_up, rwkv_a0, rwkv_aaa_up,
               rwkv_gate_up, rwkv_k_k, rwkv_k_a, rwkv_r_k, rwkv_ln_g, rwkv_ln_b, gla_alpha_up, gla_alpha_b,
               gla_norm_g, w_branch_rwkv, w_branch_gla, w_out, norm2_g, router_group, router_expert,
               expert_w_gate, expert_w_up, expert_w_down)
    Bp = x_prompt.shape[0]
    dt = x_prompt.dtype
    shift0 = jnp.zeros((DEPTH, Bp, 1, RWKV_PROJ), dt)
    srwkv0 = jnp.zeros((DEPTH, Bp, RWKV_HEADS, RWKV_HEAD_DIM, RWKV_HEAD_DIM), state_rwkv.dtype)
    sgla0 = jnp.zeros((DEPTH, Bp, GLA_HEADS, GLA_DK, GLA_DV), state_gla.dtype)
    y_prompt, p_shift, p_rwkv, p_gla = _trunk(x_prompt, c_prompt, shift0, srwkv0, sgla0, weights, final_norm_g)
    y_sample, s_shift, s_rwkv, s_gla = _trunk(x_sample, c_sample, state_rwkv_shift, state_rwkv, state_gla, weights, final_norm_g)
    return (y_prompt, y_sample, p_shift, p_rwkv, p_gla, s_shift, s_rwkv, s_gla)


_drawn_inputs = setup_inputs


def setup_inputs(seed=0):
    import zlib

    import numpy as np

    out = dict(_drawn_inputs(seed))
    spreads = {}
    factors = {'state_rwkv_shift': 4.042,
     'state_rwkv': 3.022,
     'rwkv_k_k': 8.0,
     'rwkv_ln_g': 8.0,
     'rwkv_ln_b': 8.0,
     'gla_norm_g': 8.0,
     'norm2_g': 3.208,
     'final_norm_g': 2.854}
    for name, (base, spread) in spreads.items():
        noise = np.random.default_rng([zlib.crc32(name.encode()), seed]).standard_normal(out[name].shape)
        drawn = base * np.exp(spread * noise) if base else spread * noise
        out[name] = __import__('jax').numpy.asarray(drawn.astype(out[name].dtype))
    for name, factor in factors.items():
        out[name] = (out[name] * factor).astype(out[name].dtype)
    return out
```

```python
from contextlib import ExitStack

import concourse.bass as bass
from concourse import mybir

F32 = mybir.dt.float32
U32 = mybir.dt.uint32
I32 = mybir.dt.int32
F32R = mybir.dt.float32r
ALU = mybir.AluOpType
ACT = mybir.ActivationFunctionType
AX = mybir.AxisListType

P = 128
D = 1024
KD = D // P
SEQ, DEC = 512, 32
T = SEQ + DEC
HALF = T // 2
CH = 64
NCH = SEQ // CH
TP = (NCH + 1) * CH
TILES = [(0, 128), (1, 128), (2, 128), (3, 128), (4, DEC)]
RW_TILES = 26
GL_TILES = 16
GT_TILES = 24
RWKV_PROJ = 3328
GLA_PROJ = 3088
GATE_RANK = 16
XA_COL = RWKV_PROJ + 2048
DECAY_SCALE = -0.6065306597126334
EPS = 1e-6
LN_X_EPS = 64e-5


def ds(start, size):
    return bass.ds(start, size)


def build(nc, I, O):
    ctx = ExitStack()
    with ctx:
        live = []

        def sem(name):
            live.append(nc.alloc_semaphore(name))
            return live[-1]

        def clear_semaphores():
            nc.clear_and_free_semaphores(list(live))
            live.clear()
            nc.all_engine_barrier()

        def scratch(name, shape):
            return nc.dram_tensor(name, shape, F32, kind="Internal").ap()

        ARENA, LOWER = 52992, 23232
        lower = ctx.enter_context(nc.sbuf_tensor("lower", [P, LOWER], F32))
        upper = {"scope": ExitStack()}
        ctx.callback(lambda: upper["scope"].close())

        def lay_out_upper(stage, n_r=0):
            upper["scope"].close()
            scope = ExitStack()
            upper["scope"] = scope
            upper["at"] = LOWER + n_r
            if n_r:
                upper["r"] = scope.enter_context(nc.sbuf_tensor(f"upper_r{stage}", [P, n_r], F32R))
            upper["f32"] = scope.enter_context(nc.sbuf_tensor(f"upper{stage}", [P, ARENA - LOWER - n_r], F32))

        def at_words(a, b):
            if b <= LOWER:
                return lower[:, a:b]
            if a < upper["at"]:
                return upper["r"][:, a - LOWER:b - LOWER]
            return upper["f32"][:, a - upper["at"]:b - upper["at"]]
        psum = [ctx.enter_context(nc.psum_tensor(f"bank{i}", [P, 2, 512], F32)) for i in range(4)]

        def bank(n):
            return psum[n // 2][:, n % 2, :]

        class Region:

            def __init__(self, at, end=ARENA):
                self.at, self.end = at, end

            def take(self, *dims):
                n = 1
                for d in dims:
                    n *= d
                if self.at < LOWER < self.at + n:
                    self.at = LOWER
                ap = at_words(self.at, self.at + n)
                self.at += n
                assert self.at <= self.end, (self.at, self.end)
                if len(dims) == 2:
                    ap = ap.rearrange("p (a b) -> p a b", a=dims[0])
                elif len(dims) == 3:
                    ap = ap.rearrange("p (a b c) -> p a b c", a=dims[0], b=dims[1])
                return ap

        base = 3648
        keep = Region(0, base)
        ident = keep.take(128)
        ones = keep.take(128)
        blk = keep.take(128)
        tri_c = keep.take(128)
        up_bd = keep.take(128)
        low_bd = keep.take(128)
        tri_w = keep.take(64)
        id_w = keep.take(64)
        sel2 = keep.take(2)
        vec = keep.take(128)
        mod_t = keep.take(48, 2)
        g1 = keep.take(8, 2)
        head_of = keep.take(KD, 16)
        of_head = keep.take(KD, 128)
        tri_g = keep.take(128)
        tri_bd = keep.take(128)
        VOFF = {}
        at = 0
        for name, n in (("mu", 26), ("shift", 26), ("norm1", 8), ("a0", 8), ("kk", 8), ("ka", 8), ("rk", 8),
                        ("lng", 8), ("lnb", 8), ("glan", 2)):
            VOFF[name] = (at, n)
            at += n
        NVEC = at

        def vcol(name, k):
            return vec[:, VOFF[name][0] + k:VOFF[name][0] + k + 1]

        def vcols(name):
            o, n = VOFF[name]
            return vec[:, o:o + n]

        mod_dram = scratch("mod_rows", (2, 6 * D))
        gla_dram = scratch("gla_qkv", (GL_TILES, P, T))
        gate_dram = scratch("gates", (GT_TILES, P, T))
        xa_dram = scratch("gla_xa", (GATE_RANK, T))
        xs_dram = scratch("expert_in", (32 * 64 + 2 * 5 * P, D))
        ys_dram = scratch("expert_out", (32 * 64, D))

        R = Region(base)
        p_rw = R.take(RW_TILES, TP)
        h_t = R.take(KD, TP)
        free_at = R.at

        lay_out_upper(1)
        S1 = Region(free_at)
        x_tok = S1.take(5, D)
        w_ada_s = [S1.take(KD, 512) for _ in range(3)]
        sq_junk = S1.take(D)
        S1b = Region(base, free_at - KD * TP)
        b_row = S1b.take(6 * D)
        parts = S1b.take(6 * D)
        c_row = S1b.take(D)
        c_sig = S1.take(D)
        c_t = S1.take(KD, 32)
        mod_row = S1.take(6 * D)
        vrow = keep.take(128)
        ssq = keep.take(8)
        rstd = keep.take(8)

        consts_done = sem("consts_done")
        pool_step = sem("pool_step")
        small_in = sem("small_in")
        x_in = sem("x_in")
        ada_in = [sem(f"ada_in{u}") for u in range(3)]
        ada_done = sem("ada_done")
        parts_done = sem("parts_done")
        c_sig_done = sem("c_sig_done")
        c_silu_done = sem("c_silu_done")
        c_tr = sem("c_tr")
        c_t_done = sem("c_t_done")
        vec_tr = sem("vec_tr")
        vec_done = sem("vec_done")
        row_mm = sem("row_mm")
        row_done = sem("row_done")
        modt_mm = sem("modt_mm")
        modt_done = sem("modt_done")
        g1_done = sem("g1_done")
        ssq_done = sem("ssq_done")
        ms_done = sem("ms_done")
        std_done = sem("std_done")
        rstd_done = sem("rstd_done")
        xn_done = sem("xn_done")
        x_tr = sem("x_tr")
        h_done = sem("h_done")
        v_step = sem("v_step")
        mod_out = sem("mod_out")
        zero_done = sem("zero_done")

        w_ada_v = I["w_ada"][0].rearrange("(k p) n -> p k n", p=P)
        with nc.Block() as block:
            @block.sync
            def _(sp):
                sp.dma_start(c_row[0:1, :], I["c_prompt"]).then_inc(small_in, 16)
                sp.dma_start(c_row[1:2, :], I["c_sample"]).then_inc(small_in, 16)
                for name, key in (("mu", "rwkv_mu"), ("norm1", "norm1_g"), ("a0", "rwkv_a0"), ("kk", "rwkv_k_k"),
                                  ("ka", "rwkv_k_a"), ("lng", "rwkv_ln_g"), ("lnb", "rwkv_ln_b"),
                                  ("glan", "gla_norm_g")):
                    o, n = VOFF[name]
                    sp.dma_start(vrow[o:o + n, :], I[key].rearrange("a (n p) -> (a n) p", p=P)).then_inc(small_in, 16)
                o, n = VOFF["rk"]
                sp.dma_start(vrow[o:o + n, :], I["rwkv_r_k"].rearrange("a (n h) d -> (a n) (h d)", h=2)
                             ).then_inc(small_in, 16)
                o, n = VOFF["shift"]
                sp.dma_start(vrow[o:o + n, :], I["state_rwkv_shift"].rearrange("a b c (n p) -> (a b c n) p", p=P)
                             ).then_inc(small_in, 16)
                sp.dma_start(b_row[0:1, :], I["b_ada"]).then_inc(small_in, 16)
                with sp.Fori(0, 4) as i:
                    for u in range(3):
                        sp.wait_ge(ada_done, 3 * i + (u + 1))
                        sp.dma_start(w_ada_s[u], w_ada_v[:, :, ds(i * 1536 + u * 512, 512)]).then_inc(ada_in[u], 16)

            @block.gpsimd
            def _(pool):
                pool.dma_start(x_tok[:, 0:4, :], I["x_prompt"][0].rearrange("(j p) d -> p j d", p=P)
                               ).then_inc(x_in, 16)
                pool.dma_start(x_tok[0:DEC, 4, :], I["x_sample"][0]).then_inc(x_in, 16)
                steps = [0]

                def step(ins):
                    ins.then_inc(pool_step, 1)
                    steps[0] += 1
                    pool.wait_ge(pool_step, steps[0])

                for t, v in ((ident, 0.0), (ones, 1.0), (blk, 0.0), (tri_c, 0.0), (tri_w, 1.0), (id_w, 0.0),
                             (sel2, 0.0)):
                    step(pool.memset(t, v))
                for h in (0, 64):
                    b = slice(h, h + 64)
                    step(pool.memset(blk[b, b], 1.0))
                    step(pool.memset(tri_c[b, b], DECAY_SCALE))
                    step(pool.affine_select(out=tri_w[b, :], in_=tri_w[b, :], compare_op=ALU.is_ge, fill=0.0,
                                            base=0, pattern=[[1, 64]], channel_multiplier=-1))
                    step(pool.affine_select(out=id_w[b, :], in_=id_w[b, :], compare_op=ALU.not_equal,
                                            fill=1.0, base=0, pattern=[[1, 64]], channel_multiplier=-1))
                for g in range(4):
                    b = slice(32 * g, 32 * g + 32)
                    step(pool.affine_select(out=sel2[b, :], in_=sel2[b, :], compare_op=ALU.not_equal, fill=1.0,
                                            base=0, pattern=[[1, 2]], channel_multiplier=-1))
                step(pool.affine_select(out=ident, in_=ident, compare_op=ALU.not_equal, fill=1.0, base=0,
                                        pattern=[[1, 128]], channel_multiplier=-1))
                step(pool.affine_select(out=tri_c, in_=tri_c, compare_op=ALU.is_ge, fill=0.0, base=0,
                                        pattern=[[1, 128]], channel_multiplier=-1))
                step(pool.affine_select(out=up_bd, in_=blk, compare_op=ALU.is_gt, fill=0.0, base=0,
                                        pattern=[[1, 128]], channel_multiplier=-1))
                step(pool.affine_select(out=low_bd, in_=blk, compare_op=ALU.is_gt, fill=0.0, base=0,
                                        pattern=[[-1, 128]], channel_multiplier=1))
                step(pool.affine_select(out=tri_bd, in_=blk, compare_op=ALU.is_ge, fill=0.0, base=0,
                                        pattern=[[1, 128]], channel_multiplier=-1))
                step(pool.tensor_scalar(tri_g, tri_bd, 1.0 / 16, None, ALU.mult))
                step(pool.memset(head_of, 0.0))
                step(pool.memset(of_head[0:16], 0.0))
                for h in range(2):
                    b = slice(64 * h, 64 * h + 64)
                    step(pool.affine_select(out=head_of[b], in_=head_of[b], compare_op=ALU.not_equal, fill=1.0,
                                            base=-h, pattern=[[-2, KD], [1, 16]], channel_multiplier=0))
                    step(pool.affine_select(out=of_head[0:16, :, b], in_=of_head[0:16, :, b],
                                            compare_op=ALU.not_equal, fill=1.0, base=-h,
                                            pattern=[[-2, KD], [0, 64]], channel_multiplier=1))
                pool.sem_inc(consts_done, 1)
                pool.memset(h_t[:, :, T:TP], 0.0).then_inc(zero_done, 1)
                pool.wait_ge(row_done, 12)
                pool.dma_start(mod_dram, mod_row[0:2, :]).then_inc(mod_out, 16)
                pool.wait_ge(mod_out, 16)

            @block.scalar
            def _(act):
                act.wait_ge(small_in, 16 * 13)
                nc.scalar.activation(c_sig[0:2, :], c_row[0:2, :], ACT.Sigmoid).then_inc(c_sig_done, 1)
                act.sem_inc(parts_done, 3)
                act.wait_ge(x_in, 32)
                for j, n in TILES:
                    if j:
                        act.wait_ge(ssq_done, j)
                    nc.scalar.activation(sq_junk[0:n, :], x_tok[0:n, j, :], ACT.Square,
                                         accum_out=ssq[0:n, j:j + 1]).then_inc(ssq_done, 1)
                act.wait_ge(ms_done, 2)
                for b, c in ((slice(0, P), slice(0, 4)), (slice(0, DEC), slice(4, 5))):
                    nc.scalar.activation(rstd[b, c], rstd[b, c], ACT.Sqrt).then_inc(std_done, 1)
                with act.Fori(0, 4) as i:
                    for u in range(3):
                        act.wait_ge(ada_done, 3 * i + (u + 4))
                        nc.scalar.activation(parts[:, ds(i * 1536 + u * 512, 512)], bank(u), ACT.Copy
                                             ).then_inc(parts_done, 1)

            @block.tensor
            def _(pe):
                pe.sem_inc(ada_done, 3)
                pe.wait_ge(consts_done, 1)
                pe.wait_ge(small_in, 16 * 13)
                nc.tensor.transpose(bank(6)[:, 0:NVEC], vrow[0:NVEC, :], ident[0:NVEC, 0:NVEC]).then_inc(vec_tr, 1)
                pe.wait_ge(c_silu_done, 1)
                for k in range(KD):
                    t = nc.tensor.transpose(bank(7)[:, 2 * k:2 * k + 2], c_row[0:2, k * P:(k + 1) * P],
                                            ident[0:2, 0:2])
                t.then_inc(c_tr, 1)
                pe.wait_ge(c_t_done, 1)
                with pe.Fori(0, 4) as i:
                    for u in range(3):
                        pe.wait_ge(ada_in[u], 16 * i + 16)
                        pe.wait_ge(parts_done, 3 * i + (u + 1))
                        for k in range(KD):
                            g = k % 4
                            m = nc.tensor.matmul(bank(u)[32 * g:32 * g + 32, :], c_t[:, k, :], w_ada_s[u][:, k, :],
                                                 start=k < 4, stop=k >= 4)
                        m.then_inc(ada_done, 1)
                pe.wait_ge(parts_done, 15)
                for n in range(12):
                    if n >= 2:
                        pe.wait_ge(row_done, n - 1)
                    o = bank(3 + n % 2)[0:2, :]
                    nc.tensor.matmul(o, sel2, parts[:, n * 512:(n + 1) * 512], start=True, stop=False)
                    nc.tensor.matmul(o, ones[0:1, 0:2], b_row[0:1, n * 512:(n + 1) * 512], start=False, stop=True
                                     ).then_inc(row_mm, 1)
                pe.wait_ge(row_done, 12)
                for n in range(48):
                    m = nc.tensor.matmul(bank(5)[:, 2 * n:2 * n + 2], mod_row[0:2, n * P:(n + 1) * P],
                                         ident[0:2, 0:2], start=True, stop=True)
                m.then_inc(modt_mm, 1)
                for k in range(KD):
                    if k == 0:
                        pe.wait_ge(xn_done, 5)
                    if k >= 2:
                        pe.wait_ge(h_done, k - 1)
                    for j in range(4):
                        t = nc.tensor.transpose(bank(6 + k % 2)[:, j * P:(j + 1) * P],
                                                x_tok[:, j, k * P:(k + 1) * P], ident)
                    t.then_inc(x_tr, 1)
                for k in range(KD):
                    t = nc.tensor.transpose(bank(2)[:, k * DEC:(k + 1) * DEC], x_tok[0:DEC, 4, k * P:(k + 1) * P],
                                            ident[0:DEC, 0:DEC])
                t.then_inc(x_tr, 1)

            @block.vector
            def _(v):
                v.memset(c_t, 0.0).then_inc(v_step, 1)
                v.wait_ge(c_sig_done, 1)
                nc.vector.tensor_tensor(c_row[0:2, :], c_row[0:2, :], c_sig[0:2, :], ALU.mult
                                        ).then_inc(c_silu_done, 1)
                v.wait_ge(vec_tr, 1)
                nc.vector.tensor_copy(vec[:, 0:NVEC], bank(6)[:, 0:NVEC]).then_inc(vec_done, 1)
                v.wait_ge(c_tr, 1)
                v.wait_ge(v_step, 1)
                nc.vector.tensor_copy(c_t[:, :, 0:2], bank(7)[:, 0:16].rearrange("p (k s) -> p k s", s=2)
                                      ).then_inc(c_t_done, 1)
                v.wait_ge(ssq_done, 5)
                for b, c in ((slice(0, P), slice(0, 4)), (slice(0, DEC), slice(4, 5))):
                    nc.vector.tensor_scalar(rstd[b, c], ssq[b, c], 1.0 / D, EPS, ALU.mult, ALU.add
                                            ).then_inc(ms_done, 1)
                v.wait_ge(std_done, 2)
                for b, c in ((slice(0, P), slice(0, 4)), (slice(0, DEC), slice(4, 5))):
                    nc.vector.reciprocal(rstd[b, c], rstd[b, c]).then_inc(rstd_done, 1)
                v.wait_ge(rstd_done, 2)
                for j, n in TILES:
                    nc.vector.tensor_scalar(x_tok[0:n, j, :], x_tok[0:n, j, :], rstd[0:n, j:j + 1], None, ALU.mult
                                            ).then_inc(xn_done, 1)
                for n in range(12):
                    v.wait_ge(row_mm, n + 1)
                    nc.vector.tensor_copy(mod_row[0:2, n * 512:(n + 1) * 512], bank(3 + n % 2)[0:2, :]
                                          ).then_inc(row_done, 1)
                v.wait_ge(modt_mm, 1)
                nc.vector.tensor_copy(mod_t, bank(5)[:, 0:96].rearrange("p (n s) -> p n s", s=2)
                                      ).then_inc(modt_done, 1)
                v.wait_ge(modt_done, 1)
                v.wait_ge(vec_done, 1)
                for s in range(2):
                    nc.vector.scalar_tensor_tensor(out=g1[:, :, s], in0=mod_t[:, 8:16, s], scalar=1.0,
                                                   in1=vcols("norm1"), op0=ALU.add, op1=ALU.mult
                                                   ).then_inc(g1_done, 1)
                v.wait_ge(g1_done, 2)
                for k in range(KD):
                    v.wait_ge(x_tr, k + 1)
                    nc.vector.tensor_scalar(h_t[:, k, 0:SEQ], bank(6 + k % 2), g1[:, k, 0:1],
                                            mod_t[:, k, 0:1], ALU.mult, ALU.add).then_inc(h_done, 1)
                v.wait_ge(x_tr, KD + 1)
                for k in range(KD):
                    nc.vector.tensor_scalar(h_t[:, k, SEQ:T], bank(2)[:, k * DEC:(k + 1) * DEC], g1[:, k, 1:2],
                                            mod_t[:, k, 1:2], ALU.mult, ALU.add).then_inc(h_done, 1)
                v.wait_ge(h_done, 16)

        R_WORDS = 4 * KD * 2 * P + 2 * KD * T
        lay_out_upper(2, R_WORDS)
        S2r = Region(free_at)
        S2 = Region(free_at + R_WORDS)
        w_slot = [S2.take(KD, 2 * P) for _ in range(2)]
        w_high = [S2r.take(KD, 2 * P) for _ in range(2)]
        w_rest = [S2r.take(KD, 2 * P) for _ in range(2)]
        h_high = S2r.take(KD, T)
        h_rest = S2r.take(KD, T)
        stage = [S2.take(2, T) for _ in range(2)]
        xa_w = S2.take(KD, GATE_RANK)
        xa_t = S2.take(T)
        zero_row = S2.take(D)
        w_in_v = I["w_in"][0].rearrange("(k p) n -> p k n", p=P)
        w_loaded = [sem(f"w_loaded{s}") for s in range(2)]
        h_high_done = sem("h_high_done")
        h_split = sem("h_split")
        w_high_done = sem("w_high_done")
        w_split = sem("w_split")
        proj_done = sem("proj_done")
        act_out = sem("act_out")
        dve_out = sem("dve_out")
        spilled = [sem(f"spilled{s}") for s in range(2)]
        xa_in = sem("xa_in")
        xa_done = sem("xa_done")
        xa_out = sem("xa_out")
        pad_done = sem("pad_done")
        xs_zero = sem("xs_zero")

        RUNS = [(0, 13, 0, "rw"), (13, 8, RWKV_PROJ, "gla"), (21, 12, XA_COL + GATE_RANK, "gate")]
        PAIRS = sum(n for _, n, _, _ in RUNS)

        def runs(eng, step):
            for first, n, col, kind in RUNS:
                odd = n % 2
                last = 2 if first + n == PAIRS else 0

                def pair(i, u):
                    q = u + odd + 2 * i
                    step(first + q, (first + odd + u) % 2, col + q * 2 * P, q, kind,
                         (first + odd + u) // 2 + i)
                if odd:
                    step(first, first % 2, col, 0, kind, first // 2)
                with eng.Fori(0, (n - last) // 2) as i:
                    for u in range(2):
                        pair(i, u)
                for u in range(last):
                    pair((n - last) // 2, u)

        def is_last(g):
            return isinstance(g, int) and g == PAIRS - 1

        with nc.Block() as block:
            @block.sync
            def _(sp):
                sp.dma_start(xa_w, w_in_v[:, :, XA_COL:XA_COL + GATE_RANK]).then_inc(xa_in, 16)

                def load(g, s, col, local, kind, use):
                    sp.wait_ge(w_split, g + 1)
                    sp.dma_start(w_slot[s], w_in_v[:, :, ds(col, 2 * P)]).then_inc(w_loaded[s], 16)
                runs(sp, load)

            @block.gpsimd
            def _(pool):
                pool.memset(p_rw[:, :, T:TP], 0.0).then_inc(pad_done, 1)
                pool.memset(zero_row, 0.0).then_inc(pad_done, 1)
                pool.wait_ge(pad_done, 2)
                pool.dma_start(xs_dram[0:32 * 64].rearrange("(n p) d -> p n d", p=P),
                               zero_row.unsqueeze(1).broadcast_to([P, 16, D])).then_inc(xs_zero, 16)
                pool.wait_ge(xs_zero, 16)
                pool.wait_ge(xa_done, 2)
                pool.dma_start(xa_dram, xa_t[0:GATE_RANK, :]).then_inc(xa_out, 16)
                pool.wait_ge(xa_out, 16)
                for s in range(2):
                    pool.wait_ge(spilled[s], 16 * 11)

            @block.tensor
            def _(pe):
                pe.sem_inc(proj_done, 4)

                def project(g, s, col, local, kind, use):
                    pe.wait_ge(w_split, g + 3)
                    for h in range(2):
                        pe.wait_ge(act_out if h == 0 else dve_out, g + 1)
                        for k in range(KD):
                            for w_part, h_part in ((w_high, h_high), (w_high, h_rest), (w_rest, h_high)):
                                for c in range(2):
                                    m = nc.tensor.matmul(psum[2 * s + h][:, c, 0:HALF],
                                                         w_part[s][:, k, h * P:(h + 1) * P],
                                                         h_part[:, k, c * HALF:(c + 1) * HALF],
                                                         start=k == 0 and w_part is w_high and h_part is h_high,
                                                         stop=k == KD - 1 and w_part is w_rest)
                        m.then_inc(proj_done, 1)
                pe.wait_ge(h_split, KD)
                runs(pe, project)
                pe.wait_ge(xa_in, 16)
                pe.wait_ge(act_out, 35)
                for k in range(KD):
                    for c in range(2):
                        m = nc.tensor.matmul(psum[0][0:GATE_RANK, c, 0:HALF], xa_w[:, k, :],
                                             h_t[:, k, c * HALF:(c + 1) * HALF], start=k == 0, stop=k == KD - 1)
                m.then_inc(xa_done, 1)

            def two(ap):
                return ap.rearrange("p (c t) -> p c t", c=2)

            @block.scalar
            def _(act):
                act.sem_inc(act_out, 2)
                act.sem_inc(spilled[0], 16)
                act.sem_inc(spilled[1], 16)

                def split(n, s, use):
                    act.wait_ge(w_loaded[s], 16 * use + 16)
                    act.wait_ge(proj_done, 2 * n + 2)
                    nc.scalar.activation(w_high[s], w_slot[s], ACT.Copy).then_inc(w_high_done, 1)

                for k in range(KD):
                    nc.scalar.activation(h_high[:, k, :], h_t[:, k, 0:T], ACT.Copy).then_inc(h_high_done, 1)
                split(0, 0, 0)

                def out(g, s, col, local, kind, use):
                    if not is_last(g):
                        split(g + 1, 1 - s, use + s)
                    act.wait_ge(proj_done, 2 * g + 5)
                    if kind != "rw":
                        act.wait_ge(spilled[s], 16 * (use - (6 if s == 1 else 7)) + 16)
                    dst = p_rw[:, ds(local * 2, 1), 0:T] if kind == "rw" else stage[s][:, 0:1, :]
                    nc.scalar.activation(dst.rearrange("p a (c t) -> p (a c) t", c=2), psum[2 * s][:, :, 0:HALF], ACT.Copy
                                         ).then_inc(act_out, 1)
                    if kind != "rw":
                        act.wait_ge(act_out, g + 3)
                        act.wait_ge(dve_out, g + 3)
                        dst = gla_dram if kind == "gla" else gate_dram
                        act.dma_start(dst[ds(local * 2, 2), :, :].rearrange("h p t -> p h t"), stage[s]
                                      ).then_inc(spilled[s], 16)
                runs(act, out)

            @block.vector
            def _(v):
                v.sem_inc(dve_out, 2)
                v.sem_inc(w_split, 2)

                def split(n, s):
                    v.wait_ge(w_high_done, n + 1)
                    nc.vector.tensor_tensor(w_rest[s], w_slot[s], w_high[s].bitcast(F32), ALU.subtract).then_inc(w_split, 1)

                for k in range(KD):
                    v.wait_ge(h_high_done, k + 1)
                    nc.vector.tensor_tensor(h_rest[:, k, :], h_t[:, k, 0:T], h_high[:, k, :].bitcast(F32), ALU.subtract
                                            ).then_inc(h_split, 1)
                split(0, 0)

                def out(g, s, col, local, kind, use):
                    if not is_last(g):
                        split(g + 1, 1 - s)
                    v.wait_ge(proj_done, 2 * g + 6)
                    if kind != "rw":
                        v.wait_ge(spilled[s], 16 * (use - (6 if s == 1 else 7)) + 16)
                    dst = p_rw[:, ds(local * 2 + 1, 1), 0:T] if kind == "rw" else stage[s][:, 1:2, :]
                    nc.vector.tensor_copy(dst.rearrange("p a (c t) -> p (a c) t", c=2), psum[2 * s + 1][:, :, 0:HALF]
                                          ).then_inc(dve_out, 1)
                runs(v, out)
                v.wait_ge(xa_done, 1)
                nc.vector.tensor_copy(two(xa_t[0:GATE_RANK, :]), psum[0][0:GATE_RANK, :, 0:HALF]).then_inc(xa_done, 1)

        lay_out_upper(3)
        S3 = Region(free_at)
        ka = S3.take(KD, TP)
        lam = S3.take(KD, TP)
        chunk_at = S3.at
        kk = h_t
        diff = S3.take(KD, T)
        std = S3.take(T)
        boost = S3.take(KD, T)
        sig_w = S3.take(5, D)
        w_up = S3.take(D)
        w0_row = S3.take(D)
        omka = keep.take(8)
        ends = keep.take(52)
        ends_t = keep.take(128)
        lora_in = sem("lora_in")
        ends_done = sem("ends_done")
        ends_tr = sem("ends_tr")
        ends_t_done = sem("ends_t_done")
        ends_out = sem("ends_out")
        diff_step = sem("diff_step")
        mixed = sem("mixed")
        omka_done = sem("omka_done")
        tanh_done = sem("tanh_done")
        w_mm = sem("w_mm")
        sig_w_done = sem("sig_w_done")
        a_mm = sem("a_mm")
        a_done = sem("a_done")
        boost_done = sem("boost_done")
        kk_scaled = sem("kk_scaled")
        kk_sq = sem("kk_sq")
        kk_sum = sem("kk_sum")
        kk_clamped = sem("kk_clamped")
        kk_std = sem("kk_std")
        kk_rstd = sem("kk_rstd")
        kk_wide = sem("kk_wide")
        kk_done = sem("kk_done")
        k_done = sem("k_done")
        ka_done = sem("ka_done")
        cum_mm = sem("cum_mm")
        lam_done = sem("lam_done")
        pads3 = sem("pads3")
        MIX = [(24, 26), (8, 16), (0, 8), (16, 24)]

        def halves(ap):
            return ap.rearrange("p (c t) -> p c t", c=2)

        with nc.Block() as block:
            @block.sync
            def _(sp):
                sp.dma_start(w_up[0:64, :], I["rwkv_decay_up"][0]).then_inc(lora_in, 16)
                sp.dma_start(w_up[64:128, :], I["rwkv_aaa_up"][0]).then_inc(lora_in, 16)
                sp.dma_start(w0_row[0:1, :], I["rwkv_w0"]).then_inc(lora_in, 16)
                sp.wait_ge(ends_t_done, 1)
                for s, o in ((0, O[2]), (1, O[5])):
                    sp.dma_start(o.rearrange("a b c (n p) -> (a b c n) p", p=P), ends_t[26 * s:26 * s + 26, :]
                                 ).then_inc(ends_out, 16)
                sp.wait_ge(ends_out, 32)

            @block.vector
            def _(v):
                for s, t in ((0, SEQ - 1), (1, T - 1)):
                    nc.vector.tensor_copy(ends[:, 26 * s:26 * s + 26], p_rw[:, :, t]).then_inc(ends_done, 1)
                nc.vector.tensor_scalar(omka, vcols("ka"), -1.0, 1.0, ALU.mult, ALU.add).then_inc(omka_done, 1)
                v.wait_ge(ends_done, 2)
                n = d = 0
                for a, b in MIX:
                    m = b - a
                    if d:
                        v.wait_ge(mixed, n)
                    nc.vector.tensor_tensor(diff[:, 0:m, 1:T], p_rw[:, a:b, 0:T - 1], p_rw[:, a:b, 1:T],
                                            ALU.subtract).then_inc(diff_step, 1)
                    nc.vector.tensor_scalar(diff[:, 0:m, 0:1], p_rw[:, a:b, 0:1], -1.0, None, ALU.mult
                                            ).then_inc(diff_step, 1)
                    d += 1
                    v.wait_ge(diff_step, 3 * d - 1)
                    o = VOFF["shift"][0]
                    nc.vector.tensor_tensor(diff[:, 0:m, SEQ], vec[:, o + a:o + b], p_rw[:, a:b, SEQ], ALU.subtract
                                            ).then_inc(diff_step, 1)
                    v.wait_ge(diff_step, 3 * d)
                    for f in range(a, b):
                        nc.vector.scalar_tensor_tensor(out=p_rw[:, f, 0:T], in0=diff[:, f - a, :],
                                                       scalar=vcol("mu", f), in1=p_rw[:, f, 0:T], op0=ALU.mult,
                                                       op1=ALU.add).then_inc(mixed, 1)
                        n += 1
                    if a == 8:
                        for k in range(KD):
                            v.wait_ge(mixed, 2 + k + 1)
                            nc.vector.tensor_scalar(kk[:, k, :], p_rw[:, 8 + k, :], vcol("kk", k), None, ALU.mult
                                                    ).then_inc(kk_scaled, 1)
                v.wait_ge(ends_tr, 1)
                nc.vector.tensor_copy(ends_t[0:52, :], bank(7)[0:52, 0:128]).then_inc(ends_t_done, 1)
                v.wait_ge(kk_sum, 1)
                nc.vector.tensor_scalar(halves(std[0:16]), psum[2][0:16, :, 0:HALF], 1e-24, None, ALU.max
                                        ).then_inc(kk_clamped, 1)
                v.wait_ge(kk_std, 1)
                nc.vector.reciprocal(std[0:16], std[0:16]).then_inc(kk_rstd, 1)
                for k in range(KD):
                    v.wait_ge(kk_wide, k + 1)
                    nc.vector.tensor_tensor(halves(kk[:, k, 0:T]), halves(kk[:, k, 0:T]),
                                            psum[2 + k % 2][:, :, 0:HALF], ALU.mult).then_inc(kk_done, 1)

            @block.gpsimd
            def _(pool):
                pool.memset(ka[:, :, T:TP], 0.0).then_inc(pads3, 1)
                for k in range(KD):
                    pool.wait_ge(boost_done, k + 1)
                    pool.wait_ge(kk_scaled, k + 1)
                    pool.tensor_tensor(p_rw[:, 8 + k, 0:T], p_rw[:, 8 + k, 0:T], boost[:, k, :], ALU.mult
                                       ).then_inc(k_done, 1)
                for k in range(KD):
                    pool.wait_ge(kk_done, k + 1)
                    pool.tensor_tensor(ka[:, k, 0:T], ka[:, k, 0:T], kk[:, k, 0:T], ALU.mult).then_inc(ka_done, 1)
                pool.wait_ge(ka_done, KD)

            @block.scalar
            def _(act):
                act.wait_ge(mixed, 2)
                nc.scalar.activation(p_rw[0:64, 24, 0:T], p_rw[0:64, 24, 0:T], ACT.Tanh).then_inc(tanh_done, 1)
                nc.scalar.activation(p_rw[:, 25, 0:T], p_rw[:, 25, 0:T], ACT.Sigmoid).then_inc(tanh_done, 1)
                q = 0
                for j, n in TILES:
                    for c in range(2):
                        act.wait_ge(w_mm, q + 1)
                        nc.scalar.activation(sig_w[0:n, j, c * 512:(c + 1) * 512], bank(q % 2)[0:n, :], ACT.Sigmoid
                                             ).then_inc(sig_w_done, 1)
                        q += 1
                act.wait_ge(omka_done, 1)
                for k in range(KD):
                    act.wait_ge(a_mm, k + 1)
                    nc.scalar.activation(halves(ka[:, k, 0:T]), psum[1 + k % 2][:, :, 0:HALF], ACT.Sigmoid,
                                         bias=vcol("a0", k)).then_inc(a_done, 1)
                    act.wait_ge(a_done, k + 1)
                    nc.scalar.activation(boost[:, k, :], ka[:, k, 0:T], ACT.Identity, scale=vcol("ka", k),
                                         bias=omka[:, k:k + 1]).then_inc(boost_done, 1)
                act.wait_ge(mixed, RW_TILES)
                for k in range(KD):
                    nc.scalar.activation(diff[:, k, :], kk[:, k, 0:T], ACT.Square).then_inc(kk_sq, 1)
                for k in range(KD):
                    act.wait_ge(cum_mm, k + 1)
                    nc.scalar.activation(lam[:, k, 0:SEQ], bank(k % 2), ACT.Copy).then_inc(lam_done, 1)
                act.wait_ge(cum_mm, KD + 1)
                nc.scalar.activation(lam[:, :, SEQ:TP], bank(2).rearrange("p (k t) -> p k t", t=CH), ACT.Copy
                                     ).then_inc(lam_done, 1)
                act.wait_ge(kk_clamped, 1)
                nc.scalar.activation(std[0:16], std[0:16], ACT.Sqrt).then_inc(kk_std, 1)

            @block.tensor
            def _(pe):
                pe.wait_ge(ends_done, 2)
                nc.tensor.transpose(bank(7)[0:52, 0:128], ends, ident).then_inc(ends_tr, 1)
                pe.wait_ge(lora_in, 48)
                pe.wait_ge(tanh_done, 1)
                q = 0
                for j, n in TILES:
                    for c in range(2):
                        if q >= 2:
                            pe.wait_ge(sig_w_done, q - 1)
                        o = bank(q % 2)[0:n, :]
                        nc.tensor.matmul(o, p_rw[0:64, 24, j * P:j * P + n], w_up[0:64, c * 512:(c + 1) * 512],
                                         start=True, stop=False)
                        nc.tensor.matmul(o, ones[0:1, 0:n], w0_row[0:1, c * 512:(c + 1) * 512], start=False, stop=True
                                         ).then_inc(w_mm, 1)
                        q += 1
                for k in range(KD):
                    if k >= 2:
                        pe.wait_ge(a_done, k - 1)
                    for c in range(2):
                        m = nc.tensor.matmul(psum[1 + k % 2][:, c, 0:HALF], w_up[64:128, k * P:(k + 1) * P],
                                             p_rw[64:128, 24, c * HALF:(c + 1) * HALF], start=True, stop=True)
                    m.then_inc(a_mm, 1)
                pe.wait_ge(sig_w_done, 10)
                pe.wait_ge(a_done, KD)
                for k in range(KD):
                    if k >= 2:
                        pe.wait_ge(lam_done, k - 1)
                    for j in range(4):
                        m = nc.tensor.matmul(bank(k % 2)[:, j * P:(j + 1) * P], sig_w[:, j, k * P:(k + 1) * P], tri_c,
                                             start=True, stop=True)
                    m.then_inc(cum_mm, 1)
                for k in range(KD):
                    m = nc.tensor.matmul(bank(2)[:, k * CH:(k + 1) * CH], sig_w[0:DEC, 4, k * P:(k + 1) * P],
                                         tri_c[0:DEC, 0:CH], start=True, stop=True)
                m.then_inc(cum_mm, 1)
                pe.wait_ge(ends_t_done, 1)
                for k in range(KD):
                    pe.wait_ge(kk_sq, k + 1)
                    for c in range(2):
                        m = nc.tensor.matmul(psum[2][0:16, c, 0:HALF], head_of[:, k, :],
                                             diff[:, k, c * HALF:(c + 1) * HALF], start=k == 0, stop=k == KD - 1)
                m.then_inc(kk_sum, 1)
                pe.wait_ge(kk_rstd, 1)
                for k in range(KD):
                    if k >= 2:
                        pe.wait_ge(kk_done, k - 1)
                    for c in range(2):
                        m = nc.tensor.matmul(psum[2 + k % 2][:, c, 0:HALF], of_head[0:16, k, :],
                                             std[0:16, c * HALF:(c + 1) * HALF], start=True, stop=True)
                    m.then_inc(kk_wide, 1)

        clear_semaphores()
        S4 = Region(chunk_at)
        ar = S4.take(8, 192)
        beta = S4.take(8, P)
        kap = S4.take(8, P)
        v_bdt = S4.take(8, P)
        pw = [S4.take(8, P) for _ in range(2)]
        ptt = [S4.take(8, 192) for _ in range(2)]
        inv_t = S4.take(8, P)
        m_t = S4.take(8, P)
        qb = S4.take(8, CH)
        qk = S4.take(8, CH)
        v_bd = S4.take(8, P)
        beta_s = S4.take(8, P)
        kap_s = S4.take(8, P)
        u0 = S4.take(8, P)
        u_bd = S4.take(8, P)
        s_bd = S4.take(8, P)
        lam_c = S4.take(8, CH)
        lam_i = S4.take(8, CH)
        lam_end = S4.take(8)
        rk_r = u0[:, 0:4].rearrange("p j n -> p (j n)").rearrange("p (j n) -> p j n", n=CH)
        s_tmp = pw[0]
        st_io = pw[0]
        st_c = ptt[0].rearrange("p j n -> p (j n)")[:, 0:8 * CH].rearrange("p (j n) -> p j n", n=CH)

        STEPS = ["NT", "MT", "N", "TR", "TV", "1a", "1b", "2a", "2b", "3a", "3b", "4a", "4b", "5a", "5b", "6",
                 "U0", "U", "Y", "S"]
        OUTS = {"NT": 2, "MT": 2, "TR": 2, "TV": 2, "2a": 2, "3a": 2, "4a": 2, "6": 2}
        UNITS = [(step, g) for step in STEPS for g in range(2)]
        NU = len(UNITS)
        PER = [sum(OUTS.get(st, 1) for st, _ in UNITS[s::4]) for s in range(4)]

        def unit(step, g):
            return UNITS.index((step, g))

        def copied(n):
            return sum(OUTS.get(st, 1) for st, _ in UNITS[n % 4:n + 1:4])

        units_done = sem("units_done")
        emptied = [sem(f"emptied{s}") for s in range(4)]
        lam_c_done = sem("lam_c_done")
        prep_done = sem("prep_done")
        rk_step = sem("rk_step")
        tt_done = sem("tt_done")
        lam_end_done = sem("lam_end_done")
        s_done = sem("s_done")
        zeroed = sem("zeroed")
        NPREP = 12
        def wait_unit(eng, c, step, g):
            eng.wait_ge(units_done, c * NU + (unit(step, g) + 2))

        def wait_copied(eng, c, step, g):
            n = unit(step, g)
            eng.wait_ge(emptied[n % 4], c * PER[n % 4] + (copied(n) + 1))

        def wait_banks(eng, c, step, g, *sources):
            n = unit(step, g)
            counts = {n % 4: copied(n) - OUTS.get(step, 1)}
            for source in sources:
                m = unit(source, g)
                counts[m % 4] = max(counts.get(m % 4, 0), copied(m))
            for s, count in counts.items():
                eng.wait_ge(emptied[s], c * PER[s] + (count + 1))

        def quads(ap, g):
            return ap[:, 4 * g:4 * g + 4]

        def wide(s):
            return psum[s][:, :, 0:384].rearrange("p b (q n) -> p b q n", n=192)

        def by22(ap, g, a, b):
            return ap[:, 4 * g:4 * g + 4, a:b].rearrange("p (b q) n -> p b q n", b=2)

        def mask22(m, n):
            return m.unsqueeze(1).unsqueeze(1).broadcast_to([P, 2, 2, n])

        HALVES = [(slice(0, 64), slice(0, 64)), (slice(64, 128), slice(64, 128))]

        def chunks(eng, body, which):
            if which == "prompt":
                with eng.Fori(0, NCH) as c:
                    body(c, True)
            else:
                body(NCH, False)

        def rwkv_chunks(which):
            with nc.Block() as block:
                @block.scalar
                def _(act):
                    if which == "prompt":
                        for s in range(4):
                            act.sem_inc(emptied[s], 1)
                        act.wait_ge(zeroed, 5)

                    def decays(c):
                        nc.scalar.activation(lam_c, lam[:, :, ds(c * CH, CH)], ACT.Exp).then_inc(lam_c_done, 1)
                        nc.scalar.activation(lam_i, lam[:, :, ds(c * CH, CH)], ACT.Exp, scale=-1.0
                                             ).then_inc(lam_c_done, 1)

                    def values(c):
                        for p, h in HALVES:
                            nc.scalar.activation(v_bdt[p, :, h], p_rw[p, 16:24, ds(c * CH, CH)], ACT.Copy
                                                 ).then_inc(prep_done, 1)

                    if which == "prompt":
                        decays(0)
                        values(0)

                    def chunk(c, more):
                        t0 = c * CH
                        for step, g in UNITS:
                            n = unit(step, g)
                            s = n % 4
                            if step in ("NT", "MT", "N", "6", "S", "1a", "2a", "3a", "4a", "5a"):
                                continue
                            wait_unit(act, c, step, g)
                            if more and (step, g) == ("3b", 0):
                                act.wait_ge(lam_end_done, c + 1)
                                act.wait_ge(prep_done, c * NPREP + NPREP)
                                decays(c + 1)
                            if more and (step, g) == ("5b", 0):
                                values(c + 1)
                            if step == "TR":
                                for b, dst in ((0, beta_s), (1, kap_s)):
                                    nc.scalar.activation(quads(dst, g), psum[s][:, b, :].rearrange(
                                        "p (q n) -> p q n", n=P), ACT.Copy).then_inc(emptied[s], 1)
                            elif step == "TV":
                                nc.scalar.activation(quads(v_bd, g), psum[s][:, 0, :].rearrange(
                                    "p (q n) -> p q n", n=P), ACT.Copy).then_inc(emptied[s], 1)
                            elif step in ("1b", "2b", "3b", "4b", "5b"):
                                nc.scalar.activation(quads(pw[int(step[0]) % 2], g), psum[s][:, 0, :].rearrange(
                                    "p (q n) -> p q n", n=P), ACT.Copy).then_inc(emptied[s], 1)
                            elif step == "U0":
                                nc.scalar.activation(quads(u0, g), psum[s][:, 0, :].rearrange(
                                    "p (q n) -> p q n", n=P), ACT.Copy).then_inc(emptied[s], 1)
                            elif step == "U":
                                nc.scalar.activation(quads(u_bd, g), psum[s][:, 0, :].rearrange(
                                    "p (q n) -> p q n", n=P), ACT.Copy).then_inc(emptied[s], 1)
                            elif step == "Y":
                                nc.scalar.activation(p_rw[:, 4 * g:4 * g + 4, ds(t0, CH)],
                                                     psum[s][:, 0, 0:256].rearrange("p (q n) -> p q n", n=CH),
                                                     ACT.Copy).then_inc(emptied[s], 1)
                    chunks(act, chunk, which)

                @block.vector
                def _(v):
                    if which == "prompt":
                        v.memset(s_bd, 0.0).then_inc(s_done, 2)
                        for t in (ar, beta):
                            v.memset(t, 0.0).then_inc(zeroed, 1)
                        v.wait_ge(zeroed, 5)
                        v.wait_ge(s_done, 2)

                    def keys(c):
                        t0 = c * CH
                        v.wait_ge(lam_c_done, c * 2 + 2)
                        for p, h in HALVES:
                            nc.vector.tensor_tensor(beta[p, :, h], ka[p, :, ds(t0, CH)], lam_i[p, :, :], ALU.mult
                                                    ).then_inc(prep_done, 1)
                            nc.vector.tensor_tensor(kap[p, :, h], p_rw[p, 8:16, ds(t0, CH)], lam_i[p, :, :], ALU.mult
                                                    ).then_inc(prep_done, 1)

                    def bonus(c):
                        t0 = c * CH
                        nc.vector.tensor_tensor(rk_r, p_rw[:, 0:8, ds(t0, CH)], p_rw[:, 8:16, ds(t0, CH)], ALU.mult
                                                ).then_inc(rk_step, 1)
                        v.wait_ge(rk_step, c + 1)
                        nc.vector.tensor_tensor(rk_r, rk_r, vcols("rk").unsqueeze(2).broadcast_to([P, 8, CH]),
                                                ALU.mult).then_inc(prep_done, 1)

                    def queries(c):
                        t0 = c * CH
                        for p, h in HALVES:
                            nc.vector.tensor_scalar(ar[p, :, h.start:h.start + 1], kk[p, :, ds(t0, 1)], -1.0, None,
                                                    ALU.mult).then_inc(prep_done, 1)
                            nc.vector.scalar_tensor_tensor(out=ar[p, :, h.start + 1:h.stop],
                                                           in0=kk[p, :, ds(t0 + 1, CH - 1)], scalar=-1.0,
                                                           in1=lam_c[p, :, 0:CH - 1], op0=ALU.mult, op1=ALU.mult
                                                           ).then_inc(prep_done, 1)
                        nc.vector.tensor_tensor(ar[:, :, P:192], p_rw[:, 0:8, ds(t0, CH)], lam_c, ALU.mult
                                                ).then_inc(prep_done, 1)

                    if which == "prompt":
                        keys(0)
                        bonus(0)
                        queries(0)

                    def chunk(c, more):
                        t0 = c * CH
                        v.wait_ge(lam_c_done, c * 2 + 2)
                        v.wait_ge(s_done, c * 2 + 2)
                        nc.vector.tensor_copy(lam_end, lam_c[:, :, CH - 1]).then_inc(lam_end_done, 1)
                        for step, g in UNITS:
                            n = unit(step, g)
                            s = n % 4
                            if step in ("TR", "U0", "U", "Y", "1b", "2b", "3b", "4b", "5b"):
                                continue
                            if more and (step, g) == ("5a", 0):
                                keys(c + 1)
                            if more and (step, g) == ("S", 0):
                                wait_unit(v, c, "U", 1)
                                bonus(c + 1)
                                wait_unit(v, c, "Y", 1)
                                queries(c + 1)
                            wait_unit(v, c, step, g)
                            if step in ("NT", "MT"):
                                bd, low = (ptt[0], qb) if step == "NT" else (m_t, qk)
                                nc.vector.tensor_tensor(by22(bd, g, 0, P), wide(s)[:, :, :, 0:P], mask22(up_bd, P),
                                                        ALU.mult).then_inc(emptied[s], 1)
                                nc.vector.tensor_tensor(by22(low, g, 0, CH), wide(s)[:, :, :, P:192],
                                                        mask22(tri_w, CH), ALU.mult).then_inc(emptied[s], 1)
                            elif step == "N":
                                nc.vector.tensor_tensor(quads(pw[0], g), psum[s][:, 0, :].rearrange(
                                    "p (q n) -> p q n", n=P), low_bd.unsqueeze(1).broadcast_to([P, 4, P]), ALU.mult
                                    ).then_inc(emptied[s], 1)
                            elif step == "TV":
                                nc.vector.tensor_tensor(p_rw[:, 16 + 4 * g:20 + 4 * g, ds(t0, CH)],
                                                        p_rw[:, 16 + 4 * g:20 + 4 * g, ds(t0, CH)],
                                                        psum[s][:, 1, 0:256].rearrange("p (q n) -> p q n", n=CH),
                                                        ALU.mult).then_inc(emptied[s], 1)
                            elif step == "1a":
                                nc.vector.tensor_copy(ptt[1][:, 4 * g:4 * g + 4, 0:P], psum[s][:, 0, :].rearrange(
                                    "p (q n) -> p q n", n=P)).then_inc(emptied[s], 1)
                            elif step in ("2a", "3a", "4a", "5a"):
                                k = int(step[0])
                                if k < 5:
                                    nc.vector.tensor_copy(by22(ptt[k % 2], g, 0, P), wide(s)[:, :, :, 0:P]
                                                          ).then_inc(emptied[s], 1)
                                if k == 2:
                                    v.wait_ge(tt_done, c * 4 + (2 * g + 2))
                                else:
                                    wait_copied(v, c, f"{k - 1}a", g)
                                nc.vector.tensor_tensor(by22(ptt[k % 2], g, P, 192), by22(ptt[1 - k % 2], g, P, 192),
                                                        wide(s)[:, :, :, P:192], ALU.add).then_inc(emptied[s], 1)
                            elif step == "6":
                                wait_copied(v, c, "5a", g)
                                for p, h in HALVES:
                                    nc.vector.tensor_tensor(inv_t[p, 4 * g:4 * g + 4, h],
                                                            ptt[1][p, 4 * g:4 * g + 4, P:192],
                                                            psum[s][p, 0, 0:256].rearrange("p (q n) -> p q n", n=CH),
                                                            ALU.add).then_inc(emptied[s], 1)
                            elif step == "S":
                                v.wait_ge(lam_end_done, c + 1)
                                nc.vector.tensor_tensor(quads(s_tmp, g), quads(s_bd, g),
                                                        psum[s][:, 0, :].rearrange("p (q n) -> p q n", n=P),
                                                        ALU.add).then_inc(emptied[s], 1)
                                wait_copied(v, c, "S", g)
                                nc.vector.tensor_tensor(quads(s_bd, g), quads(s_tmp, g),
                                                        lam_end[:, 4 * g:4 * g + 4].unsqueeze(2)
                                                        .broadcast_to([P, 4, P]), ALU.mult).then_inc(s_done, 1)
                    chunks(v, chunk, which)
                    v.wait_ge(s_done, 18 + (0 if which == "prompt" else 2))

                @block.gpsimd
                def _(pool):
                    if which == "prompt":
                        for t in (kap, v_bdt, inv_t):
                            pool.memset(t, 0.0).then_inc(zeroed, 1)
                        pool.wait_ge(zeroed, 5)

                    def chunk(c, more):
                        for g in range(2):
                            wait_copied(pool, c, "NT", g)
                            for p, h in HALVES:
                                pool.tensor_tensor(ptt[1][p, 4 * g:4 * g + 4, P:192], ptt[0][p, 4 * g:4 * g + 4, h],
                                                   id_w[p, :].unsqueeze(1).broadcast_to([64, 4, CH]), ALU.add
                                                   ).then_inc(tt_done, 1)
                    chunks(pool, chunk, which)

                @block.tensor
                def _(pe):
                    if which == "prompt":
                        pe.sem_inc(units_done, 1)
                        pe.wait_ge(zeroed, 5)

                    mm = nc.tensor.matmul

                    def chunk(c, more):
                        pe.wait_ge(prep_done, c * NPREP + NPREP)
                        for step, g in UNITS:
                            n = unit(step, g)
                            s = n % 4
                            k = int(step[0]) if step[0].isdigit() else 0
                            sources = {"U0": ("MT", "TV"), "U": ("6", "U0"), "Y": ("U",), "S": ("TR", "U")}.get(step, ())
                            if k == 1:
                                sources = ("NT", "N")
                            elif k:
                                sources = (f"{k - 1}a", f"{k - 1}b")
                            wait_banks(pe, c, step, g, *sources)
                            if k == 2:
                                pe.wait_ge(tt_done, c * 4 + (2 * g + 2))
                            if step == "U0":
                                pe.wait_ge(s_done, c * 2 + (g + 1))
                            if step == "TV":
                                mm(psum[s][:, 1, 0:256], blk, quads(rk_r, g), start=True, stop=True)
                            for q in range(4):
                                j = 4 * g + q
                                narrow = psum[s][:, 0, q * P:(q + 1) * P]
                                short = psum[s][:, 0, q * CH:(q + 1) * CH]
                                broad = wide(s)[:, q // 2, q % 2, :]
                                cur, pt = pw[(k + 1) % 2], ptt[(k + 1) % 2]
                                if step == "NT":
                                    m = mm(broad, beta[:, j, :], ar[:, j, :], start=True, stop=True)
                                elif step == "MT":
                                    m = mm(broad, kap[:, j, :], ar[:, j, :], start=True, stop=True)
                                elif step == "N":
                                    m = mm(narrow, ar[:, j, 0:P], beta[:, j, :], start=True, stop=True)
                                elif step == "TR":
                                    nc.tensor.transpose(narrow, beta[:, j, :], ident)
                                    m = nc.tensor.transpose(psum[s][:, 1, q * P:(q + 1) * P], kap[:, j, :], ident)
                                elif step == "TV":
                                    m = nc.tensor.transpose(narrow, v_bdt[:, j, :], ident)
                                elif step == "1a":
                                    m = mm(narrow, cur[:, j, :], pt[:, j, 0:P], start=True, stop=True)
                                elif step in ("2a", "3a", "4a"):
                                    m = mm(broad, cur[:, j, :], pt[:, j, :], start=True, stop=True)
                                elif step == "5a":
                                    m = mm(broad[:, P:192], cur[:, j, :], pt[:, j, P:192], start=True, stop=True)
                                elif step in ("1b", "2b", "3b", "4b", "5b"):
                                    m = mm(narrow, pt[:, j, 0:P], cur[:, j, :], start=True, stop=True)
                                elif step == "6":
                                    m = mm(short, cur[:, j, :], pt[:, j, P:192], start=True, stop=True)
                                elif step == "U0":
                                    mm(narrow, ar[:, j, 0:P], s_bd[:, j, :], start=True, stop=False)
                                    m = mm(narrow, m_t[:, j, :], v_bd[:, j, :], start=False, stop=True)
                                elif step == "U":
                                    m = mm(narrow, inv_t[:, j, :], u0[:, j, :], start=True, stop=True)
                                elif step == "Y":
                                    mm(short, s_bd[:, j, :], ar[:, j, P:192], start=True, stop=False)
                                    mm(short, u_bd[:, j, :], qb[:, j, :], start=False, stop=False)
                                    m = mm(short, v_bd[:, j, :], qk[:, j, :], start=False, stop=True)
                                elif step == "S":
                                    mm(narrow, beta_s[:, j, :], u_bd[:, j, :], start=True, stop=False)
                                    m = mm(narrow, kap_s[:, j, :], v_bd[:, j, :], start=False, stop=True)
                            m.then_inc(units_done, 1)
                    chunks(pe, chunk, which)

        st_in = sem("st_in")
        st_packed = [sem(f"st_packed{i}") for i in range(2)]
        st_tr = [sem(f"st_tr{i}") for i in range(2)]
        st_rows = [sem(f"st_rows{i}") for i in range(2)]
        st_out = sem("st_out")
        st_new_tr = sem("st_new_tr")
        st_bd = sem("st_bd")
        st_rows_out = st_io[0:64]
        st_rows_in = pw[1][0:64]

        def rwkv_state(n, out, load):
            with nc.Block() as block:
                @block.sync
                def _(sp):
                    if load is not None:
                        sp.dma_start(st_rows_in.rearrange("i j (h d) -> i (j h) d", h=2),
                                     load[0, 0].rearrange("h i d -> i h d")).then_inc(st_in, 16)
                    sp.wait_ge(st_rows[n], 2)
                    sp.dma_start(out[0, 0].rearrange("h i d -> i h d"),
                                 st_rows_out.rearrange("i j (h d) -> i (j h) d", h=2)).then_inc(st_out, 16)
                    sp.wait_ge(st_out, 16 * n + 16)

                @block.tensor
                def _(pe):
                    pe.wait_ge(st_packed[n], 2)
                    for j in range(8):
                        m = nc.tensor.transpose(psum[0][0:64, j // 4, (j % 4) * P:(j % 4 + 1) * P], st_c[:, j, :],
                                                ident)
                    m.then_inc(st_tr[n], 1)
                    if load is not None:
                        pe.wait_ge(st_in, 16)
                        for j in range(8):
                            m = nc.tensor.transpose(psum[1][:, 0, j * CH:(j + 1) * CH], st_rows_in[:, j, :],
                                                    ident[0:64, 0:64])
                        m.then_inc(st_new_tr, 1)

                @block.vector
                def _(v):
                    for p, h in HALVES:
                        nc.vector.tensor_copy(st_c[p], s_bd[p, :, h]).then_inc(st_packed[n], 1)
                    v.wait_ge(st_tr[n], 1)
                    for b in range(2):
                        nc.vector.tensor_copy(st_rows_out[:, 4 * b:4 * b + 4, :].rearrange("i q d -> i (q d)"),
                                              psum[0][0:64, b, :]).then_inc(st_rows[n], 1)
                    if load is not None:
                        v.wait_ge(st_new_tr, 1)
                        new = psum[1][:, 0, :].rearrange("p (j i) -> p j i", i=CH)
                        for p, h in HALVES:
                            nc.vector.tensor_copy(s_bd[p, :, h], new[p]).then_inc(st_bd, 1)
                        v.wait_ge(st_bd, 2)

        rwkv_chunks("prompt")
        rwkv_state(0, O[3], I["state_rwkv"])
        rwkv_chunks("sample")
        rwkv_state(1, O[6], None)
        y_r = p_rw[:, 0:8]
        S5 = Region(free_at)
        sq = S5.take(KD, T)
        gate_up = S5.take(D)
        head_mu = S5.take(T)
        head_rs = S5.take(T)
        gate_up_in = sem("gate_up_in")
        y_sum = sem("y_sum")
        mu_done = sem("mu_done")
        mu_wide = sem("mu_wide")
        y_centred = sem("y_centred")
        y_sq = sem("y_sq")
        y_sqsum = sem("y_sqsum")
        rs_step = sem("rs_step")
        rs_wide = sem("rs_wide")
        y_scaled = sem("y_scaled")
        y_affine = sem("y_affine")
        y_bonus = sem("y_bonus")
        gate_mm = sem("gate_mm")
        y_r_done = sem("y_r_done")

        def cols(ap, c):
            return ap[:, c * HALF:(c + 1) * HALF]

        with nc.Block() as block:
            @block.sync
            def _(sp):
                sp.dma_start(gate_up, I["rwkv_gate_up"][0]).then_inc(gate_up_in, 16)

            @block.tensor
            def _(pe):
                for k in range(KD):
                    for c in range(2):
                        m = nc.tensor.matmul(psum[0][0:16, c, 0:HALF], head_of[:, k, :], cols(y_r[:, k], c),
                                             start=k == 0, stop=k == KD - 1)
                m.then_inc(y_sum, 1)
                pe.wait_ge(mu_done, 1)
                for k in range(KD + 1):
                    if k < KD:
                        if k >= 2:
                            pe.wait_ge(y_centred, k - 1)
                        for c in range(2):
                            m = nc.tensor.matmul(psum[1 + k % 2][:, c, 0:HALF], of_head[0:16, k, :],
                                                 cols(head_mu[0:16], c), start=True, stop=True)
                        m.then_inc(mu_wide, 1)
                    if k:
                        pe.wait_ge(y_sq, k)
                        for c in range(2):
                            m = nc.tensor.matmul(psum[3][0:16, c, 0:HALF], head_of[:, k - 1, :], cols(sq[:, k - 1], c),
                                                 start=k == 1, stop=k == KD)
                m.then_inc(y_sqsum, 1)
                pe.wait_ge(gate_up_in, 16)
                pe.wait_ge(rs_step, 3)
                for k in range(KD):
                    if k >= 2:
                        pe.wait_ge(y_scaled, k - 1)
                    for c in range(2):
                        m = nc.tensor.matmul(psum[1 + k % 2][:, c, 0:HALF], of_head[0:16, k, :],
                                             cols(head_rs[0:16], c), start=True, stop=True)
                    m.then_inc(rs_wide, 1)
                    if k >= 2:
                        pe.wait_ge(y_r_done, k - 1)
                    for c in range(2):
                        m = nc.tensor.matmul(psum[3 * (k % 2)][:, c, 0:HALF], gate_up[:, k * P:(k + 1) * P],
                                             cols(p_rw[:, 25], c), start=True, stop=True)
                    m.then_inc(gate_mm, 1)

            @block.vector
            def _(v):
                v.wait_ge(y_sum, 1)
                nc.vector.tensor_scalar(halves(head_mu[0:16]), psum[0][0:16, :, 0:HALF], 1.0 / 64, None, ALU.mult
                                        ).then_inc(mu_done, 1)
                for k in range(KD):
                    v.wait_ge(mu_wide, k + 1)
                    nc.vector.tensor_tensor(halves(y_r[:, k, 0:T]), halves(y_r[:, k, 0:T]),
                                            psum[1 + k % 2][:, :, 0:HALF], ALU.subtract).then_inc(y_centred, 1)
                v.wait_ge(y_sqsum, 1)
                nc.vector.tensor_scalar(halves(head_rs[0:16]), psum[3][0:16, :, 0:HALF], 1.0 / 64, LN_X_EPS, ALU.mult,
                                        ALU.add).then_inc(rs_step, 1)
                v.wait_ge(rs_step, 2)
                nc.vector.reciprocal(head_rs[0:16], head_rs[0:16]).then_inc(rs_step, 1)
                for k in range(KD + 1):
                    if k < KD:
                        v.wait_ge(rs_wide, k + 1)
                        nc.vector.tensor_tensor(halves(y_r[:, k, 0:T]), halves(y_r[:, k, 0:T]),
                                                psum[1 + k % 2][:, :, 0:HALF], ALU.mult).then_inc(y_scaled, 1)
                    if k:
                        v.wait_ge(y_bonus, k)
                        v.wait_ge(gate_mm, k)
                        nc.vector.tensor_tensor(halves(y_r[:, k - 1, 0:T]), halves(y_r[:, k - 1, 0:T]),
                                                psum[3 * ((k - 1) % 2)][:, :, 0:HALF], ALU.mult).then_inc(y_r_done, 1)
                v.wait_ge(y_r_done, KD)

            @block.scalar
            def _(act):
                for k in range(KD):
                    act.wait_ge(y_centred, k + 1)
                    nc.scalar.activation(sq[:, k, :], y_r[:, k, 0:T], ACT.Square).then_inc(y_sq, 1)
                act.wait_ge(rs_step, 1)
                nc.scalar.activation(head_rs[0:16], head_rs[0:16], ACT.Sqrt).then_inc(rs_step, 1)
                for k in range(KD):
                    act.wait_ge(y_scaled, k + 1)
                    nc.scalar.activation(y_r[:, k, 0:T], y_r[:, k, 0:T], ACT.Identity, scale=vcol("lng", k),
                                         bias=vcol("lnb", k)).then_inc(y_affine, 1)

            @block.gpsimd
            def _(pool):
                for k in range(KD):
                    pool.wait_ge(y_affine, k + 1)
                    pool.tensor_tensor(y_r[:, k, 0:T], y_r[:, k, 0:T], p_rw[:, 16 + k, 0:T], ALU.add
                                       ).then_inc(y_bonus, 1)

        clear_semaphores()
        NG = 4
        DV = 256
        S6 = Region(base + 8 * TP)
        y_g_at = S6.at
        y_g = S6.take(8, T)
        qk = S6.take(8, TP)
        v_t = S6.take(8, TP)
        b_t = S6.take(NG, TP)
        b_mid = S6.take(NG, TP)
        xa = S6.take(T)
        alpha_up = S6.take(512)
        alpha_b = S6.take(512)
        z = S6.take(5, 512)
        ez = S6.take(5, 512)
        e_q = S6.take(NG, P)
        e_k = S6.take(NG, P)
        e_b = S6.take(NG, P)
        q_in = S6.take(NG, P)
        k_in = S6.take(NG, P)
        q_st = S6.take(NG, P)
        v_in = S6.take(8, P)
        k_tok = S6.take(NG, P)
        v_tok = S6.take(NG, DV)
        att = S6.take(NG, P)
        o_n = S6.take(NG, DV)
        o_sq = S6.take(NG, DV)
        kv_tmp = S6.take(NG, DV)
        o_ms = S6.take(NG)
        o_rs = S6.take(NG)
        st_g = [S6.take(NG, DV) for _ in range(2)]
        gla_in = sem("gla_in")
        st_g_in = sem("st_g_in")
        z_mm = sem("z_mm")
        z_min = sem("z_min")
        z_abs = sem("z_abs")
        z_exp = sem("z_exp")
        z_ln = sem("z_ln")
        z_done = sem("z_done")
        b_mm = sem("b_mm")
        b_done = sem("b_done")
        b_mid_done = sem("b_mid_done")
        gpads = sem("gpads")
        tile_free = sem("tile_free")
        g_exp = sem("g_exp")
        g_prep = sem("g_prep")
        g_turned = sem("g_turned")
        g_copied = sem("g_copied")
        g_att = sem("g_att")
        g_kv = sem("g_kv")
        kv_scaled = sem("kv_scaled")
        g_state = sem("g_state")
        g_o = sem("g_o")
        o_ssq = sem("o_ssq")
        o_mean = sem("o_mean")
        o_rstd = sem("o_rstd")
        o_done = sem("o_done")
        g_out = sem("g_out")
        y_g_out = sem("y_g_out")
        gla_st_out = sem("gla_st_out")
        GQ = 128.0 ** -0.5

        with nc.Block() as block:
            @block.sync
            def _(sp):
                sp.dma_start(xa[0:GATE_RANK, :], xa_dram).then_inc(gla_in, 16)
                sp.dma_start(alpha_up[0:GATE_RANK, :], I["gla_alpha_up"][0]).then_inc(gla_in, 16)
                sp.dma_start(alpha_b[0:1, :], I["gla_alpha_b"]).then_inc(gla_in, 16)
                sp.dma_start(qk[:, :, 0:T], gla_dram[0:8].rearrange("n p t -> p n t")).then_inc(gla_in, 16)
                sp.dma_start(v_t[:, :, 0:T], gla_dram[8:16].rearrange("n p t -> p n t")).then_inc(gla_in, 16)
                sp.dma_start(st_g[1], I["state_gla"][0, 0].rearrange("h k v -> k h v")).then_inc(st_g_in, 16)
                for s, out in ((0, O[4]), (1, O[7])):
                    sp.wait_ge(g_state, 4 + 4 * (8 + s))
                    sp.dma_start(out[0, 0].rearrange("h k v -> k h v"), st_g[s]).then_inc(gla_st_out, 16)
                sp.wait_ge(gla_st_out, 32)

            @block.gpsimd
            def _(pool):
                pool.memset(qk[:, :, T:TP], 0.0).then_inc(gpads, 1)
                pool.memset(v_t[:, :, T:TP], 0.0).then_inc(gpads, 1)
                pool.memset(st_g[0], 0.0).then_inc(gpads, 1)
                pool.wait_ge(gpads, 3)

            @block.tensor
            def _(pe):
                pe.wait_ge(gla_in, 80)
                for j, n in TILES:
                    if j >= 2:
                        pe.wait_ge(z_abs, j - 1)
                        pe.wait_ge(z_min, j - 1)
                    nc.tensor.matmul(bank(j % 2)[0:n, :], xa[0:GATE_RANK, j * P:j * P + n], alpha_up[0:GATE_RANK, :],
                                     start=True, stop=False)
                    nc.tensor.matmul(bank(j % 2)[0:n, :], ones[0:1, 0:n], alpha_b[0:1, :], start=False, stop=True
                                     ).then_inc(z_mm, 1)
                pe.wait_ge(z_done, 5)
                for h in range(NG):
                    if h >= 2:
                        pe.wait_ge(b_done, h - 1)
                    for j in range(4):
                        m = nc.tensor.matmul(bank(h % 2)[:, j * P:(j + 1) * P], z[:, j, h * P:(h + 1) * P], tri_g,
                                             start=True, stop=True)
                    m.then_inc(b_mm, 1)
                for h in range(NG):
                    m = nc.tensor.matmul(bank(2)[:, h * CH:(h + 1) * CH], z[0:DEC, 4, h * P:(h + 1) * P],
                                         tri_g[0:DEC, 0:CH], start=True, stop=True)
                m.then_inc(b_mm, 1)
                pe.wait_ge(b_done, NG + 1)

                def tile(i, w, st, chunks_in):
                    pe.wait_ge(g_prep, 4 * i + 4)
                    for n in range(8):
                        m = nc.tensor.transpose(psum[1][0:w, n // 4, (n % 4) * P:(n % 4 + 1) * P], v_in[:, n, 0:w],
                                                ident)
                    m.then_inc(g_turned, 1)
                    for h in range(NG):
                        m = nc.tensor.transpose(psum[0][0:w, 1, h * P:(h + 1) * P], k_in[:, h, 0:w], ident)
                    m.then_inc(g_turned, 1)
                    for h in range(NG):
                        m = nc.tensor.matmul(psum[0][0:w, 0, h * P:h * P + w], k_in[:, h, 0:w], q_in[:, h, 0:w],
                                             start=True, stop=True)
                    m.then_inc(g_turned, 1)
                    pe.wait_ge(g_att, i + 1)
                    pe.wait_ge(g_copied, 2 * i + 2)
                    for h in range(NG):
                        nc.tensor.matmul(psum[2][0:w, h // 2, (h % 2) * DV:(h % 2 + 1) * DV], att[0:w, h, 0:w],
                                         v_tok[0:w, h, :], start=h % 2 == 0, stop=False, skip_group_check=True)
                    for c in range(chunks_in):
                        r = slice(64 * c, 64 * c + 64)
                        pe.wait_ge(g_state, 8 * i + (4 * c + 4))
                        for h in range(NG):
                            m = nc.tensor.matmul(psum[2][r, h // 2, (h % 2) * DV:(h % 2 + 1) * DV], q_st[:, h, r],
                                                 st[:, h, :], start=False, stop=True, skip_group_check=True)
                        if c == chunks_in - 1:
                            m.then_inc(g_o, 1)
                        for h in range(NG):
                            m = nc.tensor.matmul(psum[3][:, h // 2, (h % 2) * DV:(h % 2 + 1) * DV], k_tok[r, h, :],
                                                 v_tok[r, h, :], start=True, stop=True)
                        m.then_inc(g_kv, 1)
                    pe.wait_ge(o_done, 4 * i + 4)
                    for n in range(8):
                        m = nc.tensor.transpose(psum[1][:, n // 4, (n % 4) * P:(n % 4) * P + w],
                                                o_n[0:w, n // 2, (n % 2) * P:(n % 2 + 1) * P], ident[0:w, 0:w])
                    m.then_inc(g_out, 1)
                with pe.Fori(0, 4) as i:
                    tile(i, P, st_g[0], 2)
                pe.wait_ge(st_g_in, 16)
                tile(4, CH, st_g[1], 1)

            @block.scalar
            def _(act):
                for j, n in TILES:
                    act.wait_ge(z_mm, j + 1)
                    act.wait_ge(z_min, j + 1)
                    nc.scalar.activation(ez[0:n, j, :], bank(j % 2)[0:n, :], ACT.Abs).then_inc(z_abs, 1)
                    act.wait_ge(z_abs, j + 1)
                    nc.scalar.activation(ez[0:n, j, :], ez[0:n, j, :], ACT.Exp, scale=-1.0).then_inc(z_exp, 1)
                for j, n in TILES:
                    act.wait_ge(z_exp, j + 1)
                    nc.scalar.activation(ez[0:n, j, :], ez[0:n, j, :], ACT.Ln, bias=1.0).then_inc(z_ln, 1)

                def tile(i, w):
                    act.wait_ge(tile_free, i + 1)
                    act.wait_ge(b_mid_done, 1)
                    t0 = i * P
                    nc.scalar.activation(e_q[:, :, 0:w], b_mid[:, :, ds(t0, w)], ACT.Exp).then_inc(g_exp, 1)
                    nc.scalar.activation(e_k[:, :, 0:w], b_mid[:, :, ds(t0, w)], ACT.Exp, scale=-1.0
                                         ).then_inc(g_exp, 1)
                    nc.scalar.activation(e_b[:, :, 0:w], b_t[:, :, ds(t0, w)], ACT.Exp).then_inc(g_exp, 1)
                    nc.scalar.activation(v_in[:, :, 0:w], v_t[:, :, ds(t0, w)], ACT.Copy).then_inc(g_prep, 1)
                    act.wait_ge(g_turned, 3 * i + 1)
                    nc.scalar.activation(v_tok[0:w].rearrange("t h v -> t (h v)"),
                                         psum[1][0:w].rearrange("t b v -> t (b v)"), ACT.Copy).then_inc(g_copied, 1)
                    act.wait_ge(g_turned, 3 * i + 2)
                    nc.scalar.activation(k_tok[0:w].rearrange("t h v -> t (h v)"), psum[0][0:w, 1, :], ACT.Copy
                                         ).then_inc(g_copied, 1)
                    act.wait_ge(g_o, i + 1)
                    for h in range(NG):
                        nc.scalar.activation(o_sq[0:w, h, :], psum[2][0:w, h // 2, (h % 2) * DV:(h % 2 + 1) * DV],
                                             ACT.Square, accum_out=o_ms[0:w, h:h + 1]).then_inc(o_ssq, 1)
                    act.wait_ge(o_mean, i + 1)
                    nc.scalar.activation(o_rs[0:w], o_rs[0:w], ACT.Ln).then_inc(o_rstd, 1)
                    act.wait_ge(o_rstd, 2 * i + 1)
                    nc.scalar.activation(o_rs[0:w], o_rs[0:w], ACT.Exp, scale=-0.5).then_inc(o_rstd, 1)
                    act.wait_ge(o_rstd, 2 * i + 2)
                    for h in range(NG):
                        nc.scalar.activation(o_n[0:w, h, :], psum[2][0:w, h // 2, (h % 2) * DV:(h % 2 + 1) * DV],
                                             ACT.Copy, scale=o_rs[0:w, h:h + 1]).then_inc(o_done, 1)
                act.wait_ge(gla_in, 80)
                act.wait_ge(gpads, 3)
                with act.Fori(0, 4) as i:
                    tile(i, P)
                tile(4, CH)

            @block.vector
            def _(v):
                v.sem_inc(tile_free, 1)
                for j, n in TILES:
                    v.wait_ge(z_mm, j + 1)
                    nc.vector.tensor_scalar(z[0:n, j, :], bank(j % 2)[0:n, :], 0.0, None, ALU.min).then_inc(z_min, 1)
                v.wait_ge(z_min, 5)
                for j, n in TILES:
                    v.wait_ge(z_ln, j + 1)
                    nc.vector.tensor_tensor(z[0:n, j, :], z[0:n, j, :], ez[0:n, j, :], ALU.subtract
                                            ).then_inc(z_done, 1)
                for h in range(NG):
                    v.wait_ge(b_mm, h + 1)
                    nc.vector.tensor_copy(b_t[:, h, 0:SEQ], bank(h % 2)).then_inc(b_done, 1)
                v.wait_ge(b_mm, NG + 1)
                nc.vector.tensor_copy(b_t[:, :, SEQ:TP], bank(2)[:, 0:256].rearrange("p (h t) -> p h t", t=CH)
                                      ).then_inc(b_done, 1)
                v.wait_ge(b_done, NG + 1)
                bc = b_t.rearrange("p h (c t) -> p (h c) t", t=CH)
                nc.vector.tensor_tensor(b_mid.rearrange("p h (c t) -> p (h c) t", t=CH), bc,
                                        bc[:, :, 31:32].broadcast_to([P, NG * 9, CH]), ALU.subtract
                                        ).then_inc(b_mid_done, 1)
                v.wait_ge(gla_in, 80)
                v.wait_ge(gpads, 3)
                v.sem_inc(g_state, 4)

                def tile(i, w, st, chunks_in):
                    t0 = i * P
                    v.wait_ge(tile_free, i + 1)
                    v.wait_ge(g_exp, 3 * i + 3)
                    nc.vector.scalar_tensor_tensor(out=q_in[:, :, 0:w], in0=qk[:, 0:4, ds(t0, w)], scalar=GQ,
                                                   in1=e_q[:, :, 0:w], op0=ALU.mult, op1=ALU.mult).then_inc(g_prep, 1)
                    nc.vector.tensor_tensor(k_in[:, :, 0:w], qk[:, 4:8, ds(t0, w)], e_k[:, :, 0:w], ALU.mult
                                            ).then_inc(g_prep, 1)
                    nc.vector.scalar_tensor_tensor(out=q_st[:, :, 0:w], in0=qk[:, 0:4, ds(t0, w)], scalar=GQ,
                                                   in1=e_b[:, :, 0:w], op0=ALU.mult, op1=ALU.mult).then_inc(g_prep, 1)
                    v.wait_ge(g_turned, 3 * i + 3)
                    nc.vector.tensor_tensor(att[0:w, :, 0:w], psum[0][0:w, 0, :].rearrange("s (h t) -> s h t", h=NG
                                            )[:, :, 0:w], tri_bd[0:w, 0:w].unsqueeze(1).broadcast_to([w, NG, w]),
                                            ALU.mult).then_inc(g_att, 1)
                    for c in range(chunks_in):
                        e = 64 * c + 63
                        v.wait_ge(g_kv, 2 * i + (c + 1))
                        for h in range(NG):
                            nc.vector.tensor_scalar(kv_tmp[:, h, :], psum[3][:, h // 2, (h % 2) * DV:(h % 2 + 1) * DV],
                                                    e_q[:, h, e:e + 1], None, ALU.mult).then_inc(kv_scaled, 1)
                        v.wait_ge(kv_scaled, 8 * i + (4 * c + 4))
                        for h in range(NG):
                            nc.vector.scalar_tensor_tensor(out=st[:, h, :], in0=st[:, h, :], scalar=e_b[:, h, e:e + 1],
                                                           in1=kv_tmp[:, h, :], op0=ALU.mult, op1=ALU.add
                                                           ).then_inc(g_state, 1)
                        v.wait_ge(g_state, 8 * i + (4 * c + 8))
                    v.wait_ge(o_ssq, 4 * i + 4)
                    nc.vector.tensor_scalar(o_rs[0:w], o_ms[0:w], 1.0 / DV, EPS, ALU.mult, ALU.add
                                            ).then_inc(o_mean, 1)
                    v.wait_ge(g_out, i + 1)
                    wt = min(w, T - SEQ) if w < P else w
                    for n in range(8):
                        m = nc.vector.tensor_scalar(y_g[:, n, ds(t0, wt)],
                                                    psum[1][:, n // 4, (n % 4) * P:(n % 4) * P + wt],
                                                    vcol("glan", n % 2), None, ALU.mult)
                        m.then_inc(tile_free if n == 7 else y_g_out, 1)
                with v.Fori(0, 4) as i:
                    tile(i, P, st_g[0], 2)
                v.wait_ge(st_g_in, 16)
                tile(4, CH, st_g[1], 1)

        S7 = Region(y_g_at + 8 * T)
        gates = S7.take(16, T)
        merged = S7.take(8, T)
        merge_tmp = gates[:, 0:4].rearrange("p a t -> p (a t)")[:, 0:2 * D].rearrange("p (a d) -> p a d", a=2)
        w_out_sb = S7.take(KD, D)
        wb = [[S7.take(KD, 2 * P) for _ in range(2)] for _ in range(2)]
        r_in = S7.take(8, T)
        r_sig = S7.take(8, T)
        x2_at = ARENA - 5 * D
        S7b = Region(x2_at - 2 * D)
        gt1_b = S7b.take(2, D)
        x2 = S7b.take(5, D)
        r_loaded = sem("r_loaded")
        gates_loaded = sem("gates_loaded")
        wb_in = [sem(f"wb_in{s}") for s in range(2)]
        w_out_in = sem("w_out_in")
        x2_in = sem("x2_in")
        r_sig_done = sem("r_sig_done")
        r_silu = sem("r_silu")
        y_g_done = sem("y_g_done")
        gates_done = sem("gates_done")
        br_done = sem("br_done")
        br_out = sem("br_out")
        merged_done = sem("merged_done")
        wo_mm = sem("wo_mm")
        wo_scaled = sem("wo_scaled")
        x2_done = sem("x2_done")
        wbr_v = [I[n][0].rearrange("(k p) n -> p k n", p=P) for n in ("w_branch_rwkv", "w_branch_gla")]

        with nc.Block() as block:
            @block.sync
            def _(sp):
                def load(p, s):
                    sp.wait_ge(br_done, 4 * p + 4)
                    for b in range(2):
                        sp.dma_start(wb[s][b], wbr_v[b][:, :, ds(p * 2 * P, 2 * P)]).then_inc(wb_in[s], 16)
                sp.dma_start(r_in, gate_dram[0:8].rearrange("n p t -> p n t")).then_inc(r_loaded, 16)
                sp.dma_start(gates, gate_dram[8:24].rearrange("n p t -> p n t")).then_inc(gates_loaded, 16)
                with sp.Fori(0, 2) as i:
                    for s in range(2):
                        load(2 * i + s, s)
                sp.dma_start(w_out_sb, I["w_out"][0].rearrange("(k p) n -> p k n", p=P)).then_inc(w_out_in, 16)
                sp.wait_ge(y_g_done, 8)
                sp.dma_start(x2[:, 0:4, :], I["x_prompt"][0].rearrange("(j p) d -> p j d", p=P)).then_inc(x2_in, 16)
                sp.dma_start(x2[0:DEC, 4, :], I["x_sample"][0]).then_inc(x2_in, 16)
                for s in range(2):
                    sp.dma_start(gt1_b[:, s, :], mod_dram[s, 2 * D:3 * D].partition_broadcast(P)).then_inc(x2_in, 16)

            @block.scalar
            def _(act):
                act.sem_inc(br_done, 8)
                act.wait_ge(r_loaded, 16)
                for k in range(8):
                    nc.scalar.activation(r_sig[:, k, :], r_in[:, k, :], ACT.Sigmoid).then_inc(r_sig_done, 1)
                act.wait_ge(gates_loaded, 16)
                for k in range(8):
                    for b in range(2):
                        g = gates[:, 8 * b + k, :]
                        nc.scalar.activation(g, g, ACT.Sigmoid).then_inc(gates_done, 1)

            @block.gpsimd
            def _(pool):
                for k in range(8):
                    pool.wait_ge(r_sig_done, k + 1)
                    pool.tensor_tensor(r_sig[:, k, :], r_sig[:, k, :], r_in[:, k, :], ALU.mult).then_inc(r_silu, 1)

            @block.vector
            def _(v):
                v.sem_inc(br_out, 4)
                for k in range(8):
                    v.wait_ge(r_silu, k + 1)
                    nc.vector.tensor_tensor(y_g[:, k, :], y_g[:, k, :], r_sig[:, k, :], ALU.mult).then_inc(y_g_done, 1)
                v.wait_ge(gates_done, 16)

                def pair(p):
                    for f in range(2):
                        for b in range(2):
                            u = 2 * f + b
                            v.wait_ge(br_done, 4 * p + (u + 9))
                            g = gates[:, ds(p * 2 + (8 * b + f), 1), :].rearrange("p a (c t) -> p (a c) t", c=2)
                            nc.vector.tensor_tensor(g, g, psum[u][:, :, 0:HALF], ALU.mult).then_inc(br_out, 1)
                        v.wait_ge(br_out, 4 * p + (2 * f + 6))
                        nc.vector.tensor_tensor(merged[:, ds(p * 2 + f, 1), :], gates[:, ds(p * 2 + f, 1), :],
                                                gates[:, ds(p * 2 + (8 + f), 1), :], ALU.add).then_inc(merged_done, 1)
                with v.Fori(0, 4) as p:
                    pair(p)
                v.wait_ge(x2_in, 64)
                for j, n in TILES:
                    v.wait_ge(wo_mm, j + 1)
                    s = 1 if j == 4 else 0
                    o = psum[j % 2][0:n].rearrange("t b c -> t (b c)")
                    nc.vector.tensor_tensor(merge_tmp[0:n, j % 2, :], o, gt1_b[0:n, s, :], ALU.mult
                                            ).then_inc(wo_scaled, 1)
                    v.wait_ge(wo_scaled, j + 1)
                    nc.vector.tensor_tensor(x2[0:n, j, :], x2[0:n, j, :], merge_tmp[0:n, j % 2, :], ALU.add
                                            ).then_inc(x2_done, 1)
                v.wait_ge(x2_done, 5)

            @block.tensor
            def _(pe):
                def pair(p, s, use):
                    pe.wait_ge(wb_in[s], 32 * use + 32)
                    for f in range(2):
                        for b in range(2):
                            u = 2 * f + b
                            y = (y_r, y_g)[b]
                            pe.wait_ge(br_out, 4 * p + (u + 1))
                            for k in range(KD):
                                for c in range(2):
                                    m = nc.tensor.matmul(psum[u][:, c, 0:HALF], wb[s][b][:, k, f * P:(f + 1) * P],
                                                         cols(y[:, k], c), start=k == 0, stop=k == KD - 1)
                            m.then_inc(br_done, 1)
                pe.wait_ge(y_g_done, 8)
                with pe.Fori(0, 2) as i:
                    for s in range(2):
                        pair(2 * i + s, s, i)
                pe.wait_ge(merged_done, 8)
                pe.wait_ge(w_out_in, 16)
                for j, n in TILES:
                    if j >= 2:
                        pe.wait_ge(wo_scaled, j - 1)
                    for k in range(KD):
                        for b in range(2):
                            m = nc.tensor.matmul(psum[j % 2][0:n, b, :], merged[:, k, j * P:j * P + n],
                                                 w_out_sb[:, k, b * 512:(b + 1) * 512], start=k == 0,
                                                 stop=k == KD - 1)
                    m.then_inc(wo_mm, 1)

        clear_semaphores()
        NE, NGR, EPG, FF = 32, 4, 8, 512
        BLK = 64
        NSLOT = NE * BLK
        S8 = Region(base, x2_at)
        h2 = S8.take(5, D)
        route = Region(S8.at, x2_at)
        slot_i = [route.take(5) for _ in range(2)]
        slot_g = [route.take(5) for _ in range(2)]
        wgt = [route.take(5) for _ in range(2)]
        wgt_r = [route.take(5) for _ in range(2)]
        pos = [route.take(5) for _ in range(2)]
        eid = [route.take(5) for _ in range(2)]
        trash = [route.take(5) for _ in range(2)]
        in_r = [route.take(5) for _ in range(2)]
        tmp_i = route.take(5)
        n_rounds = route.take(1)
        sums2 = route.take(5)
        moe_at = route.at
        mods2 = [route.take(2, D) for _ in range(2)]
        norm2_b = route.take(D)
        h2_t = route.take(KD, T)
        router = route.take(KD, 36)
        lg = route.take(5, 36)
        g8 = route.take(5, 8)
        top_g = route.take(5, 8)
        top_e = route.take(5, 8)
        idx_g = route.take(5, 8)
        idx_e = route.take(5, 8)
        gid = route.take(5)
        eidx = [route.take(5) for _ in range(2)]
        pexp = route.take(5, 4)
        psum_g = route.take(5)
        iota_e = route.take(NE)
        valid = route.take(5)
        goh = route.take(5, 4)
        prod = route.take(5, NGR, EPG)
        within = route.take(5, 8)
        oh = [route.take(5, NE) for _ in range(2)]
        both = route.take(5, NE)
        before = route.take(5, NE)
        ohp = route.take(5, NE)
        up_full = route.take(128)
        cnt = route.take(NE)
        cmax = route.take(1)
        junk2 = route.take(D)
        n2_in = sem("n2_in")
        rt_const = sem("rt_const")
        x2_sq = sem("x2_sq")
        x2_ms = sem("x2_ms")
        x2_std = sem("x2_std")
        x2_rs = sem("x2_rs")
        m2_done = sem("m2_done")
        h2_half = sem("h2_half")
        h2_done = sem("h2_done")
        h2_tr = sem("h2_tr")
        h2_t_out = sem("h2_t_out")
        lg_mm = sem("lg_mm")
        lg_done = sem("lg_done")
        rt = sem("rt")
        rt_shift = sem("rt_shift")
        rt_exp = sem("rt_exp")
        rt_gap = sem("rt_gap")
        both_done = sem("both_done")
        pos_mm = sem("pos_mm")
        routed = sem("routed")

        def as_u32(ap):
            return ap.bitcast(U32)

        with nc.Block() as block:
            @block.sync
            def _(sp):
                for s in range(2):
                    sp.dma_start(mods2[0][:, s, :], mod_dram[s, 4 * D:5 * D].partition_broadcast(P)).then_inc(n2_in, 16)
                    sp.dma_start(mods2[1][:, s, :], mod_dram[s, 3 * D:4 * D].partition_broadcast(P)).then_inc(n2_in, 16)
                sp.dma_start(norm2_b, I["norm2_g"][0].partition_broadcast(P)).then_inc(n2_in, 16)
                sp.dma_start(router[:, :, 0:4], I["router_group"][0].rearrange("(k p) n -> p k n", p=P)
                             ).then_inc(n2_in, 16)
                sp.dma_start(router[:, :, 4:36], I["router_expert"][0].rearrange("(k p) n -> p k n", p=P)
                             ).then_inc(n2_in, 16)

            @block.gpsimd
            def _(pool):
                steps = [0]

                def step(ins):
                    ins.then_inc(rt_const, 1)
                    steps[0] += 1
                    pool.wait_ge(rt_const, steps[0])
                iota_i = ohp[:, 0, :].bitcast(I32)
                step(pool.iota(iota_i, pattern=[[1, NE]], base=0, channel_multiplier=0))
                step(pool.tensor_copy(iota_e, iota_i))
                for k in range(2):
                    step(pool.iota(tmp_i.bitcast(I32), pattern=[[2 * P, 5]], base=NSLOT + k, channel_multiplier=2))
                    step(pool.tensor_copy(trash[k], tmp_i.bitcast(I32)))
                step(pool.memset(valid, 1.0))
                step(pool.memset(valid[:, 4:5], 0.0))
                step(pool.memset(valid[0:DEC, 4:5], 1.0))
                step(pool.memset(lg, 0.0))
                step(pool.memset(g8, -3.0e38))
                step(pool.affine_select(out=up_full, in_=ones, compare_op=ALU.is_gt, fill=0.0, base=0,
                                        pattern=[[1, 128]], channel_multiplier=-1))

            @block.scalar
            def _(act):
                for j, n in TILES:
                    if j:
                        act.wait_ge(x2_sq, j)
                    nc.scalar.activation(junk2[0:n], x2[0:n, j, :], ACT.Square, accum_out=sums2[0:n, j:j + 1]
                                         ).then_inc(x2_sq, 1)
                act.wait_ge(x2_ms, 2)
                for b, c in ((slice(0, P), slice(0, 4)), (slice(0, DEC), slice(4, 5))):
                    nc.scalar.activation(sums2[b, c], sums2[b, c], ACT.Sqrt).then_inc(x2_std, 1)
                act.wait_ge(rt_shift, 1)
                nc.scalar.activation(pexp, pexp, ACT.Exp).then_inc(rt_exp, 1)
                act.wait_ge(rt_gap, 1)
                nc.scalar.activation(wgt[1], wgt[1], ACT.Exp).then_inc(rt_exp, 1)

            @block.tensor
            def _(pe):
                u = 0
                for j, n in TILES:
                    pe.wait_ge(h2_done, j + 1)
                    for b in range(2):
                        if u >= 2:
                            pe.wait_ge(h2_t_out, u - 1)
                        for q in range(4):
                            k = 4 * b + q
                            m = nc.tensor.transpose(bank(u % 2)[:, q * P:q * P + n], h2[0:n, j, k * P:(k + 1) * P],
                                                    ident[0:n, 0:n])
                        m.then_inc(h2_tr, 1)
                        u += 1
                pe.wait_ge(h2_t_out, 10)
                for j, n in TILES:
                    for k in range(KD):
                        m = nc.tensor.matmul(bank(2)[0:n, j * 36:(j + 1) * 36], h2_t[:, k, j * P:j * P + n],
                                             router[:, k, :], start=k == 0, stop=k == KD - 1)
                m.then_inc(lg_mm, 1)
                pe.wait_ge(both_done, 1)
                pe.wait_ge(rt_const, 12)
                nc.tensor.matmul(bank(3)[:, 0:160], up_full, both.rearrange("p j e -> p (j e)"), start=True, stop=True)
                nc.tensor.matmul(bank(3)[:, 256:416], ones, both.rearrange("p j e -> p (j e)"), start=True, stop=True
                                 ).then_inc(pos_mm, 1)

            @block.vector
            def _(v):
                v.wait_ge(x2_sq, 5)
                parts2 = ((slice(0, P), slice(0, 4)), (slice(0, DEC), slice(4, 5)))
                for b, c in parts2:
                    nc.vector.tensor_scalar(sums2[b, c], sums2[b, c], 1.0 / D, EPS, ALU.mult, ALU.add
                                            ).then_inc(x2_ms, 1)
                v.wait_ge(n2_in, 16 * 7)
                for s in range(2):
                    nc.vector.scalar_tensor_tensor(out=mods2[0][:, s, :], in0=mods2[0][:, s, :], scalar=1.0,
                                                   in1=norm2_b, op0=ALU.add, op1=ALU.mult).then_inc(m2_done, 1)
                v.wait_ge(x2_std, 2)
                for b, c in parts2:
                    nc.vector.reciprocal(sums2[b, c], sums2[b, c]).then_inc(x2_rs, 1)
                v.wait_ge(x2_rs, 2)
                v.wait_ge(m2_done, 2)
                for j, n in TILES:
                    s = 1 if j == 4 else 0
                    nc.vector.scalar_tensor_tensor(out=h2[0:n, j, :], in0=x2[0:n, j, :], scalar=sums2[0:n, j:j + 1],
                                                   in1=mods2[0][0:n, s, :], op0=ALU.mult, op1=ALU.mult
                                                   ).then_inc(h2_half, 1)
                    v.wait_ge(h2_half, j + 1)
                    nc.vector.tensor_tensor(h2[0:n, j, :], h2[0:n, j, :], mods2[1][0:n, s, :], ALU.add
                                            ).then_inc(h2_done, 1)
                u = 0
                for j, n in TILES:
                    for b in range(2):
                        v.wait_ge(h2_tr, u + 1)
                        nc.vector.tensor_copy(h2_t[:, 4 * b:4 * b + 4, j * P:j * P + n],
                                              bank(u % 2).rearrange("p (q t) -> p q t", q=4)[:, :, 0:n]
                                              ).then_inc(h2_t_out, 1)
                        u += 1
                v.wait_ge(rt_const, 12)
                v.wait_ge(lg_mm, 1)
                nc.vector.tensor_copy(lg[:, 0:4, :], bank(2)[:, 0:144].rearrange("p (j n) -> p j n", n=36)
                                      ).then_inc(lg_done, 1)
                nc.vector.tensor_copy(lg[0:DEC, 4, :], bank(2)[0:DEC, 144:180]).then_inc(lg_done, 1)
                v.wait_ge(lg_done, 2)
                done = [0]

                def step(*ins):
                    for i in ins:
                        i.then_inc(rt, 1)
                        done[0] += 1
                    v.wait_ge(rt, done[0])
                ve = nc.vector
                step(ve.tensor_copy(g8[:, :, 0:4], lg[:, :, 0:4]))
                step(*[ve.max(top_g[:, j, :], g8[:, j, :]) for j in range(5)])
                step(*[ve.max_index(as_u32(idx_g[:, j, :]), top_g[:, j, :], g8[:, j, :]) for j in range(5)])
                step(ve.tensor_copy(gid, as_u32(idx_g[:, :, 0])))
                ve.tensor_tensor(pexp, lg[:, :, 0:4], top_g[:, :, 0:1].broadcast_to([P, 5, 4]), ALU.subtract
                                 ).then_inc(rt_shift, 1)
                step(ve.tensor_tensor(goh, iota_e[:, 0:4].unsqueeze(1).broadcast_to([P, 5, 4]),
                                      gid.unsqueeze(2).broadcast_to([P, 5, 4]), ALU.is_equal))
                step(*[ve.tensor_tensor(prod[:, j], lg[:, j, 4:36].rearrange("p (g e) -> p g e", g=NGR),
                                        goh[:, j, :].unsqueeze(2).broadcast_to([P, NGR, EPG]), ALU.mult)
                       for j in range(5)])
                step(ve.tensor_reduce(within, prod.rearrange("p j g e -> p j e g"), AX.X, ALU.add))
                step(*[ve.max(top_e[:, j, :], within[:, j, :]) for j in range(5)])
                step(*[ve.max_index(as_u32(idx_e[:, j, :]), top_e[:, j, :], within[:, j, :]) for j in range(5)])
                step(*[ve.tensor_copy(eidx[k], as_u32(idx_e[:, :, k])) for k in range(2)])
                step(*[ve.scalar_tensor_tensor(out=eid[k], in0=gid, scalar=float(EPG), in1=eidx[k], op0=ALU.mult,
                                               op1=ALU.add) for k in range(2)])
                ve.tensor_tensor(wgt[1], top_e[:, :, 1], top_e[:, :, 0], ALU.subtract).then_inc(rt_gap, 1)
                step(*[ve.tensor_tensor(oh[k], iota_e.unsqueeze(1).broadcast_to([P, 5, NE]),
                                        eid[k].unsqueeze(2).broadcast_to([P, 5, NE]), ALU.is_equal)
                       for k in range(2)])
                step(*[ve.tensor_tensor(oh[k], oh[k], valid.unsqueeze(2).broadcast_to([P, 5, NE]), ALU.mult)
                       for k in range(2)])
                ve.tensor_tensor(both, oh[0], oh[1], ALU.add).then_inc(both_done, 1)
                v.wait_ge(rt_exp, 2)
                step(ve.tensor_reduce(psum_g, pexp, AX.X, ALU.add), ve.tensor_scalar(wgt[0], wgt[1], 1.0, None,
                                                                                   ALU.add))
                step(ve.tensor_tensor(wgt[0], wgt[0], psum_g, ALU.mult))
                step(ve.reciprocal(wgt[0], wgt[0]))
                step(ve.tensor_tensor(wgt[1], wgt[1], wgt[0], ALU.mult))
                v.wait_ge(pos_mm, 1)
                step(ve.tensor_copy(before, bank(3)[:, 0:160].rearrange("p (j e) -> p j e", e=NE)),
                     ve.tensor_copy(cnt, bank(3)[:, 256:256 + NE]))
                for j in range(1, 5):
                    step(ve.tensor_tensor(before[:, j, :], before[:, j, :], cnt, ALU.add))
                    step(ve.tensor_tensor(cnt, cnt, bank(3)[:, 256 + j * NE:256 + (j + 1) * NE], ALU.add))
                for k in range(2):
                    step(ve.tensor_tensor(ohp, oh[k], before, ALU.mult))
                    step(ve.tensor_reduce(pos[k], ohp, AX.X, ALU.add))
                    step(ve.tensor_scalar(tmp_i, valid, -1.0e6, 1.0e6, ALU.mult, ALU.add))
                    step(ve.tensor_tensor(pos[k], pos[k], tmp_i, ALU.add))
                step(ve.tensor_reduce(cmax, cnt, AX.X, ALU.max))
                step(ve.tensor_scalar(cmax, cmax, float(BLK - 1), None, ALU.add))
                step(ve.tensor_copy(n_rounds.bitcast(I32), cmax))
                ve.tensor_single_scalar(n_rounds.bitcast(I32), n_rounds.bitcast(I32), 6, ALU.arith_shift_right
                                        ).then_inc(routed, 1)
                v.wait_ge(routed, 1)

        low = Region(moe_at, x2_at)
        gt2_b = low.take(2, D)
        gath = [low.take(2, D) for _ in range(2)]
        x_blk = [low.take(D) for _ in range(2)]
        x_t = [low.take(KD, 2 * BLK) for _ in range(2)]
        gu = low.take(512)
        act_g = low.take(4, BLK)
        hid = low.take(4, BLK)
        y_blk = [low.take(512) for _ in range(2)]
        w_gu = [low.take(2, KD, FF) for _ in range(2)]
        w_dn = [low.take(4, D) for _ in range(2)]
        wg_in = [sem(f"wg_in{s}") for s in range(2)]
        wd_in = [sem(f"wd_in{s}") for s in range(2)]
        gt2_in = sem("gt2_in")
        slots_done = sem("slots_done")
        slot_step = sem("slot_step")
        pool_go = sem("pool_go")
        w_done = sem("w_done")
        scattered = sem("scattered")
        x_in9 = [sem(f"x_in9_{s}") for s in range(2)]
        x_tr9 = sem("x_tr9")
        x_t9 = sem("x_t9")
        gu_mm = sem("gu_mm")
        gu_out = sem("gu_out")
        gu_tr = sem("gu_tr")
        silu_done = sem("silu_done")
        hid_done = sem("hid_done")
        dn_mm = sem("dn_mm")
        y_done = sem("y_done")
        y_out9 = [sem(f"y_out9_{s}") for s in range(2)]
        gathered = [sem(f"gathered{s}") for s in range(2)]
        g_sum = sem("g_sum")
        x3_done = sem("x3_done")
        egate = I["expert_w_gate"][0].rearrange("e (k p) f -> e p k f", p=P)
        eup = I["expert_w_up"][0].rearrange("e (k p) f -> e p k f", p=P)
        edown = I["expert_w_down"][0].rearrange("e (k p) f -> e p k f", p=P)
        xs_v = xs_dram[0:NSLOT].rearrange("(e s) d -> e s d", s=2 * BLK)
        ys_v = ys_dram.rearrange("(e s) d -> e s d", s=BLK)
        ROUNDS_MAX = (T + BLK - 1) // BLK

        def experts(eng, before_loop, expert, after_loop):
            n = eng.value_load(n_rounds[0:1, 0:1].bitcast(I32), min_val=1, max_val=ROUNDS_MAX)
            with eng.Fori(0, n) as r:
                before_loop(r)
                with eng.Fori(0, NE // 4) as i:
                    for u in range(4):
                        expert(r, 4 * i + u, u, r * NE + 4 * i + u, 2 * i + u // 2, r * (NE // 4) + i)
                after_loop(r)

        def nothing(r):
            pass

        with nc.Block() as block:
            @block.sync
            def _(sp):
                for s in range(2):
                    sp.dma_start(gt2_b[:, s, :], mod_dram[s, 5 * D:6 * D].partition_broadcast(P)).then_inc(gt2_in, 16)

                def expert(r, e, u, n, pair, pair_use):
                    s = u % 2
                    sp.wait_ge(dn_mm, n + 1)
                    sp.dma_start(w_gu[s][:, 0], egate[ds(e, 1)].rearrange("e p k f -> (e p) k f")
                                 ).then_inc(wg_in[s], 16)
                    sp.dma_start(w_gu[s][:, 1], eup[ds(e, 1)].rearrange("e p k f -> (e p) k f")
                                 ).then_inc(wg_in[s], 16)
                    if s == 0:
                        sp.wait_ge(scattered, r * 160 + 160)
                        sp.dma_start(x_blk[u // 2], xs_v[ds(pair, 1)].rearrange("e s d -> (e s) d")
                                     ).then_inc(x_in9[u // 2], 16)
                    sp.dma_start(w_dn[s], edown[ds(e, 1)].rearrange("e p k f -> (e p) k f")).then_inc(wd_in[s], 16)
                experts(sp, nothing, expert, nothing)

            @block.gpsimd
            def _(pool):
                def scatter(r):
                    pool.wait_ge(slots_done, r * 6 + 6)
                    pool.sem_inc(pool_go, 1)
                    for j, n in TILES:
                        for k in range(2):
                            pool.indirect_dma_start(
                                xs_dram, bass.IndirectOffsetOnAxis(ap=as_u32(slot_i[k][0:n, j:j + 1]), axis=0),
                                h2[0:n, j, :], None).then_inc(scattered, 16)

                def gather(r):
                    for s in range(2):
                        pool.wait_ge(y_out9[s], r * (NE * 16) + (NE * 16 + 32))
                        pool.sem_inc(pool_go, 1)
                    for j, n in TILES:
                        pool.wait_ge(x3_done, r * 5 + (j + 1))
                        pool.sem_inc(pool_go, 1)
                        for k in range(2):
                            pool.indirect_dma_start(
                                gath[j % 2][0:n, k, :], None, ys_dram,
                                bass.IndirectOffsetOnAxis(ap=as_u32(slot_g[k][0:n, j:j + 1]), axis=0)
                                ).then_inc(gathered[j % 2], 16)
                n = pool.value_load(n_rounds[0:1, 0:1].bitcast(I32), min_val=1, max_val=ROUNDS_MAX)
                with pool.Fori(0, n) as r:
                    scatter(r)
                    gather(r)

            @block.tensor
            def _(pe):
                pe.sem_inc(dn_mm, 2)

                def expert(r, e, u, n, pair, pair_use):
                    s = u % 2
                    if s == 0:
                        pe.wait_ge(x_in9[u // 2], 16 * pair_use + 16)
                        for h in range(2):
                            for k in range(4):
                                m = nc.tensor.transpose(psum[h][:, 0, k * P:(k + 1) * P],
                                                        x_blk[u // 2][:, (4 * h + k) * P:(4 * h + k + 1) * P], ident)
                            m.then_inc(x_tr9, 1)
                        pe.wait_ge(x_t9, n + 2)
                    pe.wait_ge(wg_in[s], 32 * (2 * pair_use + u // 2) + 32)
                    for k in range(KD):
                        for b in range(2):
                            m = nc.tensor.matmul(psum[s][64 * b:64 * b + 64, 1, :], x_t[u // 2][:, k, s * BLK:(s + 1) * BLK],
                                                 w_gu[s][:, b, k, :], start=k == 0, stop=k == KD - 1)
                    m.then_inc(gu_mm, 1)
                    pe.wait_ge(gu_out, n + 1)
                    for f in range(4):
                        m = nc.tensor.transpose(psum[2 + s][:, 0, f * P:(f + 1) * P], gu[:, f * P:(f + 1) * P], ident)
                    m.then_inc(gu_tr, 1)
                    pe.wait_ge(hid_done, n + 1)
                    pe.wait_ge(wd_in[s], 16 * (2 * pair_use + u // 2) + 16)
                    pe.wait_ge(y_done, n + 1)
                    for f in range(4):
                        for b in range(2):
                            m = nc.tensor.matmul(psum[2 + s][64 * b:64 * b + 64, 1, :], hid[:, f, :],
                                                 w_dn[s][:, f, b * 512:(b + 1) * 512], start=f == 0, stop=f == 3)
                    m.then_inc(dn_mm, 1)
                experts(pe, nothing, expert, nothing)

            @block.scalar
            def _(act):
                for s in range(2):
                    act.sem_inc(y_out9[s], 32)

                def expert(r, e, u, n, pair, pair_use):
                    s = u % 2
                    if s == 0:
                        for h in range(2):
                            act.wait_ge(x_tr9, n + (h + 1))
                            nc.scalar.activation(x_t[u // 2][:, 4 * h:4 * h + 4, :].rearrange("p k t -> p (k t)"),
                                                 psum[h][:, 0, :], ACT.Copy).then_inc(x_t9, 1)
                    act.wait_ge(gu_tr, n + 1)
                    nc.scalar.activation(act_g, psum[2 + s][:, 0, :].rearrange("p (f t) -> p f t", f=4)[:, :, 0:BLK],
                                         ACT.Silu).then_inc(silu_done, 1)
                    act.wait_ge(y_done, n + 3)
                    for b in range(2):
                        act.dma_start(ys_v[ds(e, 1), :, b * 512:(b + 1) * 512].rearrange("e s d -> (e s) d"),
                                      y_blk[s][64 * b:64 * b + 64, :]).then_inc(y_out9[s], 16)
                experts(act, nothing, expert, nothing)

            @block.vector
            def _(v):
                v.sem_inc(y_done, 2)
                v.sem_inc(x3_done, 2)
                v.wait_ge(gt2_in, 32)

                def slots(r):
                    ve = nc.vector
                    for k in range(2):
                        ve.tensor_scalar(tmp_i, pos[k], 0.0, None, ALU.is_ge).then_inc(slot_step, 1)
                        ve.tensor_scalar(in_r[k], pos[k], float(BLK), None, ALU.is_lt).then_inc(slot_step, 1)
                        v.wait_ge(slot_step, r * 14 + (7 * k + 2))
                        ve.tensor_tensor(in_r[k], in_r[k], tmp_i, ALU.mult).then_inc(slot_step, 1)
                        ve.scalar_tensor_tensor(out=wgt_r[k], in0=eid[k], scalar=float(BLK), in1=pos[k],
                                                op0=ALU.mult, op1=ALU.add).then_inc(slot_step, 1)
                        v.wait_ge(slot_step, r * 14 + (7 * k + 4))
                        ve.tensor_tensor(tmp_i, wgt_r[k], in_r[k], ALU.mult).then_inc(slot_step, 1)
                        ve.tensor_tensor(wgt_r[k], wgt_r[k], trash[k], ALU.subtract).then_inc(slot_step, 1)
                        v.wait_ge(slot_step, r * 14 + (7 * k + 6))
                        ve.tensor_copy(as_u32(slot_g[k]), tmp_i).then_inc(slots_done, 1)
                        ve.tensor_tensor(wgt_r[k], wgt_r[k], in_r[k], ALU.mult).then_inc(slot_step, 1)
                        v.wait_ge(slot_step, r * 14 + (7 * k + 7))
                        ve.tensor_tensor(wgt_r[k], wgt_r[k], trash[k], ALU.add).then_inc(slots_done, 1)
                        v.wait_ge(slots_done, r * 6 + (3 * k + 2))
                        ve.tensor_copy(as_u32(slot_i[k]), wgt_r[k]).then_inc(slots_done, 1)
                        v.wait_ge(slots_done, r * 6 + (3 * k + 3))
                        ve.tensor_tensor(wgt_r[k], wgt[k], in_r[k], ALU.mult).then_inc(w_done, 1)
                        ve.tensor_scalar(pos[k], pos[k], -float(BLK), None, ALU.add).then_inc(w_done, 1)

                def expert(r, e, u, n, pair, pair_use):
                    s = u % 2
                    v.wait_ge(gu_mm, n + 1)
                    nc.vector.tensor_copy(gu, psum[s][:, 1, :]).then_inc(gu_out, 1)
                    v.wait_ge(silu_done, n + 1)
                    nc.vector.tensor_tensor(hid, act_g, psum[2 + s][:, 0, :].rearrange("p (f t) -> p f t", f=4
                                                                                       )[:, :, BLK:2 * BLK], ALU.mult
                                            ).then_inc(hid_done, 1)
                    v.wait_ge(dn_mm, n + 3)
                    v.wait_ge(y_out9[s], 32 * (2 * pair_use + u // 2) + 32)
                    nc.vector.tensor_copy(y_blk[s], psum[2 + s][:, 1, :]).then_inc(y_done, 1)

                def add(r):
                    ve = nc.vector
                    for j, n in TILES:
                        b = j % 2
                        g = gath[b]
                        use = (3, 2)[b]
                        v.wait_ge(gathered[b], r * (32 * use) + 32 * (j // 2 + 1))
                        if j == 0:
                            v.wait_ge(w_done, r * 4 + 4)
                        ve.tensor_scalar(g[0:n, 0, :], g[0:n, 0, :], wgt_r[0][0:n, j:j + 1], None, ALU.mult
                                         ).then_inc(g_sum, 1)
                        v.wait_ge(g_sum, r * 15 + (3 * j + 1))
                        ve.scalar_tensor_tensor(out=g[0:n, 0, :], in0=g[0:n, 1, :], scalar=wgt_r[1][0:n, j:j + 1],
                                                in1=g[0:n, 0, :], op0=ALU.mult, op1=ALU.add).then_inc(g_sum, 1)
                        v.wait_ge(g_sum, r * 15 + (3 * j + 2))
                        ve.tensor_tensor(g[0:n, 0, :], g[0:n, 0, :], gt2_b[0:n, 1 if j == 4 else 0, :], ALU.mult
                                         ).then_inc(g_sum, 1)
                        v.wait_ge(g_sum, r * 15 + (3 * j + 3))
                        v.wait_ge(x3_done, r * 5 + (j + 2))
                        ve.tensor_tensor(x2[0:n, j, :], x2[0:n, j, :], g[0:n, 0, :], ALU.add).then_inc(x3_done, 1)
                experts(v, slots, expert, add)

        S10 = Region(moe_at)
        fin_g = S10.take(D)
        fin_junk = S10.take(D)
        fg_in = sem("fg_in")
        f_sq = sem("f_sq")
        f_ms = sem("f_ms")
        f_std = sem("f_std")
        f_rs = sem("f_rs")
        f_done = sem("f_done")
        y_final = sem("y_final")
        with nc.Block() as block:
            @block.sync
            def _(sp):
                sp.dma_start(fin_g, I["final_norm_g"].partition_broadcast(P)).then_inc(fg_in, 16)
                for j, n in TILES:
                    sp.wait_ge(f_done, j + 1)
                    dst = O[0][0, j * P:(j + 1) * P, :] if j < 4 else O[1][0]
                    sp.dma_start(dst, x2[0:n, j, :]).then_inc(y_final, 16)
                sp.wait_ge(y_final, 80)

            @block.scalar
            def _(act):
                for j, n in TILES:
                    if j:
                        act.wait_ge(f_sq, j)
                    nc.scalar.activation(fin_junk[0:n], x2[0:n, j, :], ACT.Square, accum_out=sums2[0:n, j:j + 1]
                                         ).then_inc(f_sq, 1)
                act.wait_ge(f_ms, 2)
                for b, c in ((slice(0, P), slice(0, 4)), (slice(0, DEC), slice(4, 5))):
                    nc.scalar.activation(sums2[b, c], sums2[b, c], ACT.Sqrt).then_inc(f_std, 1)

            @block.vector
            def _(v):
                v.wait_ge(f_sq, 5)
                parts2 = ((slice(0, P), slice(0, 4)), (slice(0, DEC), slice(4, 5)))
                for b, c in parts2:
                    nc.vector.tensor_scalar(sums2[b, c], sums2[b, c], 1.0 / D, EPS, ALU.mult, ALU.add
                                            ).then_inc(f_ms, 1)
                v.wait_ge(f_std, 2)
                for b, c in parts2:
                    nc.vector.reciprocal(sums2[b, c], sums2[b, c]).then_inc(f_rs, 1)
                v.wait_ge(f_rs, 2)
                v.wait_ge(fg_in, 16)
                for j, n in TILES:
                    nc.vector.scalar_tensor_tensor(out=x2[0:n, j, :], in0=x2[0:n, j, :], scalar=sums2[0:n, j:j + 1],
                                                   in1=fin_g[0:n], op0=ALU.mult, op1=ALU.mult).then_inc(f_done, 1)


_OUTS = [(1, 512, 1024), (1, 32, 1024), (1, 1, 1, 3328), (1, 1, 16, 64, 64), (1, 1, 4, 128, 256),
         (1, 1, 1, 3328), (1, 1, 16, 64, 64), (1, 1, 4, 128, 256)]


def kernel(**inputs):
    import numpy as np
    import concourse.bacc as bacc
    from concourse.bass_utils import run_bass_kernel_spmd

    nc = bacc.Bacc("TRN2", target_bir_lowering=False, num_devices=1)
    arrays, ins, outs = {}, {}, []
    for name, a in inputs.items():
        a = np.ascontiguousarray(a)
        arrays[f"in_{name}"] = a
        ins[name] = nc.dram_tensor(f"in_{name}", a.shape, mybir.dt.from_np(a.dtype), kind="ExternalInput").ap()
    for i, shape in enumerate(_OUTS):
        outs.append(nc.dram_tensor(f"out_{i}", shape, F32, kind="ExternalOutput").ap())
    build(nc, ins, outs)
    r = run_bass_kernel_spmd(nc, [arrays], core_ids=[0])
    return tuple(r.results[0][f"out_{i}"] for i in range(len(_OUTS)))
```

```python
from contextlib import ExitStack

import concourse.bass as bass
from concourse import mybir

F32 = mybir.dt.float32
U32 = mybir.dt.uint32
I32 = mybir.dt.int32
F32R = mybir.dt.float32r
ALU = mybir.AluOpType
ACT = mybir.ActivationFunctionType
AX = mybir.AxisListType

P = 128
D = 1024
KD = D // P
SEQ, DEC = 512, 32
T = SEQ + DEC
HALF = T // 2
CH = 64
NCH = SEQ // CH
TP = (NCH + 1) * CH
TILES = [(0, 128), (1, 128), (2, 128), (3, 128), (4, DEC)]
RW_TILES = 26
GL_TILES = 16
GT_TILES = 24
RWKV_PROJ = 3328
GLA_PROJ = 3088
GATE_RANK = 16
XA_COL = RWKV_PROJ + 2048
DECAY_SCALE = -0.6065306597126334
EPS = 1e-6
LN_X_EPS = 64e-5


def ds(start, size):
    return bass.ds(start, size)


def build(nc, I, O):
    ctx = ExitStack()
    with ctx:
        live = []

        def sem(name):
            live.append(nc.alloc_semaphore(name))
            return live[-1]

        def clear_semaphores():
            nc.clear_and_free_semaphores(list(live))
            live.clear()
            nc.all_engine_barrier()

        def scratch(name, shape):
            return nc.dram_tensor(name, shape, F32, kind="Internal").ap()

        ARENA, LOWER = 53184, 23488
        lower = ctx.enter_context(nc.sbuf_tensor("lower", [P, LOWER], F32))
        upper = {"scope": ExitStack()}
        ctx.callback(lambda: upper["scope"].close())

        def lay_out_upper(stage, n_r=0):
            upper["scope"].close()
            scope = ExitStack()
            upper["scope"] = scope
            upper["at"] = LOWER + n_r
            if n_r:
                upper["r"] = scope.enter_context(nc.sbuf_tensor(f"upper_r{stage}", [P, n_r], F32R))
            upper["f32"] = scope.enter_context(nc.sbuf_tensor(f"upper{stage}", [P, ARENA - LOWER - n_r], F32))

        def at_words(a, b):
            if b <= LOWER:
                return lower[:, a:b]
            if a < upper["at"]:
                return upper["r"][:, a - LOWER:b - LOWER]
            return upper["f32"][:, a - upper["at"]:b - upper["at"]]
        psum = [ctx.enter_context(nc.psum_tensor(f"bank{i}", [P, 2, 512], F32)) for i in range(4)]

        def bank(n):
            return psum[n // 2][:, n % 2, :]

        class Region:

            def __init__(self, at, end=ARENA):
                self.at, self.end = at, end

            def take(self, *dims):
                n = 1
                for d in dims:
                    n *= d
                if self.at < LOWER < self.at + n:
                    self.at = LOWER
                ap = at_words(self.at, self.at + n)
                self.at += n
                assert self.at <= self.end, (self.at, self.end)
                if len(dims) == 2:
                    ap = ap.rearrange("p (a b) -> p a b", a=dims[0])
                elif len(dims) == 3:
                    ap = ap.rearrange("p (a b c) -> p a b c", a=dims[0], b=dims[1])
                return ap

        base = 3904
        keep = Region(0, base)
        ident = keep.take(128)
        ones = keep.take(128)
        blk = keep.take(128)
        tri_c = keep.take(128)
        up_bd = keep.take(128)
        low32 = keep.take(128)
        up32 = keep.take(128)
        up_off = keep.take(128)
        tri_w = keep.take(64)
        id_w = keep.take(64)
        sel2 = keep.take(2)
        vec = keep.take(128)
        mod_t = keep.take(48, 2)
        g1 = keep.take(8, 2)
        head_of = keep.take(KD, 16)
        of_head = keep.take(KD, 128)
        tri_g = keep.take(128)
        tri_bd = keep.take(128)
        VOFF = {}
        at = 0
        for name, n in (("mu", 26), ("shift", 26), ("norm1", 8), ("a0", 8), ("kk", 8), ("ka", 8), ("rk", 8),
                        ("lng", 8), ("lnb", 8), ("glan", 2)):
            VOFF[name] = (at, n)
            at += n
        NVEC = at

        def vcol(name, k):
            return vec[:, VOFF[name][0] + k:VOFF[name][0] + k + 1]

        def vcols(name):
            o, n = VOFF[name]
            return vec[:, o:o + n]

        mod_dram = scratch("mod_rows", (2, 6 * D))
        gla_dram = scratch("gla_qkv", (GL_TILES, P, T))
        gate_dram = scratch("gates", (GT_TILES, P, T))
        xa_dram = scratch("gla_xa", (GATE_RANK, T))
        xs_dram = scratch("expert_in", (32 * 64 + 2 * 5 * P, D))
        ys_dram = scratch("expert_out", (32 * 64, D))

        R = Region(base)
        p_rw = R.take(RW_TILES, TP)
        h_t = R.take(KD, TP)
        free_at = R.at

        lay_out_upper(1)
        S1 = Region(free_at)
        x_tok = S1.take(5, D)
        NSL = 4
        NRND = 6 * D // 512 // NSL
        w_ada_s = [S1.take(KD, 512) for _ in range(NSL)]
        parts = [S1.take(512) for _ in range(NSL)]
        sq_junk = S1.take(D)
        S1b = Region(base, free_at - KD * TP)
        b_rows = S1b.take(P)
        b_t = S1b.take(48)
        c_row = S1b.take(D)
        c_sig = S1.take(D)
        c_t = S1.take(KD, 32)
        mod_rows = S1b.take(2, P)
        vrow = keep.take(128)
        ssq = keep.take(8)
        rstd = keep.take(8)

        consts_done = sem("consts_done")
        pool_step = sem("pool_step")
        small_in = sem("small_in")
        x_in = sem("x_in")
        ada_in = [sem(f"ada_in{u}") for u in range(NSL)]
        ada_done = sem("ada_done")
        parts_done = sem("parts_done")
        cols_mm = sem("cols_mm")
        b_tr = sem("b_tr")
        b_t_done = sem("b_t_done")
        x_t_done = sem("x_t_done")
        c_sig_done = sem("c_sig_done")
        c_silu_done = sem("c_silu_done")
        c_tr = sem("c_tr")
        c_t_done = sem("c_t_done")
        vec_tr = sem("vec_tr")
        vec_done = sem("vec_done")
        row_mm = sem("row_mm")
        row_done = sem("row_done")
        modt_done = sem("modt_done")
        g1_done = sem("g1_done")
        ssq_done = sem("ssq_done")
        ms_done = sem("ms_done")
        std_done = sem("std_done")
        rstd_done = sem("rstd_done")
        xn_done = sem("xn_done")
        x_tr = sem("x_tr")
        h_done = sem("h_done")
        v_step = sem("v_step")
        mod_out = sem("mod_out")
        zero_done = sem("zero_done")

        w_ada_v = I["w_ada"][0].rearrange("(k p) n -> p k n", p=P)
        with nc.Block() as block:
            @block.sync
            def _(sp):
                sp.dma_start(c_row[0:1, :], I["c_prompt"]).then_inc(small_in, 16)
                sp.dma_start(c_row[1:2, :], I["c_sample"]).then_inc(small_in, 16)
                for name, key in (("mu", "rwkv_mu"), ("norm1", "norm1_g"), ("a0", "rwkv_a0"), ("kk", "rwkv_k_k"),
                                  ("ka", "rwkv_k_a"), ("lng", "rwkv_ln_g"), ("lnb", "rwkv_ln_b"),
                                  ("glan", "gla_norm_g")):
                    o, n = VOFF[name]
                    sp.dma_start(vrow[o:o + n, :], I[key].rearrange("a (n p) -> (a n) p", p=P)).then_inc(small_in, 16)
                o, n = VOFF["rk"]
                sp.dma_start(vrow[o:o + n, :], I["rwkv_r_k"].rearrange("a (n h) d -> (a n) (h d)", h=2)
                             ).then_inc(small_in, 16)
                o, n = VOFF["shift"]
                sp.dma_start(vrow[o:o + n, :], I["state_rwkv_shift"].rearrange("a b c (n p) -> (a b c n) p", p=P)
                             ).then_inc(small_in, 16)
                sp.dma_start(b_rows[0:48, :], I["b_ada"].rearrange("a (n p) -> (a n) p", p=P)).then_inc(small_in, 16)
                with sp.Fori(0, NRND) as i:
                    for u in range(NSL):
                        sp.wait_ge(ada_done, NSL * i + (u + 1))
                        sp.dma_start(w_ada_s[u], w_ada_v[:, :, ds(i * (NSL * 512) + u * 512, 512)]
                                     ).then_inc(ada_in[u], 16)

            @block.gpsimd
            def _(pool):
                pool.dma_start(x_tok[:, 0:4, :], I["x_prompt"][0].rearrange("(j p) d -> p j d", p=P)
                               ).then_inc(x_in, 16)
                pool.dma_start(x_tok[0:DEC, 4, :], I["x_sample"][0]).then_inc(x_in, 16)
                steps = [0]

                def step(ins):
                    ins.then_inc(pool_step, 1)
                    steps[0] += 1
                    pool.wait_ge(pool_step, steps[0])

                for t, v in ((ident, 0.0), (ones, 1.0), (blk, 0.0), (tri_c, 0.0), (tri_w, 1.0), (id_w, 0.0),
                             (sel2, 0.0)):
                    step(pool.memset(t, v))
                for h in (0, 64):
                    b = slice(h, h + 64)
                    step(pool.memset(blk[b, b], 1.0))
                    step(pool.memset(tri_c[b, b], DECAY_SCALE))
                    step(pool.affine_select(out=tri_w[b, :], in_=tri_w[b, :], compare_op=ALU.is_ge, fill=0.0,
                                            base=0, pattern=[[1, 64]], channel_multiplier=-1))
                    step(pool.affine_select(out=id_w[b, :], in_=id_w[b, :], compare_op=ALU.not_equal,
                                            fill=1.0, base=0, pattern=[[1, 64]], channel_multiplier=-1))
                for g in range(4):
                    b = slice(32 * g, 32 * g + 32)
                    step(pool.affine_select(out=sel2[b, :], in_=sel2[b, :], compare_op=ALU.not_equal, fill=1.0,
                                            base=0, pattern=[[1, 2]], channel_multiplier=-1))
                step(pool.affine_select(out=ident, in_=ident, compare_op=ALU.not_equal, fill=1.0, base=0,
                                        pattern=[[1, 128]], channel_multiplier=-1))
                step(pool.affine_select(out=tri_c, in_=tri_c, compare_op=ALU.is_ge, fill=0.0, base=0,
                                        pattern=[[1, 128]], channel_multiplier=-1))
                step(pool.affine_select(out=up_bd, in_=blk, compare_op=ALU.is_gt, fill=0.0, base=0,
                                        pattern=[[1, 128]], channel_multiplier=-1))
                step(pool.affine_select(out=low32, in_=blk, compare_op=ALU.is_gt, fill=0.0, base=0,
                                        pattern=[[-1, 128]], channel_multiplier=1))
                step(pool.memset(up_off, 0.0))
                for g in range(4):
                    b = slice(32 * g, 32 * g + 32)
                    step(pool.memset(up_off[b, b], 1.0))
                step(pool.tensor_tensor(up32, up_bd, up_off, ALU.mult))
                step(pool.tensor_tensor(low32, low32, up_off, ALU.mult))
                step(pool.tensor_tensor(up_off, up_bd, up32, ALU.subtract))
                step(pool.affine_select(out=tri_bd, in_=blk, compare_op=ALU.is_ge, fill=0.0, base=0,
                                        pattern=[[1, 128]], channel_multiplier=-1))
                step(pool.tensor_scalar(tri_g, tri_bd, 1.0 / 16, None, ALU.mult))
                step(pool.memset(head_of, 0.0))
                step(pool.memset(of_head[0:16], 0.0))
                for h in range(2):
                    b = slice(64 * h, 64 * h + 64)
                    step(pool.affine_select(out=head_of[b], in_=head_of[b], compare_op=ALU.not_equal, fill=1.0,
                                            base=-h, pattern=[[-2, KD], [1, 16]], channel_multiplier=0))
                    step(pool.affine_select(out=of_head[0:16, :, b], in_=of_head[0:16, :, b],
                                            compare_op=ALU.not_equal, fill=1.0, base=-h,
                                            pattern=[[-2, KD], [0, 64]], channel_multiplier=1))
                pool.sem_inc(consts_done, 1)
                pool.memset(h_t[:, :, T:TP], 0.0).then_inc(zero_done, 1)
                pool.wait_ge(row_done, 1)
                pool.dma_start(mod_dram.rearrange("s (n p) -> n s p", p=P), mod_rows[0:48]).then_inc(mod_out, 16)
                pool.wait_ge(mod_out, 16)

            @block.scalar
            def _(act):
                act.wait_ge(small_in, 16 * 13)
                nc.scalar.activation(c_sig[0:2, :], c_row[0:2, :], ACT.Sigmoid).then_inc(c_sig_done, 1)
                act.sem_inc(parts_done, NSL)
                act.wait_ge(x_in, 32)
                for j, n in TILES:
                    if j:
                        act.wait_ge(ssq_done, j)
                    nc.scalar.activation(sq_junk[0:n, :], x_tok[0:n, j, :], ACT.Square,
                                         accum_out=ssq[0:n, j:j + 1]).then_inc(ssq_done, 1)
                act.wait_ge(ms_done, 2)
                for b, c in ((slice(0, P), slice(0, 4)), (slice(0, DEC), slice(4, 5))):
                    nc.scalar.activation(rstd[b, c], rstd[b, c], ACT.Sqrt).then_inc(std_done, 1)
                with act.Fori(0, NRND) as i:
                    for u in range(NSL):
                        act.wait_ge(ada_done, NSL * i + (u + NSL + 1))
                        act.wait_ge(cols_mm, NSL * i + (u + 1))
                        nc.scalar.activation(parts[u], bank(u), ACT.Copy).then_inc(parts_done, 1)
                act.wait_ge(g1_done, 2)
                for k in range(4, KD):
                    nc.scalar.activation(h_t[:, k, 0:SEQ], h_t[:, k, 0:SEQ], ACT.Identity, scale=g1[:, k, 0:1],
                                         bias=mod_t[:, k, 0:1]).then_inc(h_done, 1)

            @block.tensor
            def _(pe):
                pe.sem_inc(ada_done, NSL)
                pe.sem_inc(cols_mm, NSL)
                pe.wait_ge(consts_done, 1)
                pe.wait_ge(small_in, 16 * 13)
                nc.tensor.transpose(bank(6)[:, 0:NVEC], vrow[0:NVEC, :], ident[0:NVEC, 0:NVEC]).then_inc(vec_tr, 1)
                nc.tensor.transpose(bank(5)[:, 0:48], b_rows[0:48, :], ident[0:48, 0:48]).then_inc(b_tr, 1)
                pe.wait_ge(c_silu_done, 1)
                for k in range(KD):
                    t = nc.tensor.transpose(bank(7)[:, 2 * k:2 * k + 2], c_row[0:2, k * P:(k + 1) * P],
                                            ident[0:2, 0:2])
                t.then_inc(c_tr, 1)
                pe.wait_ge(c_t_done, 1)

                def block_sums(i, u):
                    pe.wait_ge(ada_in[u], 16 * i + 16)
                    pe.wait_ge(parts_done, NSL * i + (u + 1))
                    for k in range(KD):
                        g = k % 4
                        m = nc.tensor.matmul(bank(u)[32 * g:32 * g + 32, :], c_t[:, k, :], w_ada_s[u][:, k, :],
                                             start=k < 4, stop=k >= 4)
                    m.then_inc(ada_done, 1)

                def block_columns(i, u):
                    pe.wait_ge(parts_done, NSL * i + (u + NSL + 1))
                    for q in range(4):
                        m = nc.tensor.matmul(bank(4)[:, ds(i * (8 * NSL) + (8 * u + 2 * q), 2)],
                                             parts[u][:, q * P:(q + 1) * P], sel2, start=True, stop=True)
                    m.then_inc(cols_mm, 1)

                def modulation_round(i):
                    for u in range(NSL):
                        block_sums(i, u)
                        if u:
                            block_columns(i, u - 1)
                    block_columns(i, NSL - 1)

                modulation_round(0)
                pe.wait_ge(xn_done, 5)
                pe.wait_ge(vec_done, 1)
                pe.wait_ge(c_t_done, 1)
                pe.wait_ge(b_t_done, 1)
                for k in range(KD):
                    if k >= 2:
                        pe.wait_ge(x_t_done, k - 1)
                    for j in range(4):
                        t = nc.tensor.transpose(bank(6 + k % 2)[:, j * P:(j + 1) * P],
                                                x_tok[:, j, k * P:(k + 1) * P], ident)
                    t.then_inc(x_tr, 1)
                for k in range(KD):
                    t = nc.tensor.transpose(bank(5)[:, k * DEC:(k + 1) * DEC], x_tok[0:DEC, 4, k * P:(k + 1) * P],
                                            ident[0:DEC, 0:DEC])
                t.then_inc(x_tr, 1)
                with pe.Fori(1, NRND) as i:
                    modulation_round(i)
                pe.wait_ge(modt_done, 1)
                pe.wait_ge(x_t_done, KD)
                for s in range(2):
                    m = nc.tensor.transpose(bank(6)[0:48, s * P:(s + 1) * P], mod_t[:, :, s], ident)
                m.then_inc(row_mm, 1)

            @block.vector
            def _(v):
                v.memset(c_t, 0.0).then_inc(v_step, 1)
                v.wait_ge(c_sig_done, 1)
                nc.vector.tensor_tensor(c_row[0:2, :], c_row[0:2, :], c_sig[0:2, :], ALU.mult
                                        ).then_inc(c_silu_done, 1)
                v.wait_ge(vec_tr, 1)
                nc.vector.tensor_copy(vec[:, 0:NVEC], bank(6)[:, 0:NVEC]).then_inc(vec_done, 1)
                v.wait_ge(b_tr, 1)
                nc.vector.tensor_copy(b_t, bank(5)[:, 0:48]).then_inc(b_t_done, 1)
                v.wait_ge(c_tr, 1)
                v.wait_ge(v_step, 1)
                nc.vector.tensor_copy(c_t[:, :, 0:2], bank(7)[:, 0:16].rearrange("p (k s) -> p k s", s=2)
                                      ).then_inc(c_t_done, 1)
                v.wait_ge(ssq_done, 5)
                for b, c in ((slice(0, P), slice(0, 4)), (slice(0, DEC), slice(4, 5))):
                    nc.vector.tensor_scalar(rstd[b, c], ssq[b, c], 1.0 / D, EPS, ALU.mult, ALU.add
                                            ).then_inc(ms_done, 1)
                v.wait_ge(std_done, 2)
                for b, c in ((slice(0, P), slice(0, 4)), (slice(0, DEC), slice(4, 5))):
                    nc.vector.reciprocal(rstd[b, c], rstd[b, c]).then_inc(rstd_done, 1)
                v.wait_ge(rstd_done, 2)
                for j, n in TILES:
                    nc.vector.tensor_scalar(x_tok[0:n, j, :], x_tok[0:n, j, :], rstd[0:n, j:j + 1], None, ALU.mult
                                            ).then_inc(xn_done, 1)
                for k in range(KD):
                    v.wait_ge(x_tr, k + 1)
                    nc.vector.tensor_copy(h_t[:, k, 0:SEQ], bank(6 + k % 2)).then_inc(x_t_done, 1)
                v.wait_ge(x_tr, KD + 1)
                nc.vector.tensor_copy(h_t[:, :, SEQ:T], bank(5)[:, 0:KD * DEC].rearrange("p (k t) -> p k t", t=DEC)
                                      ).then_inc(x_t_done, 1)
                v.wait_ge(b_t_done, 1)
                v.wait_ge(cols_mm, 12 + NSL)
                nc.vector.tensor_tensor(mod_t, bank(4)[:, 0:96].rearrange("p (n s) -> p n s", s=2),
                                        b_t.unsqueeze(2).broadcast_to([P, 48, 2]), ALU.add).then_inc(modt_done, 1)
                v.wait_ge(modt_done, 1)
                v.wait_ge(vec_done, 1)
                for s in range(2):
                    nc.vector.scalar_tensor_tensor(out=g1[:, :, s], in0=mod_t[:, 8:16, s], scalar=1.0,
                                                   in1=vcols("norm1"), op0=ALU.add, op1=ALU.mult
                                                   ).then_inc(g1_done, 1)
                v.wait_ge(g1_done, 2)
                v.wait_ge(x_t_done, KD + 1)
                for k in range(4):
                    nc.vector.tensor_scalar(h_t[:, k, 0:SEQ], h_t[:, k, 0:SEQ], g1[:, k, 0:1],
                                            mod_t[:, k, 0:1], ALU.mult, ALU.add).then_inc(h_done, 1)
                for k in range(KD):
                    nc.vector.tensor_scalar(h_t[:, k, SEQ:T], h_t[:, k, SEQ:T], g1[:, k, 1:2],
                                            mod_t[:, k, 1:2], ALU.mult, ALU.add).then_inc(h_done, 1)
                v.wait_ge(row_mm, 1)
                nc.vector.tensor_copy(mod_rows[0:48].rearrange("n s p -> n (s p)"), bank(6)[0:48, 0:2 * P]
                                      ).then_inc(row_done, 1)
                v.wait_ge(h_done, 16)

        R_WORDS = 4 * KD * 2 * P + 2 * KD * T
        lay_out_upper(2, R_WORDS)
        S2r = Region(free_at)
        S2 = Region(free_at + R_WORDS)
        w_slot = [S2.take(KD, 2 * P) for _ in range(2)]
        w_high = [S2r.take(KD, 2 * P) for _ in range(2)]
        w_rest = [S2r.take(KD, 2 * P) for _ in range(2)]
        h_high = S2r.take(KD, T)
        h_rest = S2r.take(KD, T)
        stage = [S2.take(2, T) for _ in range(2)]
        xa_w = S2.take(KD, GATE_RANK)
        xa_t = S2.take(T)
        zero_row = S2.take(D)
        w_in_v = I["w_in"][0].rearrange("(k p) n -> p k n", p=P)
        w_loaded = [sem(f"w_loaded{s}") for s in range(2)]
        h_high_done = sem("h_high_done")
        h_split = sem("h_split")
        w_high_done = sem("w_high_done")
        w_split = sem("w_split")
        proj_done = sem("proj_done")
        act_out = sem("act_out")
        dve_out = sem("dve_out")
        spilled = [sem(f"spilled{s}") for s in range(2)]
        xa_in = sem("xa_in")
        xa_done = sem("xa_done")
        xa_out = sem("xa_out")
        pad_done = sem("pad_done")
        xs_zero = sem("xs_zero")

        RUNS = [(0, 13, 0, "rw"), (13, 8, RWKV_PROJ, "gla"), (21, 12, XA_COL + GATE_RANK, "gate")]
        PAIRS = sum(n for _, n, _, _ in RUNS)

        def runs(eng, step):
            for first, n, col, kind in RUNS:
                odd = n % 2
                last = 2 if first + n == PAIRS else 0

                def pair(i, u):
                    q = u + odd + 2 * i
                    step(first + q, (first + odd + u) % 2, col + q * 2 * P, q, kind,
                         (first + odd + u) // 2 + i)
                if odd:
                    step(first, first % 2, col, 0, kind, first // 2)
                with eng.Fori(0, (n - last) // 2) as i:
                    for u in range(2):
                        pair(i, u)
                for u in range(last):
                    pair((n - last) // 2, u)

        def is_last(g):
            return isinstance(g, int) and g == PAIRS - 1

        with nc.Block() as block:
            @block.sync
            def _(sp):
                sp.dma_start(xa_w, w_in_v[:, :, XA_COL:XA_COL + GATE_RANK]).then_inc(xa_in, 16)

                def load(g, s, col, local, kind, use):
                    sp.wait_ge(w_split, g + 1)
                    sp.dma_start(w_slot[s], w_in_v[:, :, ds(col, 2 * P)]).then_inc(w_loaded[s], 16)
                runs(sp, load)

            @block.gpsimd
            def _(pool):
                pool.memset(p_rw[:, :, T:TP], 0.0).then_inc(pad_done, 1)
                pool.memset(zero_row, 0.0).then_inc(pad_done, 1)
                pool.wait_ge(pad_done, 2)
                pool.dma_start(xs_dram[0:32 * 64].rearrange("(n p) d -> p n d", p=P),
                               zero_row.unsqueeze(1).broadcast_to([P, 16, D])).then_inc(xs_zero, 16)
                pool.wait_ge(xs_zero, 16)
                pool.wait_ge(xa_done, 2)
                pool.dma_start(xa_dram, xa_t[0:GATE_RANK, :]).then_inc(xa_out, 16)
                pool.wait_ge(xa_out, 16)
                for s in range(2):
                    pool.wait_ge(spilled[s], 16 * 11)

            @block.tensor
            def _(pe):
                pe.sem_inc(proj_done, 4)

                def project(g, s, col, local, kind, use):
                    pe.wait_ge(w_split, g + 3)
                    for h in range(2):
                        pe.wait_ge(act_out if h == 0 else dve_out, g + 1)
                        for k in range(KD):
                            for w_part, h_part in ((w_high, h_high), (w_high, h_rest), (w_rest, h_high)):
                                for c in range(2):
                                    m = nc.tensor.matmul(psum[2 * s + h][:, c, 0:HALF],
                                                         w_part[s][:, k, h * P:(h + 1) * P],
                                                         h_part[:, k, c * HALF:(c + 1) * HALF],
                                                         start=k == 0 and w_part is w_high and h_part is h_high,
                                                         stop=k == KD - 1 and w_part is w_rest)
                        m.then_inc(proj_done, 1)
                pe.wait_ge(h_split, KD)
                runs(pe, project)
                pe.wait_ge(xa_in, 16)
                pe.wait_ge(act_out, 35)
                for k in range(KD):
                    for c in range(2):
                        m = nc.tensor.matmul(psum[0][0:GATE_RANK, c, 0:HALF], xa_w[:, k, :],
                                             h_t[:, k, c * HALF:(c + 1) * HALF], start=k == 0, stop=k == KD - 1)
                m.then_inc(xa_done, 1)

            def two(ap):
                return ap.rearrange("p (c t) -> p c t", c=2)

            @block.scalar
            def _(act):
                act.sem_inc(act_out, 2)
                act.sem_inc(spilled[0], 16)
                act.sem_inc(spilled[1], 16)

                def split(n, s, use):
                    act.wait_ge(w_loaded[s], 16 * use + 16)
                    act.wait_ge(proj_done, 2 * n + 2)
                    nc.scalar.activation(w_high[s], w_slot[s], ACT.Copy).then_inc(w_high_done, 1)

                for k in range(KD):
                    nc.scalar.activation(h_high[:, k, :], h_t[:, k, 0:T], ACT.Copy).then_inc(h_high_done, 1)
                split(0, 0, 0)

                def out(g, s, col, local, kind, use):
                    if not is_last(g):
                        split(g + 1, 1 - s, use + s)
                    act.wait_ge(proj_done, 2 * g + 5)
                    if kind != "rw":
                        act.wait_ge(spilled[s], 16 * (use - (6 if s == 1 else 7)) + 16)
                    dst = p_rw[:, ds(local * 2, 1), 0:T] if kind == "rw" else stage[s][:, 0:1, :]
                    nc.scalar.activation(dst.rearrange("p a (c t) -> p (a c) t", c=2), psum[2 * s][:, :, 0:HALF], ACT.Copy
                                         ).then_inc(act_out, 1)
                    if kind != "rw":
                        act.wait_ge(act_out, g + 3)
                        act.wait_ge(dve_out, g + 3)
                        dst = gla_dram if kind == "gla" else gate_dram
                        act.dma_start(dst[ds(local * 2, 2), :, :].rearrange("h p t -> p h t"), stage[s]
                                      ).then_inc(spilled[s], 16)
                runs(act, out)

            @block.vector
            def _(v):
                v.sem_inc(dve_out, 2)
                v.sem_inc(w_split, 2)

                def split(n, s):
                    v.wait_ge(w_high_done, n + 1)
                    nc.vector.tensor_tensor(w_rest[s], w_slot[s], w_high[s].bitcast(F32), ALU.subtract).then_inc(w_split, 1)

                for k in range(KD):
                    v.wait_ge(h_high_done, k + 1)
                    nc.vector.tensor_tensor(h_rest[:, k, :], h_t[:, k, 0:T], h_high[:, k, :].bitcast(F32), ALU.subtract
                                            ).then_inc(h_split, 1)
                split(0, 0)

                def out(g, s, col, local, kind, use):
                    if not is_last(g):
                        split(g + 1, 1 - s)
                    v.wait_ge(proj_done, 2 * g + 6)
                    if kind != "rw":
                        v.wait_ge(spilled[s], 16 * (use - (6 if s == 1 else 7)) + 16)
                    dst = p_rw[:, ds(local * 2 + 1, 1), 0:T] if kind == "rw" else stage[s][:, 1:2, :]
                    nc.vector.tensor_copy(dst.rearrange("p a (c t) -> p (a c) t", c=2), psum[2 * s + 1][:, :, 0:HALF]
                                          ).then_inc(dve_out, 1)
                runs(v, out)
                v.wait_ge(xa_done, 1)
                nc.vector.tensor_copy(two(xa_t[0:GATE_RANK, :]), psum[0][0:GATE_RANK, :, 0:HALF]).then_inc(xa_done, 1)

        lay_out_upper(3)
        S3 = Region(free_at)
        ka = S3.take(KD, TP)
        lam = S3.take(KD, TP)
        chunk_at = S3.at
        kk = h_t
        diff = S3.take(KD, T)
        kk_sq_t = lam
        boost = S3.take(KD, T)
        sig_w = S3.take(5, D)
        w_up = S3.take(D)
        a_up = S3.take(D)
        low_rank = S3.take(T)
        omka = keep.take(8)
        ends = keep.take(52)
        ends_t = keep.take(128)
        lora_in = sem("lora_in")
        ends_done = sem("ends_done")
        ends_tr = sem("ends_tr")
        ends_t_done = sem("ends_t_done")
        ends_out = sem("ends_out")
        diff_step = sem("diff_step")
        mixed = sem("mixed")
        omka_done = sem("omka_done")
        tanh_done = sem("tanh_done")
        filled = sem("filled")
        w_mm = sem("w_mm")
        sig_w_done = sem("sig_w_done")
        a_mm = sem("a_mm")
        a_done = sem("a_done")
        boost_done = sem("boost_done")
        kk_scaled = sem("kk_scaled")
        kk_sq = sem("kk_sq")
        kk_sum = sem("kk_sum")
        kk_clamped = sem("kk_clamped")
        kk_ln = sem("kk_ln")
        kk_rstd = sem("kk_rstd")
        kk_done = sem("kk_done")
        k_done = sem("k_done")
        ka_done = sem("ka_done")
        cum_mm = sem("cum_mm")
        lam_done = sem("lam_done")
        pads3 = sem("pads3")
        MIX = [(24, 26), (8, 16), (0, 8), (16, 24)]

        def halves(ap):
            return ap.rearrange("p (c t) -> p c t", c=2)

        with nc.Block() as block:
            @block.sync
            def _(sp):
                sp.dma_start(w_up[0:64, :], I["rwkv_decay_up"][0]).then_inc(lora_in, 16)
                sp.dma_start(a_up[64:128, :], I["rwkv_aaa_up"][0]).then_inc(lora_in, 16)
                sp.wait_ge(filled, 4)
                sp.dma_start(w_up[64:65, :], I["rwkv_w0"]).then_inc(lora_in, 16)
                sp.wait_ge(ends_t_done, 1)
                for s, o in ((0, O[2]), (1, O[5])):
                    sp.dma_start(o.rearrange("a b c (n p) -> (a b c n) p", p=P), ends_t[26 * s:26 * s + 26, :]
                                 ).then_inc(ends_out, 16)
                sp.wait_ge(ends_out, 32)

            @block.vector
            def _(v):
                for s, t in ((0, SEQ - 1), (1, T - 1)):
                    nc.vector.tensor_copy(ends[:, 26 * s:26 * s + 26], p_rw[:, :, t]).then_inc(ends_done, 1)
                nc.vector.tensor_scalar(omka, vcols("ka"), -1.0, 1.0, ALU.mult, ALU.add).then_inc(omka_done, 1)
                v.wait_ge(ends_done, 2)
                n = d = 0
                for a, b in MIX:
                    m = b - a
                    if d == 1:
                        v.wait_ge(ends_tr, 1)
                        nc.vector.tensor_copy(ends_t[0:52, :], bank(7)[0:52, 0:128]).then_inc(ends_t_done, 1)
                    if d:
                        v.wait_ge(mixed, n)
                    nc.vector.tensor_tensor(diff[:, 0:m, 1:T], p_rw[:, a:b, 0:T - 1], p_rw[:, a:b, 1:T],
                                            ALU.subtract).then_inc(diff_step, 1)
                    nc.vector.tensor_scalar(diff[:, 0:m, 0:1], p_rw[:, a:b, 0:1], -1.0, None, ALU.mult
                                            ).then_inc(diff_step, 1)
                    d += 1
                    v.wait_ge(diff_step, 3 * d - 1)
                    o = VOFF["shift"][0]
                    nc.vector.tensor_tensor(diff[:, 0:m, SEQ], vec[:, o + a:o + b], p_rw[:, a:b, SEQ], ALU.subtract
                                            ).then_inc(diff_step, 1)
                    v.wait_ge(diff_step, 3 * d)
                    for f in range(a, b):
                        nc.vector.scalar_tensor_tensor(out=p_rw[:, f, 0:T], in0=diff[:, f - a, :],
                                                       scalar=vcol("mu", f), in1=p_rw[:, f, 0:T], op0=ALU.mult,
                                                       op1=ALU.add).then_inc(mixed, 1)
                        n += 1
                    if a == 8:
                        for k in range(KD):
                            v.wait_ge(mixed, 2 + k + 1)
                            nc.vector.tensor_scalar(kk[:, k, :], p_rw[:, 8 + k, :], vcol("kk", k), None, ALU.mult
                                                    ).then_inc(kk_scaled, 1)
                for k in range(KD):
                    v.wait_ge(kk_sum, k + 1)
                    nc.vector.tensor_scalar(halves(kk_sq_t[:, k, 0:T]), psum[2 + k % 2][:, :, 0:HALF], 1e-24, None,
                                            ALU.max).then_inc(kk_clamped, 1)
                for k in range(KD):
                    v.wait_ge(kk_rstd, k + 1)
                    nc.vector.tensor_tensor(kk[:, k, 0:T], kk[:, k, 0:T], kk_sq_t[:, k, 0:T], ALU.mult
                                            ).then_inc(kk_done, 1)
                for k in range(KD // 2, KD):
                    v.wait_ge(kk_done, k + 1)
                    v.wait_ge(boost_done, k + 1)
                    nc.vector.tensor_tensor(ka[:, k, 0:T], ka[:, k, 0:T], kk[:, k, 0:T], ALU.mult).then_inc(ka_done, 1)
                v.wait_ge(ka_done, KD)

            @block.gpsimd
            def _(pool):
                pool.memset(w_up[64:128, :], 0.0).then_inc(filled, 1)
                pool.wait_ge(filled, 1)
                pool.memset(a_up[0:64, :], 0.0).then_inc(filled, 1)
                pool.wait_ge(filled, 2)
                pool.memset(low_rank[64:128, :], 0.0).then_inc(filled, 1)
                pool.wait_ge(filled, 3)
                pool.memset(low_rank[64:65, :], 1.0).then_inc(filled, 1)
                pool.wait_ge(filled, 4)
                pool.memset(ka[:, :, T:TP], 0.0).then_inc(pads3, 1)
                for k in range(KD):
                    pool.wait_ge(boost_done, k + 1)
                    pool.wait_ge(kk_scaled, k + 1)
                    pool.tensor_tensor(p_rw[:, 8 + k, 0:T], p_rw[:, 8 + k, 0:T], boost[:, k, :], ALU.mult
                                       ).then_inc(k_done, 1)
                for k in range(KD // 2):
                    pool.wait_ge(kk_done, k + 1)
                    pool.tensor_tensor(ka[:, k, 0:T], ka[:, k, 0:T], kk[:, k, 0:T], ALU.mult).then_inc(ka_done, 1)
                pool.wait_ge(ka_done, KD)

            @block.scalar
            def _(act):
                act.wait_ge(mixed, 2)
                nc.scalar.activation(low_rank[0:64, :], p_rw[0:64, 24, 0:T], ACT.Tanh).then_inc(tanh_done, 1)
                nc.scalar.activation(p_rw[:, 25, 0:T], p_rw[:, 25, 0:T], ACT.Sigmoid).then_inc(tanh_done, 1)
                q = 0
                for j, n in TILES:
                    for c in range(2):
                        act.wait_ge(w_mm, q + 1)
                        nc.scalar.activation(sig_w[0:n, j, c * 512:(c + 1) * 512], bank(q % 2)[0:n, :], ACT.Sigmoid
                                             ).then_inc(sig_w_done, 1)
                        q += 1
                act.wait_ge(omka_done, 1)
                for k in range(KD):
                    act.wait_ge(a_mm, k + 1)
                    nc.scalar.activation(halves(ka[:, k, 0:T]), psum[1 + k % 2][:, :, 0:HALF], ACT.Sigmoid,
                                         bias=vcol("a0", k)).then_inc(a_done, 1)
                    act.wait_ge(a_done, k + 1)
                    nc.scalar.activation(boost[:, k, :], ka[:, k, 0:T], ACT.Identity, scale=vcol("ka", k),
                                         bias=omka[:, k:k + 1]).then_inc(boost_done, 1)
                for k in range(KD):
                    act.wait_ge(kk_scaled, k + 1)
                    nc.scalar.activation(kk_sq_t[:, k, 0:T], kk[:, k, 0:T], ACT.Square).then_inc(kk_sq, 1)
                for k in range(KD):
                    act.wait_ge(kk_clamped, k + 1)
                    nc.scalar.activation(kk_sq_t[:, k, 0:T], kk_sq_t[:, k, 0:T], ACT.Ln).then_inc(kk_ln, 1)
                for k in range(KD):
                    act.wait_ge(kk_ln, k + 1)
                    nc.scalar.activation(kk_sq_t[:, k, 0:T], kk_sq_t[:, k, 0:T], ACT.Exp, scale=-0.5
                                         ).then_inc(kk_rstd, 1)
                act.wait_ge(kk_done, KD)
                for k in range(KD):
                    act.wait_ge(cum_mm, k + 1)
                    nc.scalar.activation(lam[:, k, 0:SEQ], bank(k % 2), ACT.Copy).then_inc(lam_done, 1)
                act.wait_ge(cum_mm, KD + 1)
                nc.scalar.activation(lam[:, :, SEQ:TP], bank(2).rearrange("p (k t) -> p k t", t=CH), ACT.Copy
                                     ).then_inc(lam_done, 1)

            @block.tensor
            def _(pe):
                pe.wait_ge(ends_done, 2)
                nc.tensor.transpose(bank(7)[0:52, 0:128], ends, ident).then_inc(ends_tr, 1)
                pe.wait_ge(lora_in, 48)
                pe.wait_ge(filled, 4)
                pe.wait_ge(tanh_done, 1)
                q = 0
                for j, n in TILES:
                    for c in range(2):
                        if q >= 2:
                            pe.wait_ge(sig_w_done, q - 1)
                        o = bank(q % 2)[0:n, :]
                        nc.tensor.matmul(o, low_rank[:, j * P:j * P + n], w_up[:, c * 512:(c + 1) * 512],
                                         start=True, stop=True).then_inc(w_mm, 1)
                        q += 1
                for k in range(KD):
                    if k >= 2:
                        pe.wait_ge(a_done, k - 1)
                    for c in range(2):
                        m = nc.tensor.matmul(psum[1 + k % 2][:, c, 0:HALF], a_up[:, k * P:(k + 1) * P],
                                             p_rw[:, 24, c * HALF:(c + 1) * HALF], start=True, stop=True)
                    m.then_inc(a_mm, 1)
                pe.wait_ge(ends_t_done, 1)
                pe.wait_ge(a_done, KD)
                for k in range(KD):
                    pe.wait_ge(kk_sq, k + 1)
                    if k >= 2:
                        pe.wait_ge(kk_clamped, k - 1)
                    for c in range(2):
                        m = nc.tensor.matmul(psum[2 + k % 2][:, c, 0:HALF], blk, kk_sq_t[:, k, c * HALF:(c + 1) * HALF],
                                             start=True, stop=True)
                    m.then_inc(kk_sum, 1)
                pe.wait_ge(sig_w_done, 10)
                for k in range(KD):
                    if k >= 2:
                        pe.wait_ge(lam_done, k - 1)
                    for j in range(4):
                        m = nc.tensor.matmul(bank(k % 2)[:, j * P:(j + 1) * P], sig_w[:, j, k * P:(k + 1) * P], tri_c,
                                             start=True, stop=True)
                    m.then_inc(cum_mm, 1)
                for k in range(KD):
                    m = nc.tensor.matmul(bank(2)[:, k * CH:(k + 1) * CH], sig_w[0:DEC, 4, k * P:(k + 1) * P],
                                         tri_c[0:DEC, 0:CH], start=True, stop=True)
                m.then_inc(cum_mm, 1)

        clear_semaphores()
        S4 = Region(chunk_at)
        ar = S4.take(8, 192)
        beta = S4.take(8, P)
        kap = S4.take(8, P)
        v_bdt = S4.take(8, P)
        pw = [S4.take(8, P) for _ in range(2)]
        ptt = [S4.take(8, 192) for _ in range(2)]
        inv_t = S4.take(8, P)
        m_t = S4.take(8, P)
        qb = S4.take(8, CH)
        qk = S4.take(8, CH)
        v_bd = S4.take(8, P)
        beta_s = S4.take(8, P)
        kap_s = S4.take(8, P)
        u0 = S4.take(8, P)
        u_bd = S4.take(8, P)
        off_t = u_bd
        w_bd = pw[1]
        s_bd = S4.take(8, P)
        lam_c = S4.take(8, CH)
        lam_i = S4.take(8, CH)
        lam_end = S4.take(8)
        rk_r = u0[:, 0:4].rearrange("p j n -> p (j n)").rearrange("p (j n) -> p j n", n=CH)
        s_tmp = pw[0]
        st_io = pw[0]
        st_c = ptt[0].rearrange("p j n -> p (j n)")[:, 0:8 * CH].rearrange("p (j n) -> p j n", n=CH)

        STEPS = ["NT", "MT", "N", "TR", "TV", "1a", "1b", "2a", "2b", "3a", "3b", "4a", "4b", "5",
                 "U0", "W", "E", "U", "Y", "S"]
        OUTS = {"NT": 3, "MT": 2, "TR": 2, "TV": 2, "2a": 2, "3a": 2, "5": 2}
        UNITS = [(step, g) for step in STEPS for g in range(2)]
        NU = len(UNITS)
        PER = [sum(OUTS.get(st, 1) for st, _ in UNITS[s::4]) for s in range(4)]

        def unit(step, g):
            return UNITS.index((step, g))

        def copied(n):
            return sum(OUTS.get(st, 1) for st, _ in UNITS[n % 4:n + 1:4])

        units_done = sem("units_done")
        emptied = [sem(f"emptied{s}") for s in range(4)]
        lam_c_done = sem("lam_c_done")
        prep_done = sem("prep_done")
        rk_step = sem("rk_step")
        tt_done = sem("tt_done")
        lam_end_done = sem("lam_end_done")
        s_done = sem("s_done")
        zeroed = sem("zeroed")
        NPREP = 12
        def wait_unit(eng, c, step, g):
            eng.wait_ge(units_done, c * NU + (unit(step, g) + 2))

        def wait_copied(eng, c, step, g):
            n = unit(step, g)
            eng.wait_ge(emptied[n % 4], c * PER[n % 4] + (copied(n) + 1))

        def wait_banks(eng, c, step, g, *sources):
            n = unit(step, g)
            counts = {n % 4: copied(n) - OUTS.get(step, 1)}
            for source in sources:
                m = unit(source, g)
                counts[m % 4] = max(counts.get(m % 4, 0), copied(m))
            for s, count in counts.items():
                eng.wait_ge(emptied[s], c * PER[s] + (count + 1))

        def quads(ap, g):
            return ap[:, 4 * g:4 * g + 4]

        def wide(s):
            return psum[s][:, :, 0:384].rearrange("p b (q n) -> p b q n", n=192)

        def by22(ap, g, a, b):
            return ap[:, 4 * g:4 * g + 4, a:b].rearrange("p (b q) n -> p b q n", b=2)

        def mask22(m, n):
            return m.unsqueeze(1).unsqueeze(1).broadcast_to([P, 2, 2, n])

        HALVES = [(slice(0, 64), slice(0, 64)), (slice(64, 128), slice(64, 128))]

        def chunks(eng, body, which):
            if which == "prompt":
                with eng.Fori(0, NCH) as c:
                    body(c, True)
            else:
                body(NCH, False)

        def rwkv_chunks(which):
            with nc.Block() as block:
                @block.scalar
                def _(act):
                    if which == "prompt":
                        for s in range(4):
                            act.sem_inc(emptied[s], 1)
                        act.wait_ge(zeroed, 5)

                    def decays(c):
                        nc.scalar.activation(lam_c, lam[:, :, ds(c * CH, CH)], ACT.Exp).then_inc(lam_c_done, 1)
                        nc.scalar.activation(lam_i, lam[:, :, ds(c * CH, CH)], ACT.Exp, scale=-1.0
                                             ).then_inc(lam_c_done, 1)

                    def values(c):
                        for p, h in HALVES:
                            nc.scalar.activation(v_bdt[p, :, h], p_rw[p, 16:24, ds(c * CH, CH)], ACT.Copy
                                                 ).then_inc(prep_done, 1)

                    if which == "prompt":
                        decays(0)
                        values(0)

                    def chunk(c, more):
                        t0 = c * CH
                        for step, g in UNITS:
                            n = unit(step, g)
                            s = n % 4
                            if step in ("NT", "MT", "N", "1a", "2a", "3a", "4a", "5", "E", "S"):
                                continue
                            wait_unit(act, c, step, g)
                            if more and (step, g) == ("3b", 0):
                                act.wait_ge(lam_end_done, c + 1)
                                act.wait_ge(prep_done, c * NPREP + NPREP)
                                decays(c + 1)
                            if more and (step, g) == ("4b", 0):
                                values(c + 1)
                            if step == "TR":
                                for b, dst in ((0, beta_s), (1, kap_s)):
                                    nc.scalar.activation(quads(dst, g), psum[s][:, b, :].rearrange(
                                        "p (q n) -> p q n", n=P), ACT.Copy).then_inc(emptied[s], 1)
                            elif step == "TV":
                                nc.scalar.activation(quads(v_bd, g), psum[s][:, 0, :].rearrange(
                                    "p (q n) -> p q n", n=P), ACT.Copy).then_inc(emptied[s], 1)
                            elif step in ("1b", "2b", "3b", "4b"):
                                nc.scalar.activation(quads(pw[int(step[0]) % 2], g), psum[s][:, 0, :].rearrange(
                                    "p (q n) -> p q n", n=P), ACT.Copy).then_inc(emptied[s], 1)
                            elif step == "U0":
                                nc.scalar.activation(quads(u0, g), psum[s][:, 0, :].rearrange(
                                    "p (q n) -> p q n", n=P), ACT.Copy).then_inc(emptied[s], 1)
                            elif step in ("W", "U"):
                                nc.scalar.activation(quads(w_bd if step == "W" else u_bd, g), psum[s][:, 0, :].rearrange(
                                    "p (q n) -> p q n", n=P), ACT.Copy).then_inc(emptied[s], 1)
                            elif step == "Y":
                                nc.scalar.activation(p_rw[:, 4 * g:4 * g + 4, ds(t0, CH)],
                                                     psum[s][:, 0, 0:256].rearrange("p (q n) -> p q n", n=CH),
                                                     ACT.Copy).then_inc(emptied[s], 1)
                    chunks(act, chunk, which)

                @block.vector
                def _(v):
                    if which == "prompt":
                        v.memset(s_bd, 0.0).then_inc(s_done, 2)
                        for t in (ar, beta):
                            v.memset(t, 0.0).then_inc(zeroed, 1)
                        v.wait_ge(zeroed, 5)
                        v.wait_ge(s_done, 2)

                    def keys(c):
                        t0 = c * CH
                        v.wait_ge(lam_c_done, c * 2 + 2)
                        for p, h in HALVES:
                            nc.vector.tensor_tensor(beta[p, :, h], ka[p, :, ds(t0, CH)], lam_i[p, :, :], ALU.mult
                                                    ).then_inc(prep_done, 1)
                            nc.vector.tensor_tensor(kap[p, :, h], p_rw[p, 8:16, ds(t0, CH)], lam_i[p, :, :], ALU.mult
                                                    ).then_inc(prep_done, 1)

                    def bonus(c):
                        t0 = c * CH
                        nc.vector.tensor_tensor(rk_r, p_rw[:, 0:8, ds(t0, CH)], p_rw[:, 8:16, ds(t0, CH)], ALU.mult
                                                ).then_inc(rk_step, 1)
                        v.wait_ge(rk_step, c + 1)
                        nc.vector.tensor_tensor(rk_r, rk_r, vcols("rk").unsqueeze(2).broadcast_to([P, 8, CH]),
                                                ALU.mult).then_inc(prep_done, 1)

                    def queries(c):
                        t0 = c * CH
                        for p, h in HALVES:
                            nc.vector.tensor_scalar(ar[p, :, h.start:h.start + 1], kk[p, :, ds(t0, 1)], -1.0, None,
                                                    ALU.mult).then_inc(prep_done, 1)
                            nc.vector.scalar_tensor_tensor(out=ar[p, :, h.start + 1:h.stop],
                                                           in0=kk[p, :, ds(t0 + 1, CH - 1)], scalar=-1.0,
                                                           in1=lam_c[p, :, 0:CH - 1], op0=ALU.mult, op1=ALU.mult
                                                           ).then_inc(prep_done, 1)
                        nc.vector.tensor_tensor(ar[:, :, P:192], p_rw[:, 0:8, ds(t0, CH)], lam_c, ALU.mult
                                                ).then_inc(prep_done, 1)

                    if which == "prompt":
                        keys(0)
                        bonus(0)
                        queries(0)

                    def chunk(c, more):
                        t0 = c * CH
                        v.wait_ge(lam_c_done, c * 2 + 2)
                        v.wait_ge(s_done, c * 2 + 2)
                        nc.vector.tensor_copy(lam_end, lam_c[:, :, CH - 1]).then_inc(lam_end_done, 1)
                        for step, g in UNITS:
                            n = unit(step, g)
                            s = n % 4
                            if step in ("TR", "U0", "W", "U", "Y", "1b", "2b", "3b", "4b"):
                                continue
                            if more and (step, g) == ("4a", 0):
                                keys(c + 1)
                            if more and (step, g) == ("S", 0):
                                wait_unit(v, c, "U", 1)
                                bonus(c + 1)
                                wait_unit(v, c, "Y", 1)
                                queries(c + 1)
                            wait_unit(v, c, step, g)
                            if step in ("NT", "MT"):
                                low = qb if step == "NT" else qk
                                for bd, mask in ((ptt[0], up32), (off_t, up_off)) if step == "NT" else ((m_t, up_bd),):
                                    nc.vector.tensor_tensor(by22(bd, g, 0, P), wide(s)[:, :, :, 0:P], mask22(mask, P),
                                                            ALU.mult).then_inc(emptied[s], 1)
                                nc.vector.tensor_tensor(by22(low, g, 0, CH), wide(s)[:, :, :, P:192],
                                                        mask22(tri_w, CH), ALU.mult).then_inc(emptied[s], 1)
                            elif step == "N":
                                nc.vector.tensor_tensor(quads(pw[0], g), psum[s][:, 0, :].rearrange(
                                    "p (q n) -> p q n", n=P), low32.unsqueeze(1).broadcast_to([P, 4, P]), ALU.mult
                                    ).then_inc(emptied[s], 1)
                            elif step == "TV":
                                nc.vector.tensor_tensor(p_rw[:, 16 + 4 * g:20 + 4 * g, ds(t0, CH)],
                                                        p_rw[:, 16 + 4 * g:20 + 4 * g, ds(t0, CH)],
                                                        psum[s][:, 1, 0:256].rearrange("p (q n) -> p q n", n=CH),
                                                        ALU.mult).then_inc(emptied[s], 1)
                            elif step == "1a":
                                nc.vector.tensor_copy(ptt[1][:, 4 * g:4 * g + 4, 0:P], psum[s][:, 0, :].rearrange(
                                    "p (q n) -> p q n", n=P)).then_inc(emptied[s], 1)
                            elif step in ("2a", "3a", "4a"):
                                k = int(step[0])
                                if k < 4:
                                    nc.vector.tensor_copy(by22(ptt[k % 2], g, 0, P), wide(s)[:, :, :, 0:P]
                                                          ).then_inc(emptied[s], 1)
                                if k == 2:
                                    v.wait_ge(tt_done, c * 4 + (2 * g + 2))
                                else:
                                    wait_copied(v, c, f"{k - 1}a", g)
                                nc.vector.tensor_tensor(by22(ptt[k % 2], g, P, 192), by22(ptt[1 - k % 2], g, P, 192),
                                                        wide(s)[:, :, :, P:192], ALU.add).then_inc(emptied[s], 1)
                            elif step == "E":
                                nc.vector.tensor_tensor(quads(u0, g), quads(u0, g), psum[s][:, 0, :].rearrange(
                                    "p (q n) -> p q n", n=P), ALU.add).then_inc(emptied[s], 1)
                            elif step == "5":
                                wait_copied(v, c, "4a", g)
                                for p, h in HALVES:
                                    nc.vector.tensor_tensor(inv_t[p, 4 * g:4 * g + 4, h],
                                                            ptt[0][p, 4 * g:4 * g + 4, P:192],
                                                            psum[s][p, 0, 0:256].rearrange("p (q n) -> p q n", n=CH),
                                                            ALU.add).then_inc(emptied[s], 1)
                            elif step == "S":
                                v.wait_ge(lam_end_done, c + 1)
                                nc.vector.tensor_tensor(quads(s_tmp, g), quads(s_bd, g),
                                                        psum[s][:, 0, :].rearrange("p (q n) -> p q n", n=P),
                                                        ALU.add).then_inc(emptied[s], 1)
                                wait_copied(v, c, "S", g)
                                nc.vector.tensor_tensor(quads(s_bd, g), quads(s_tmp, g),
                                                        lam_end[:, 4 * g:4 * g + 4].unsqueeze(2)
                                                        .broadcast_to([P, 4, P]), ALU.mult).then_inc(s_done, 1)
                    chunks(v, chunk, which)
                    v.wait_ge(s_done, 18 + (0 if which == "prompt" else 2))

                @block.gpsimd
                def _(pool):
                    if which == "prompt":
                        for t in (kap, v_bdt, inv_t):
                            pool.memset(t, 0.0).then_inc(zeroed, 1)
                        pool.wait_ge(zeroed, 5)

                    def chunk(c, more):
                        for g in range(2):
                            wait_copied(pool, c, "NT", g)
                            for p, h in HALVES:
                                pool.tensor_tensor(ptt[1][p, 4 * g:4 * g + 4, P:192], ptt[0][p, 4 * g:4 * g + 4, h],
                                                   id_w[p, :].unsqueeze(1).broadcast_to([64, 4, CH]), ALU.add
                                                   ).then_inc(tt_done, 1)
                    chunks(pool, chunk, which)

                @block.tensor
                def _(pe):
                    if which == "prompt":
                        pe.sem_inc(units_done, 1)
                        pe.wait_ge(zeroed, 5)

                    mm = nc.tensor.matmul

                    def chunk(c, more):
                        pe.wait_ge(prep_done, c * NPREP + NPREP)
                        for step, g in UNITS:
                            n = unit(step, g)
                            s = n % 4
                            k = int(step[0]) if step[0].isdigit() else 0
                            sources = {"U0": ("MT", "TV"), "W": ("5", "U0"), "E": ("NT", "W"), "U": ("E",),
                                       "Y": ("U",), "S": ("TR", "U")}.get(step, ())
                            if k == 1:
                                sources = ("NT", "N")
                            elif k:
                                sources = (f"{k - 1}a", f"{k - 1}b")
                            wait_banks(pe, c, step, g, *sources)
                            if k == 2:
                                pe.wait_ge(tt_done, c * 4 + (2 * g + 2))
                            if step == "U0":
                                pe.wait_ge(s_done, c * 2 + (g + 1))
                            if step == "TV":
                                mm(psum[s][:, 1, 0:256], blk, quads(rk_r, g), start=True, stop=True)
                            for q in range(4):
                                j = 4 * g + q
                                narrow = psum[s][:, 0, q * P:(q + 1) * P]
                                short = psum[s][:, 0, q * CH:(q + 1) * CH]
                                broad = wide(s)[:, q // 2, q % 2, :]
                                cur, pt = pw[(k + 1) % 2], ptt[(k + 1) % 2]
                                if step == "NT":
                                    m = mm(broad, beta[:, j, :], ar[:, j, :], start=True, stop=True)
                                elif step == "MT":
                                    m = mm(broad, kap[:, j, :], ar[:, j, :], start=True, stop=True)
                                elif step == "N":
                                    m = mm(narrow, ar[:, j, 0:P], beta[:, j, :], start=True, stop=True)
                                elif step == "TR":
                                    nc.tensor.transpose(narrow, beta[:, j, :], ident)
                                    m = nc.tensor.transpose(psum[s][:, 1, q * P:(q + 1) * P], kap[:, j, :], ident)
                                elif step == "TV":
                                    m = nc.tensor.transpose(narrow, v_bdt[:, j, :], ident)
                                elif step == "1a":
                                    m = mm(narrow, cur[:, j, :], pt[:, j, 0:P], start=True, stop=True)
                                elif step in ("2a", "3a"):
                                    m = mm(broad, cur[:, j, :], pt[:, j, :], start=True, stop=True)
                                elif step == "4a":
                                    m = mm(broad[:, P:192], cur[:, j, :], pt[:, j, P:192], start=True, stop=True)
                                elif step in ("1b", "2b", "3b", "4b"):
                                    m = mm(narrow, pt[:, j, 0:P], cur[:, j, :], start=True, stop=True)
                                elif step == "5":
                                    m = mm(short, cur[:, j, :], pt[:, j, P:192], start=True, stop=True)
                                elif step == "U0":
                                    mm(narrow, ar[:, j, 0:P], s_bd[:, j, :], start=True, stop=False)
                                    m = mm(narrow, m_t[:, j, :], v_bd[:, j, :], start=False, stop=True)
                                elif step in ("W", "U"):
                                    m = mm(narrow, inv_t[:, j, :], u0[:, j, :], start=True, stop=True)
                                elif step == "E":
                                    m = mm(narrow, off_t[:, j, :], w_bd[:, j, :], start=True, stop=True)
                                elif step == "Y":
                                    mm(short, s_bd[:, j, :], ar[:, j, P:192], start=True, stop=False)
                                    mm(short, u_bd[:, j, :], qb[:, j, :], start=False, stop=False)
                                    m = mm(short, v_bd[:, j, :], qk[:, j, :], start=False, stop=True)
                                elif step == "S":
                                    mm(narrow, beta_s[:, j, :], u_bd[:, j, :], start=True, stop=False)
                                    m = mm(narrow, kap_s[:, j, :], v_bd[:, j, :], start=False, stop=True)
                            m.then_inc(units_done, 1)
                    chunks(pe, chunk, which)

        st_in = sem("st_in")
        st_packed = [sem(f"st_packed{i}") for i in range(2)]
        st_tr = [sem(f"st_tr{i}") for i in range(2)]
        st_rows = [sem(f"st_rows{i}") for i in range(2)]
        st_out = sem("st_out")
        st_new_tr = sem("st_new_tr")
        st_bd = sem("st_bd")
        st_rows_out = st_io[0:64]
        st_rows_in = pw[1][0:64]

        def rwkv_state(n, out, load):
            with nc.Block() as block:
                @block.sync
                def _(sp):
                    if load is not None:
                        sp.dma_start(st_rows_in.rearrange("i j (h d) -> i (j h) d", h=2),
                                     load[0, 0].rearrange("h i d -> i h d")).then_inc(st_in, 16)
                    sp.wait_ge(st_rows[n], 2)
                    sp.dma_start(out[0, 0].rearrange("h i d -> i h d"),
                                 st_rows_out.rearrange("i j (h d) -> i (j h) d", h=2)).then_inc(st_out, 16)
                    sp.wait_ge(st_out, 16 * n + 16)

                @block.tensor
                def _(pe):
                    pe.wait_ge(st_packed[n], 2)
                    for j in range(8):
                        m = nc.tensor.transpose(psum[0][0:64, j // 4, (j % 4) * P:(j % 4 + 1) * P], st_c[:, j, :],
                                                ident)
                    m.then_inc(st_tr[n], 1)
                    if load is not None:
                        pe.wait_ge(st_in, 16)
                        for j in range(8):
                            m = nc.tensor.transpose(psum[1][:, 0, j * CH:(j + 1) * CH], st_rows_in[:, j, :],
                                                    ident[0:64, 0:64])
                        m.then_inc(st_new_tr, 1)

                @block.vector
                def _(v):
                    for p, h in HALVES:
                        nc.vector.tensor_copy(st_c[p], s_bd[p, :, h]).then_inc(st_packed[n], 1)
                    v.wait_ge(st_tr[n], 1)
                    for b in range(2):
                        nc.vector.tensor_copy(st_rows_out[:, 4 * b:4 * b + 4, :].rearrange("i q d -> i (q d)"),
                                              psum[0][0:64, b, :]).then_inc(st_rows[n], 1)
                    if load is not None:
                        v.wait_ge(st_new_tr, 1)
                        new = psum[1][:, 0, :].rearrange("p (j i) -> p j i", i=CH)
                        for p, h in HALVES:
                            nc.vector.tensor_copy(s_bd[p, :, h], new[p]).then_inc(st_bd, 1)
                        v.wait_ge(st_bd, 2)

        rwkv_chunks("prompt")
        rwkv_state(0, O[3], I["state_rwkv"])
        rwkv_chunks("sample")
        rwkv_state(1, O[6], None)
        y_r = p_rw[:, 0:8]
        S5 = Region(free_at)
        sq = S5.take(KD, T)
        gate_up = S5.take(D)
        NG = 4
        DV = 256
        S56 = Region(S5.at)
        TQ = 5 * P
        xa = S56.take(T)
        alpha_up = S56.take(512)
        z = S56.take(5, 512)
        ez = S56.take(5, 512)
        gla_kept = S56.at
        qk = S56.take(8, TQ)
        v_t = S56.take(8, TQ)
        b_t = S56.take(NG, TQ)
        b_mid = S56.take(NG, TQ)
        gate_up_in = sem("gate_up_in")
        small_gla_in = sem("small_gla_in")
        gla_in = sem("gla_in")
        z_mm = sem("z_mm")
        z_min = sem("z_min")
        z_abs = sem("z_abs")
        z_exp = sem("z_exp")
        z_ln = sem("z_ln")
        z_done = sem("z_done")
        b_mm = sem("b_mm")
        b_done = sem("b_done")
        b_mid_done = sem("b_mid_done")
        gpads = sem("gpads")
        filled5 = sem("filled5")
        mu_wide = sem("mu_wide")
        y_centred = sem("y_centred")
        y_sq = sem("y_sq")
        y_sqsum = sem("y_sqsum")
        var_done = sem("var_done")
        y_ln = sem("y_ln")
        y_rs = sem("y_rs")
        y_scaled = sem("y_scaled")
        y_affine = sem("y_affine")
        y_bonus = sem("y_bonus")
        gate_mm = sem("gate_mm")
        y_r_done = sem("y_r_done")

        def cols(ap, c):
            return ap[:, c * HALF:(c + 1) * HALF]

        with nc.Block() as block:
            @block.sync
            def _(sp):
                sp.wait_ge(filled5, 3)
                sp.dma_start(xa[0:GATE_RANK, :], xa_dram).then_inc(small_gla_in, 16)
                sp.dma_start(alpha_up[0:GATE_RANK, :], I["gla_alpha_up"][0]).then_inc(small_gla_in, 16)
                sp.dma_start(alpha_up[32:33, :], I["gla_alpha_b"]).then_inc(small_gla_in, 16)
                sp.dma_start(gate_up, I["rwkv_gate_up"][0]).then_inc(gate_up_in, 16)
                sp.dma_start(qk[:, :, 0:T], gla_dram[0:8].rearrange("n p t -> p n t")).then_inc(gla_in, 16)
                sp.dma_start(v_t[:, :, 0:T], gla_dram[8:16].rearrange("n p t -> p n t")).then_inc(gla_in, 16)
                sp.wait_ge(gla_in, 32)

            @block.tensor
            def _(pe):
                pe.wait_ge(small_gla_in, 48)
                for j, n in TILES:
                    if j >= 2:
                        pe.wait_ge(z_abs, j - 1)
                        pe.wait_ge(z_min, j - 1)
                    nc.tensor.matmul(bank(6 + j % 2)[0:n, :], xa[:, j * P:j * P + n], alpha_up, start=True, stop=True
                                     ).then_inc(z_mm, 1)
                pe.wait_ge(z_abs, 5)
                pe.wait_ge(z_min, 5)
                for k in range(KD + 1):
                    if k < KD:
                        if k >= 2:
                            pe.wait_ge(y_centred, k - 1)
                        for c in range(2):
                            m = nc.tensor.matmul(psum[k % 2][:, c, 0:HALF], blk, cols(y_r[:, k], c), start=True,
                                                 stop=True)
                        m.then_inc(mu_wide, 1)
                    if k:
                        pe.wait_ge(y_sq, k)
                        if k >= 3:
                            pe.wait_ge(var_done, k - 2)
                        for c in range(2):
                            m = nc.tensor.matmul(psum[2 + (k - 1) % 2][:, c, 0:HALF], blk, cols(sq[:, k - 1], c),
                                                 start=True, stop=True)
                        m.then_inc(y_sqsum, 1)
                pe.wait_ge(gate_up_in, 16)
                pe.wait_ge(y_centred, KD)
                for k in range(KD):
                    if k >= 2:
                        pe.wait_ge(y_r_done, k - 1)
                    for c in range(2):
                        m = nc.tensor.matmul(psum[k % 2][:, c, 0:HALF], gate_up[:, k * P:(k + 1) * P],
                                             cols(p_rw[:, 25], c), start=True, stop=True)
                    m.then_inc(gate_mm, 1)
                pe.wait_ge(z_done, 5)
                pe.wait_ge(var_done, KD)
                for h in range(NG):
                    if h >= 2:
                        pe.wait_ge(b_done, h - 1)
                    for j in range(4):
                        m = nc.tensor.matmul(bank(4 + h % 2)[:, j * P:(j + 1) * P], z[:, j, h * P:(h + 1) * P], tri_g,
                                             start=True, stop=True)
                    m.then_inc(b_mm, 1)
                for h in range(NG):
                    m = nc.tensor.matmul(bank(6)[:, h * CH:(h + 1) * CH], z[0:DEC, 4, h * P:(h + 1) * P],
                                         tri_g[0:DEC, 0:CH], start=True, stop=True)
                m.then_inc(b_mm, 1)

            @block.vector
            def _(v):
                for j, n in TILES:
                    v.wait_ge(z_mm, j + 1)
                    nc.vector.tensor_scalar(z[0:n, j, :], bank(6 + j % 2)[0:n, :], 0.0, None, ALU.min).then_inc(z_min, 1)
                for k in range(KD + 1):
                    if k < KD:
                        v.wait_ge(mu_wide, k + 1)
                        nc.vector.scalar_tensor_tensor(out=halves(y_r[:, k, 0:T]), in0=psum[k % 2][:, :, 0:HALF],
                                                       scalar=-1.0 / 64, in1=halves(y_r[:, k, 0:T]), op0=ALU.mult,
                                                       op1=ALU.add).then_inc(y_centred, 1)
                    if k:
                        v.wait_ge(y_sqsum, k)
                        nc.vector.tensor_scalar(halves(sq[:, k - 1, :]), psum[2 + (k - 1) % 2][:, :, 0:HALF], 1.0 / 64,
                                                LN_X_EPS, ALU.mult, ALU.add).then_inc(var_done, 1)
                for k in range(KD):
                    v.wait_ge(y_rs, k + 1)
                    nc.vector.tensor_tensor(y_r[:, k, 0:T], y_r[:, k, 0:T], sq[:, k, :], ALU.mult
                                            ).then_inc(y_scaled, 1)
                v.wait_ge(z_min, 5)
                for j, n in TILES:
                    v.wait_ge(z_ln, j + 1)
                    nc.vector.tensor_tensor(z[0:n, j, :], z[0:n, j, :], ez[0:n, j, :], ALU.subtract
                                            ).then_inc(z_done, 1)
                for k in range(KD):
                    v.wait_ge(y_bonus, k + 1)
                    v.wait_ge(gate_mm, k + 1)
                    nc.vector.tensor_tensor(halves(y_r[:, k, 0:T]), halves(y_r[:, k, 0:T]), psum[k % 2][:, :, 0:HALF],
                                            ALU.mult).then_inc(y_r_done, 1)
                v.wait_ge(y_r_done, KD)
                for h in range(NG):
                    v.wait_ge(b_mm, h + 1)
                    nc.vector.tensor_copy(b_t[:, h, 0:SEQ], bank(4 + h % 2)).then_inc(b_done, 1)
                v.wait_ge(b_mm, NG + 1)
                nc.vector.tensor_copy(b_t[:, :, SEQ:TP], bank(6)[:, 0:256].rearrange("p (h t) -> p h t", t=CH)
                                      ).then_inc(b_done, 1)
                v.wait_ge(b_done, NG + 1)
                v.wait_ge(gpads, 3)
                bc = b_t.rearrange("p h (c t) -> p (h c) t", t=CH)
                nc.vector.tensor_tensor(b_mid.rearrange("p h (c t) -> p (h c) t", t=CH), bc,
                                        bc[:, :, 31:32].broadcast_to([P, NG * 10, CH]), ALU.subtract
                                        ).then_inc(b_mid_done, 1)
                v.wait_ge(b_mid_done, 1)

            @block.scalar
            def _(act):
                for j, n in TILES:
                    act.wait_ge(z_mm, j + 1)
                    act.wait_ge(z_min, j + 1)
                    nc.scalar.activation(ez[0:n, j, :], bank(6 + j % 2)[0:n, :], ACT.Abs).then_inc(z_abs, 1)
                for j, n in TILES:
                    act.wait_ge(z_abs, j + 1)
                    nc.scalar.activation(ez[0:n, j, :], ez[0:n, j, :], ACT.Exp, scale=-1.0).then_inc(z_exp, 1)
                for j, n in TILES:
                    act.wait_ge(z_exp, j + 1)
                    nc.scalar.activation(ez[0:n, j, :], ez[0:n, j, :], ACT.Ln, bias=1.0).then_inc(z_ln, 1)
                for k in range(KD):
                    act.wait_ge(y_centred, k + 1)
                    nc.scalar.activation(sq[:, k, :], y_r[:, k, 0:T], ACT.Square).then_inc(y_sq, 1)
                for k in range(KD):
                    act.wait_ge(var_done, k + 1)
                    nc.scalar.activation(sq[:, k, :], sq[:, k, :], ACT.Ln).then_inc(y_ln, 1)
                for k in range(KD):
                    act.wait_ge(y_ln, k + 1)
                    nc.scalar.activation(sq[:, k, :], sq[:, k, :], ACT.Exp, scale=-0.5).then_inc(y_rs, 1)
                for k in range(KD):
                    act.wait_ge(y_scaled, k + 1)
                    nc.scalar.activation(y_r[:, k, 0:T], y_r[:, k, 0:T], ACT.Identity, scale=vcol("lng", k),
                                         bias=vcol("lnb", k)).then_inc(y_affine, 1)

            @block.gpsimd
            def _(pool):
                pool.memset(xa, 0.0).then_inc(filled5, 1)
                pool.memset(alpha_up, 0.0).then_inc(filled5, 1)
                pool.wait_ge(filled5, 2)
                pool.memset(xa[32:33, :], 1.0).then_inc(filled5, 1)
                pool.wait_ge(filled5, 3)
                pool.memset(qk[:, :, T:TQ], 0.0).then_inc(gpads, 1)
                pool.memset(v_t[:, :, T:TQ], 0.0).then_inc(gpads, 1)
                pool.memset(b_t[:, :, TP:TQ], 0.0).then_inc(gpads, 1)
                for k in range(KD):
                    pool.wait_ge(y_affine, k + 1)
                    pool.tensor_tensor(y_r[:, k, 0:T], y_r[:, k, 0:T], p_rw[:, 16 + k, 0:T], ALU.add
                                       ).then_inc(y_bonus, 1)

        clear_semaphores()
        r_in = Region(S5.at).take(8, T)
        assert S5.at + 8 * T <= gla_kept
        S6 = Region(base + 8 * TP)
        y_g_at = S6.at
        y_g = S6.take(8, T)
        e_q = [S6.take(NG, P) for _ in range(2)]
        e_k = S6.take(NG, P)
        e_b = [S6.take(NG, P) for _ in range(2)]
        q_in = S6.take(NG, P)
        k_in = S6.take(NG, P)
        q_st = [S6.take(NG, P) for _ in range(2)]
        v_in = S6.take(8, P)
        k_tok = S6.take(NG, P)
        v_tok = S6.take(NG, DV)
        att = S6.take(NG, P)
        o_n = S6.take(NG, DV)
        o_sq = S6.take(NG, DV)
        kv_tmp = S6.take(NG, DV)
        o_ms = S6.take(NG)
        o_rs = S6.take(NG)
        st_g = [S6.take(NG, DV) for _ in range(2)]
        assert S6.at <= S5.at
        st_g_in = sem("st_g_in")
        st_g_zero = sem("st_g_zero")
        r_loaded = sem("r_loaded")
        g_exp = sem("g_exp")
        g_prep = sem("g_prep")
        g_turned = sem("g_turned")
        g_copied = sem("g_copied")
        g_att = sem("g_att")
        g_kv = sem("g_kv")
        kv_scaled = sem("kv_scaled")
        g_state = sem("g_state")
        g_o = sem("g_o")
        o_ssq = sem("o_ssq")
        o_mean = sem("o_mean")
        o_rstd = sem("o_rstd")
        o_done = sem("o_done")
        g_out = sem("g_out")
        y_g_out = sem("y_g_out")
        gla_st_out = sem("gla_st_out")
        GQ = 128.0 ** -0.5

        with nc.Block() as block:
            @block.sync
            def _(sp):
                sp.dma_start(r_in, gate_dram[0:8].rearrange("n p t -> p n t")).then_inc(r_loaded, 16)
                sp.dma_start(st_g[1], I["state_gla"][0, 0].rearrange("h k v -> k h v")).then_inc(st_g_in, 16)
                for s, out in ((0, O[4]), (1, O[7])):
                    sp.wait_ge(g_state, 4 + 4 * (8 + s))
                    sp.dma_start(out[0, 0].rearrange("h k v -> k h v"), st_g[s]).then_inc(gla_st_out, 16)
                sp.wait_ge(gla_st_out, 32)

            @block.gpsimd
            def _(pool):
                pool.memset(st_g[0], 0.0).then_inc(st_g_zero, 1)

            @block.tensor
            def _(pe):
                def front(i):
                    pe.wait_ge(g_prep, 4 * i + 4)
                    for n in range(8):
                        m = nc.tensor.transpose(psum[1][:, n // 4, (n % 4) * P:(n % 4 + 1) * P], v_in[:, n, :], ident)
                    m.then_inc(g_turned, 1)
                    for h in range(NG):
                        m = nc.tensor.transpose(psum[0][:, 1, h * P:(h + 1) * P], k_in[:, h, :], ident)
                    m.then_inc(g_turned, 1)
                    for h in range(NG):
                        m = nc.tensor.matmul(psum[0][:, 0, h * P:(h + 1) * P], k_in[:, h, :], q_in[:, h, :],
                                             start=True, stop=True)
                    m.then_inc(g_turned, 1)

                def two_heads(bank2, h):
                    return bank2[:, h // 2, (h % 2) * DV:(h % 2 + 1) * DV]

                def with_state(r, st, s):
                    for h in range(NG):
                        m = nc.tensor.matmul(two_heads(psum[2][r], h), q_st[s][:, h, r], st[:, h, :], start=False,
                                             stop=True, skip_group_check=True)
                    return m

                def tile(i, s, w, st, chunks_in, more):
                    pe.wait_ge(g_att, i + 1)
                    pe.wait_ge(g_copied, 2 * i + 2)
                    pe.wait_ge(o_done, 4 * i + 4)
                    for h in range(NG):
                        nc.tensor.matmul(two_heads(psum[2][0:w], h), att[0:w, h, 0:w], v_tok[0:w, h, :],
                                         start=h % 2 == 0, stop=False, skip_group_check=True)
                    pe.wait_ge(g_state, 8 * i + 4)
                    m = with_state(slice(0, 64), st, s)
                    if chunks_in == 1:
                        m.then_inc(g_o, 1)
                    for c in range(chunks_in):
                        r = slice(64 * c, 64 * c + 64)
                        pe.wait_ge(kv_scaled, 8 * i + (4 * c + 4))
                        for h in range(NG):
                            m = nc.tensor.matmul(two_heads(psum[3], h), k_tok[r, h, :], v_tok[r, h, :], start=True,
                                                 stop=True)
                        m.then_inc(g_kv, 1)
                    if chunks_in == 2:
                        pe.wait_ge(g_state, 8 * i + 8)
                        with_state(slice(64, 128), st, s).then_inc(g_o, 1)
                    if more:
                        pe.wait_ge(y_g_out, 8 * i + 8)
                        front(i + 1)
                        pe.wait_ge(g_copied, 2 * i + 3)
                    pe.wait_ge(o_done, 4 * i + 8)
                    for n in range(8):
                        m = nc.tensor.transpose(psum[1][:, n // 4, (n % 4) * P:(n % 4) * P + w],
                                                o_n[0:w, n // 2, (n % 2) * P:(n % 2 + 1) * P], ident[0:w, 0:w])
                    m.then_inc(g_out, 1)
                pe.sem_inc(kv_scaled, 4)
                pe.sem_inc(o_done, 4)
                pe.sem_inc(y_g_out, 8)
                front(0)
                with pe.Fori(0, 2) as i:
                    for s in range(2):
                        tile(2 * i + s, s, P, st_g[0], 2, True)
                pe.wait_ge(st_g_in, 16)
                tile(4, 0, CH, st_g[1], 1, False)

            @block.scalar
            def _(act):
                def prepare(i, s):
                    nc.scalar.activation(e_q[s], b_mid[:, :, ds(i * P, P)], ACT.Exp).then_inc(g_exp, 1)
                    nc.scalar.activation(e_k, b_mid[:, :, ds(i * P, P)], ACT.Exp, scale=-1.0).then_inc(g_exp, 1)
                    nc.scalar.activation(e_b[s], b_t[:, :, ds(i * P, P)], ACT.Exp).then_inc(g_exp, 1)
                    nc.scalar.activation(v_in, v_t[:, :, ds(i * P, P)], ACT.Copy).then_inc(g_prep, 1)

                def front(i):
                    act.wait_ge(g_turned, 3 * i + 1)
                    nc.scalar.activation(v_tok.rearrange("t h v -> t (h v)"), psum[1].rearrange("t b v -> t (b v)"),
                                         ACT.Copy).then_inc(g_copied, 1)
                    act.wait_ge(g_turned, 3 * i + 2)
                    nc.scalar.activation(k_tok.rearrange("t h v -> t (h v)"), psum[0][:, 1, :], ACT.Copy
                                         ).then_inc(g_copied, 1)

                def tile(i, s, w, more):
                    if more:
                        act.wait_ge(g_state, 8 * i + 4)
                        prepare(i + 1, 1 - s)
                    act.wait_ge(g_o, i + 1)
                    for h in range(NG):
                        nc.scalar.activation(o_sq[0:w, h, :], psum[2][0:w, h // 2, (h % 2) * DV:(h % 2 + 1) * DV],
                                             ACT.Square, accum_out=o_ms[0:w, h:h + 1]).then_inc(o_ssq, 1)
                    if more:
                        front(i + 1)
                    act.wait_ge(o_mean, i + 1)
                    nc.scalar.activation(o_rs[0:w], o_rs[0:w], ACT.Ln).then_inc(o_rstd, 1)
                    act.wait_ge(o_rstd, 2 * i + 1)
                    nc.scalar.activation(o_rs[0:w], o_rs[0:w], ACT.Exp, scale=-0.5).then_inc(o_rstd, 1)
                    act.wait_ge(o_rstd, 2 * i + 2)
                    act.wait_ge(g_out, i + 1)
                    for h in range(NG):
                        nc.scalar.activation(o_n[0:w, h, :], psum[2][0:w, h // 2, (h % 2) * DV:(h % 2 + 1) * DV],
                                             ACT.Copy, scale=o_rs[0:w, h:h + 1]).then_inc(o_done, 1)
                act.sem_inc(g_out, 1)
                prepare(0, 0)
                front(0)
                with act.Fori(0, 2) as i:
                    for s in range(2):
                        tile(2 * i + s, s, P, True)
                tile(4, 0, CH, False)
                act.wait_ge(r_loaded, 16)
                nc.scalar.activation(r_in, r_in, ACT.Silu)

            @block.vector
            def _(v):
                v.wait_ge(st_g_zero, 1)
                v.sem_inc(g_state, 4)

                def prepare(i, s):
                    t0 = i * P
                    v.wait_ge(g_exp, 3 * i + 3)
                    nc.vector.scalar_tensor_tensor(out=q_in, in0=qk[:, 0:4, ds(t0, P)], scalar=GQ, in1=e_q[s],
                                                   op0=ALU.mult, op1=ALU.mult).then_inc(g_prep, 1)
                    nc.vector.tensor_tensor(k_in, qk[:, 4:8, ds(t0, P)], e_k, ALU.mult).then_inc(g_prep, 1)
                    nc.vector.scalar_tensor_tensor(out=q_st[s], in0=qk[:, 0:4, ds(t0, P)], scalar=GQ, in1=e_b[s],
                                                   op0=ALU.mult, op1=ALU.mult).then_inc(g_prep, 1)

                def front(i):
                    v.wait_ge(g_turned, 3 * i + 3)
                    nc.vector.tensor_tensor(att, psum[0][:, 0, :].rearrange("s (h t) -> s h t", h=NG),
                                            tri_bd.unsqueeze(1).broadcast_to([P, NG, P]), ALU.mult
                                            ).then_inc(g_att, 1)

                def tile(i, s, w, st, chunks_in, more):
                    t0 = i * P
                    for c in range(chunks_in):
                        e = 64 * c + 63
                        v.wait_ge(g_kv, 2 * i + (c + 1))
                        v.wait_ge(g_state, 8 * i + (4 * c + 4))
                        for h in range(NG):
                            nc.vector.tensor_scalar(kv_tmp[:, h, :], psum[3][:, h // 2, (h % 2) * DV:(h % 2 + 1) * DV],
                                                    e_q[s][:, h, e:e + 1], None, ALU.mult).then_inc(kv_scaled, 1)
                        v.wait_ge(kv_scaled, 8 * i + (4 * c + 8))
                        if c:
                            v.wait_ge(g_o, i + 1)
                        for h in range(NG):
                            nc.vector.scalar_tensor_tensor(out=st[:, h, :], in0=st[:, h, :],
                                                           scalar=e_b[s][:, h, e:e + 1], in1=kv_tmp[:, h, :],
                                                           op0=ALU.mult, op1=ALU.add).then_inc(g_state, 1)
                        if c == 0 and more:
                            prepare(i + 1, 1 - s)
                    v.wait_ge(o_ssq, 4 * i + 4)
                    nc.vector.tensor_scalar(o_rs[0:w], o_ms[0:w], 1.0 / DV, EPS, ALU.mult, ALU.add
                                            ).then_inc(o_mean, 1)
                    if more:
                        front(i + 1)
                    v.wait_ge(g_out, i + 2)
                    wt = min(w, T - SEQ) if w < P else w
                    for n in range(8):
                        nc.vector.tensor_scalar(y_g[:, n, ds(t0, wt)], psum[1][:, n // 4, (n % 4) * P:(n % 4) * P + wt],
                                                vcol("glan", n % 2), None, ALU.mult).then_inc(y_g_out, 1)
                prepare(0, 0)
                front(0)
                with v.Fori(0, 2) as i:
                    for s in range(2):
                        tile(2 * i + s, s, P, st_g[0], 2, True)
                v.wait_ge(st_g_in, 16)
                tile(4, 0, CH, st_g[1], 1, False)

        S7 = Region(y_g_at + 8 * T)
        gates = S7.take(16, T)
        merged = S7.take(8, T)
        S7g = Region(y_g_at + 8 * T, y_g_at + 24 * T)
        merge_tmp = S7g.take(2, D)
        mods2 = [S7g.take(2, D) for _ in range(2)]
        norm2_b = S7g.take(D)
        h2 = Region(base).take(5, D)
        sq2 = Region(base + 5 * D, y_g_at + 8 * T).take(D)
        sums2 = rstd[:, 0:5]
        gt1_b = S7.take(2, D)
        w_out_sb = S7.take(KD, D)
        wb = [[S7.take(KD, 2 * P) for _ in range(2)] for _ in range(2)]
        x2_at = ARENA - 5 * D
        assert S7.at <= x2_at
        x2 = Region(x2_at).take(5, D)
        gates_loaded = sem("gates_loaded")
        wb_in = [sem(f"wb_in{s}") for s in range(2)]
        w_out_in = sem("w_out_in")
        x2_in = sem("x2_in")
        y_g_done = sem("y_g_done")
        gates_done = sem("gates_done")
        br_done = sem("br_done")
        br_out = sem("br_out")
        merged_done = sem("merged_done")
        wo_mm = sem("wo_mm")
        wo_scaled = sem("wo_scaled")
        x2_done = sem("x2_done")
        n2_in = sem("n2_in")
        x2_sq = sem("x2_sq")
        x2_ms = sem("x2_ms")
        x2_std = sem("x2_std")
        x2_rs = sem("x2_rs")
        m2_done = sem("m2_done")
        h2_half = sem("h2_half")
        h2_done = sem("h2_done")
        wbr_v = [I[n][0].rearrange("(k p) n -> p k n", p=P) for n in ("w_branch_rwkv", "w_branch_gla")]

        with nc.Block() as block:
            @block.sync
            def _(sp):
                def load(p, s):
                    sp.wait_ge(br_done, 4 * p + 4)
                    for b in range(2):
                        sp.dma_start(wb[s][b], wbr_v[b][:, :, p * 2 * P:(p + 1) * 2 * P]).then_inc(wb_in[s], 16)
                load(0, 0)
                sp.dma_start(gates, gate_dram[8:24].rearrange("n p t -> p n t")).then_inc(gates_loaded, 16)
                load(1, 1)
                sp.wait_ge(y_g_done, 8)
                sp.dma_start(w_out_sb, I["w_out"][0].rearrange("(k p) n -> p k n", p=P)).then_inc(w_out_in, 16)
                sp.dma_start(x2[:, 0:4, :], I["x_prompt"][0].rearrange("(j p) d -> p j d", p=P)).then_inc(x2_in, 16)
                sp.dma_start(x2[0:DEC, 4, :], I["x_sample"][0]).then_inc(x2_in, 16)
                for s in range(2):
                    sp.dma_start(gt1_b[:, s, :], mod_dram[s, 2 * D:3 * D].partition_broadcast(P)).then_inc(x2_in, 16)
                load(2, 0)
                load(3, 1)
                sp.wait_ge(merged_done, 8)
                for s in range(2):
                    sp.dma_start(mods2[0][:, s, :], mod_dram[s, 4 * D:5 * D].partition_broadcast(P)).then_inc(n2_in, 16)
                    sp.dma_start(mods2[1][:, s, :], mod_dram[s, 3 * D:4 * D].partition_broadcast(P)).then_inc(n2_in, 16)
                sp.dma_start(norm2_b, I["norm2_g"][0].partition_broadcast(P)).then_inc(n2_in, 16)

            @block.scalar
            def _(act):
                act.sem_inc(br_done, 8)
                act.wait_ge(gates_loaded, 16)
                for k in range(8):
                    for b in range(2):
                        g = gates[:, 8 * b + k, :]
                        nc.scalar.activation(g, g, ACT.Sigmoid).then_inc(gates_done, 1)
                for j, n in TILES:
                    act.wait_ge(x2_done, j + 1)
                    nc.scalar.activation(sq2[0:n], x2[0:n, j, :], ACT.Square, accum_out=sums2[0:n, j:j + 1]
                                         ).then_inc(x2_sq, 1)
                    act.wait_ge(x2_ms, j + 1)
                    nc.scalar.activation(sums2[0:n, j:j + 1], sums2[0:n, j:j + 1], ACT.Sqrt).then_inc(x2_std, 1)

            @block.vector
            def _(v):
                v.sem_inc(br_out, 4)
                for k in range(8):
                    nc.vector.tensor_tensor(y_g[:, k, :], y_g[:, k, :], r_in[:, k, :], ALU.mult).then_inc(y_g_done, 1)
                v.wait_ge(gates_done, 16)

                def pair(p):
                    for f in range(2):
                        for b in range(2):
                            u = 2 * f + b
                            v.wait_ge(br_done, 4 * p + (u + 9))
                            g = gates[:, ds(p * 2 + (8 * b + f), 1), :].rearrange("p a (c t) -> p (a c) t", c=2)
                            nc.vector.tensor_tensor(g, g, psum[u][:, :, 0:HALF], ALU.mult).then_inc(br_out, 1)
                        v.wait_ge(br_out, 4 * p + (2 * f + 6))
                        nc.vector.tensor_tensor(merged[:, ds(p * 2 + f, 1), :], gates[:, ds(p * 2 + f, 1), :],
                                                gates[:, ds(p * 2 + (8 + f), 1), :], ALU.add).then_inc(merged_done, 1)
                with v.Fori(0, 4) as p:
                    pair(p)
                def second_norm(j, n):
                    stream = 1 if j == 4 else 0
                    rs = sums2[0:n, j:j + 1]
                    v.wait_ge(x2_sq, j + 1)
                    nc.vector.tensor_scalar(rs, rs, 1.0 / D, EPS, ALU.mult, ALU.add).then_inc(x2_ms, 1)
                    v.wait_ge(x2_std, j + 1)
                    nc.vector.reciprocal(rs, rs).then_inc(x2_rs, 1)
                    v.wait_ge(x2_rs, j + 1)
                    nc.vector.scalar_tensor_tensor(out=h2[0:n, j, :], in0=x2[0:n, j, :], scalar=rs,
                                                   in1=mods2[0][0:n, stream, :], op0=ALU.mult, op1=ALU.mult
                                                   ).then_inc(h2_half, 1)
                    v.wait_ge(h2_half, j + 1)
                    nc.vector.tensor_tensor(h2[0:n, j, :], h2[0:n, j, :], mods2[1][0:n, stream, :], ALU.add
                                            ).then_inc(h2_done, 1)

                v.wait_ge(n2_in, 16 * 5)
                for s in range(2):
                    nc.vector.scalar_tensor_tensor(out=mods2[0][:, s, :], in0=mods2[0][:, s, :], scalar=1.0,
                                                   in1=norm2_b, op0=ALU.add, op1=ALU.mult).then_inc(m2_done, 1)
                v.wait_ge(m2_done, 2)
                v.wait_ge(x2_in, 64)
                for j, n in TILES:
                    v.wait_ge(wo_mm, j + 1)
                    s = 1 if j == 4 else 0
                    o = psum[j % 2][0:n].rearrange("t b c -> t (b c)")
                    nc.vector.tensor_tensor(merge_tmp[0:n, j % 2, :], o, gt1_b[0:n, s, :], ALU.mult
                                            ).then_inc(wo_scaled, 1)
                    v.wait_ge(wo_scaled, j + 1)
                    nc.vector.tensor_tensor(x2[0:n, j, :], x2[0:n, j, :], merge_tmp[0:n, j % 2, :], ALU.add
                                            ).then_inc(x2_done, 1)
                    if j:
                        second_norm(j - 1, P)
                second_norm(4, DEC)
                v.wait_ge(h2_done, 5)

            @block.tensor
            def _(pe):
                def pair(p, s, use):
                    pe.wait_ge(wb_in[s], 32 * use + 32)
                    for f in range(2):
                        for b in range(2):
                            u = 2 * f + b
                            y = (y_r, y_g)[b]
                            pe.wait_ge(br_out, 4 * p + (u + 1))
                            if b:
                                pe.wait_ge(y_g_done, 8)
                            for k in range(KD):
                                for c in range(2):
                                    m = nc.tensor.matmul(psum[u][:, c, 0:HALF], wb[s][b][:, k, f * P:(f + 1) * P],
                                                         cols(y[:, k], c), start=k == 0, stop=k == KD - 1)
                            m.then_inc(br_done, 1)
                with pe.Fori(0, 2) as i:
                    for s in range(2):
                        pair(2 * i + s, s, i)
                pe.wait_ge(merged_done, 8)
                pe.wait_ge(w_out_in, 16)
                for j, n in TILES:
                    if j >= 2:
                        pe.wait_ge(wo_scaled, j - 1)
                    for k in range(KD):
                        for b in range(2):
                            m = nc.tensor.matmul(psum[j % 2][0:n, b, :], merged[:, k, j * P:j * P + n],
                                                 w_out_sb[:, k, b * 512:(b + 1) * 512], start=k == 0,
                                                 stop=k == KD - 1)
                    m.then_inc(wo_mm, 1)

        clear_semaphores()
        NE, NGR, EPG, FF = 32, 4, 8, 512
        BLK = 64
        NSLOT = NE * BLK
        S8 = Region(base, x2_at)
        S8.take(5, D)
        route = Region(S8.at, x2_at)
        slot_i = [route.take(5) for _ in range(2)]
        slot_g = [route.take(5) for _ in range(2)]
        wgt = [route.take(5) for _ in range(2)]
        wgt_r = [route.take(5) for _ in range(2)]
        pos = [route.take(5) for _ in range(2)]
        eid = [route.take(5) for _ in range(2)]
        trash = [route.take(5) for _ in range(2)]
        in_r = [route.take(5) for _ in range(2)]
        tmp_i = route.take(5)
        n_rounds = route.take(2)
        moe_at = route.at
        h2_t = route.take(KD, T)
        router = route.take(KD, 36)
        lg_t = route.take(T)
        lg = route.take(5, 36)
        g8 = route.take(5, 8)
        top_g = route.take(5, 8)
        top_e = route.take(5, 8)
        idx_g = route.take(5, 8)
        idx_e = route.take(5, 8)
        gid = route.take(5)
        eidx = [route.take(5) for _ in range(2)]
        pexp = route.take(5, 4)
        psum_g = route.take(5)
        iota_e = route.take(NE)
        valid = route.take(5)
        goh = route.take(5, 4)
        prod = route.take(5, NGR, EPG)
        within = route.take(5, 8)
        oh = [route.take(5, NE) for _ in range(2)]
        both = route.take(5, NE)
        before = route.take(5, NE)
        ohp = route.take(5, NE)
        up_full = route.take(128)
        cnt = route.take(NE)
        cmax = route.take(1)
        experts_at = x2_at - 2 * (2 * KD * FF + 4 * D)
        assert route.at <= experts_at
        EW = Region(experts_at, x2_at)
        w_gu = [EW.take(2, KD, FF) for _ in range(2)]
        w_dn = [EW.take(4, D) for _ in range(2)]
        wg_in = [sem(f"wg_in{s}") for s in range(2)]
        wd_in = [sem(f"wd_in{s}") for s in range(2)]
        egate = I["expert_w_gate"][0].rearrange("e (k p) f -> e p k f", p=P)
        eup = I["expert_w_up"][0].rearrange("e (k p) f -> e p k f", p=P)
        edown = I["expert_w_down"][0].rearrange("e (k p) f -> e p k f", p=P)

        def load_gate_up(sp, e, s):
            for w, b in ((egate, 0), (eup, 1)):
                sp.dma_start(w_gu[s][:, b], w[ds(e, 1)].rearrange("e p k f -> (e p) k f")).then_inc(wg_in[s], 16)

        def load_down(sp, e, s):
            sp.dma_start(w_dn[s], edown[ds(e, 1)].rearrange("e p k f -> (e p) k f")).then_inc(wd_in[s], 16)

        router_in = sem("router_in")
        rt_const = sem("rt_const")
        h2_tr = sem("h2_tr")
        h2_t_out = sem("h2_t_out")
        lg_t_mm = sem("lg_t_mm")
        lg_t_done = sem("lg_t_done")
        lg_mm = sem("lg_mm")
        lg_done = sem("lg_done")
        rt = sem("rt")
        rt_shift = sem("rt_shift")
        rt_exp = sem("rt_exp")
        rt_gap = sem("rt_gap")
        both_done = sem("both_done")
        pos_mm = sem("pos_mm")
        routed = sem("routed")

        def as_u32(ap):
            return ap.bitcast(U32)

        with nc.Block() as block:
            @block.sync
            def _(sp):
                sp.dma_start(router[:, :, 0:4], I["router_group"][0].rearrange("(k p) n -> p k n", p=P)
                             ).then_inc(router_in, 16)
                sp.dma_start(router[:, :, 4:36], I["router_expert"][0].rearrange("(k p) n -> p k n", p=P)
                             ).then_inc(router_in, 16)
                for e in range(2):
                    load_gate_up(sp, e, e)
                    load_down(sp, e, e)

            @block.gpsimd
            def _(pool):
                steps = [0]

                def step(ins):
                    ins.then_inc(rt_const, 1)
                    steps[0] += 1
                    pool.wait_ge(rt_const, steps[0])
                iota_i = ohp[:, 0, :].bitcast(I32)
                step(pool.iota(iota_i, pattern=[[1, NE]], base=0, channel_multiplier=0))
                step(pool.tensor_copy(iota_e, iota_i))
                for k in range(2):
                    step(pool.iota(tmp_i.bitcast(I32), pattern=[[2 * P, 5]], base=NSLOT + k, channel_multiplier=2))
                    step(pool.tensor_copy(trash[k], tmp_i.bitcast(I32)))
                step(pool.memset(valid, 1.0))
                step(pool.memset(valid[:, 4:5], 0.0))
                step(pool.memset(valid[0:DEC, 4:5], 1.0))
                step(pool.memset(lg, 0.0))
                step(pool.memset(g8, -3.0e38))
                step(pool.affine_select(out=up_full, in_=ones, compare_op=ALU.is_gt, fill=0.0, base=0,
                                        pattern=[[1, 128]], channel_multiplier=-1))

            @block.scalar
            def _(act):
                act.wait_ge(rt_shift, 1)
                nc.scalar.activation(pexp, pexp, ACT.Exp).then_inc(rt_exp, 1)
                act.wait_ge(rt_gap, 1)
                nc.scalar.activation(wgt[1], wgt[1], ACT.Exp).then_inc(rt_exp, 1)

            @block.tensor
            def _(pe):
                u = 0
                for j, n in TILES:
                    for b in range(2):
                        if u >= 2:
                            pe.wait_ge(h2_t_out, u - 1)
                        for q in range(4):
                            k = 4 * b + q
                            m = nc.tensor.transpose(bank(u % 2)[:, q * P:q * P + n], h2[0:n, j, k * P:(k + 1) * P],
                                                    ident[0:n, 0:n])
                        m.then_inc(h2_tr, 1)
                        u += 1
                pe.wait_ge(h2_t_out, 10)
                pe.wait_ge(router_in, 32)
                for k in range(KD):
                    for c in range(2):
                        m = nc.tensor.matmul(psum[2][0:36, c, 0:HALF], router[:, k, :], cols(h2_t[:, k], c),
                                             start=k == 0, stop=k == KD - 1)
                m.then_inc(lg_t_mm, 1)
                pe.wait_ge(lg_t_done, 1)
                for j, n in TILES:
                    m = nc.tensor.transpose(bank(2)[0:n, j * 36:(j + 1) * 36], lg_t[0:36, j * P:j * P + n],
                                            ident[0:36, 0:36])
                m.then_inc(lg_mm, 1)
                pe.wait_ge(both_done, 1)
                pe.wait_ge(rt_const, 12)
                nc.tensor.matmul(bank(3)[:, 0:160], up_full, both.rearrange("p j e -> p (j e)"), start=True, stop=True)
                nc.tensor.matmul(bank(3)[:, 256:416], ones, both.rearrange("p j e -> p (j e)"), start=True, stop=True
                                 ).then_inc(pos_mm, 1)

            @block.vector
            def _(v):
                u = 0
                for j, n in TILES:
                    for b in range(2):
                        v.wait_ge(h2_tr, u + 1)
                        nc.vector.tensor_copy(h2_t[:, 4 * b:4 * b + 4, j * P:j * P + n],
                                              bank(u % 2).rearrange("p (q t) -> p q t", q=4)[:, :, 0:n]
                                              ).then_inc(h2_t_out, 1)
                        u += 1
                v.wait_ge(lg_t_mm, 1)
                nc.vector.tensor_copy(halves(lg_t[0:36, :]), psum[2][0:36, :, 0:HALF]).then_inc(lg_t_done, 1)
                v.wait_ge(rt_const, 12)
                v.wait_ge(lg_mm, 1)
                nc.vector.tensor_copy(lg[:, 0:4, :], bank(2)[:, 0:144].rearrange("p (j n) -> p j n", n=36)
                                      ).then_inc(lg_done, 1)
                nc.vector.tensor_copy(lg[0:DEC, 4, :], bank(2)[0:DEC, 144:180]).then_inc(lg_done, 1)
                v.wait_ge(lg_done, 2)
                done = [0]

                def step(*ins):
                    for i in ins:
                        i.then_inc(rt, 1)
                        done[0] += 1
                    v.wait_ge(rt, done[0])
                ve = nc.vector
                step(ve.tensor_copy(g8[:, :, 0:4], lg[:, :, 0:4]))
                step(*[ve.max(top_g[:, j, :], g8[:, j, :]) for j in range(5)])
                step(*[ve.max_index(as_u32(idx_g[:, j, :]), top_g[:, j, :], g8[:, j, :]) for j in range(5)])
                step(ve.tensor_copy(gid, as_u32(idx_g[:, :, 0])))
                ve.tensor_tensor(pexp, lg[:, :, 0:4], top_g[:, :, 0:1].broadcast_to([P, 5, 4]), ALU.subtract
                                 ).then_inc(rt_shift, 1)
                step(ve.tensor_tensor(goh, iota_e[:, 0:4].unsqueeze(1).broadcast_to([P, 5, 4]),
                                      gid.unsqueeze(2).broadcast_to([P, 5, 4]), ALU.is_equal))
                step(*[ve.tensor_tensor(prod[:, j], lg[:, j, 4:36].rearrange("p (g e) -> p g e", g=NGR),
                                        goh[:, j, :].unsqueeze(2).broadcast_to([P, NGR, EPG]), ALU.mult)
                       for j in range(5)])
                step(ve.tensor_reduce(within, prod.rearrange("p j g e -> p j e g"), AX.X, ALU.add))
                step(*[ve.max(top_e[:, j, :], within[:, j, :]) for j in range(5)])
                step(*[ve.max_index(as_u32(idx_e[:, j, :]), top_e[:, j, :], within[:, j, :]) for j in range(5)])
                step(*[ve.tensor_copy(eidx[k], as_u32(idx_e[:, :, k])) for k in range(2)])
                step(*[ve.scalar_tensor_tensor(out=eid[k], in0=gid, scalar=float(EPG), in1=eidx[k], op0=ALU.mult,
                                               op1=ALU.add) for k in range(2)])
                ve.tensor_tensor(wgt[1], top_e[:, :, 1], top_e[:, :, 0], ALU.subtract).then_inc(rt_gap, 1)
                step(*[ve.tensor_tensor(oh[k], iota_e.unsqueeze(1).broadcast_to([P, 5, NE]),
                                        eid[k].unsqueeze(2).broadcast_to([P, 5, NE]), ALU.is_equal)
                       for k in range(2)])
                step(*[ve.tensor_tensor(oh[k], oh[k], valid.unsqueeze(2).broadcast_to([P, 5, NE]), ALU.mult)
                       for k in range(2)])
                ve.tensor_tensor(both, oh[0], oh[1], ALU.add).then_inc(both_done, 1)
                v.wait_ge(rt_exp, 2)
                step(ve.tensor_reduce(psum_g, pexp, AX.X, ALU.add), ve.tensor_scalar(wgt[0], wgt[1], 1.0, None,
                                                                                   ALU.add))
                step(ve.tensor_tensor(wgt[0], wgt[0], psum_g, ALU.mult))
                step(ve.reciprocal(wgt[0], wgt[0]))
                step(ve.tensor_tensor(wgt[1], wgt[1], wgt[0], ALU.mult))
                v.wait_ge(pos_mm, 1)
                step(ve.tensor_copy(before, bank(3)[:, 0:160].rearrange("p (j e) -> p j e", e=NE)),
                     ve.tensor_copy(cnt, bank(3)[:, 256:256 + NE]))
                for j in range(1, 5):
                    step(ve.tensor_tensor(before[:, j, :], before[:, j, :], cnt, ALU.add))
                    step(ve.tensor_tensor(cnt, cnt, bank(3)[:, 256 + j * NE:256 + (j + 1) * NE], ALU.add))
                for k in range(2):
                    step(ve.tensor_tensor(ohp, oh[k], before, ALU.mult))
                    step(ve.tensor_reduce(pos[k], ohp, AX.X, ALU.add))
                    step(ve.tensor_scalar(tmp_i, valid, -1.0e6, 1.0e6, ALU.mult, ALU.add))
                    step(ve.tensor_tensor(pos[k], pos[k], tmp_i, ALU.add))
                step(ve.tensor_reduce(cmax, cnt, AX.X, ALU.max))
                step(ve.tensor_scalar(cmax, cmax, float(BLK - 1), None, ALU.add))
                step(ve.tensor_copy(n_rounds[:, 0:1].bitcast(I32), cmax))
                step(ve.tensor_scalar(cmax, cmax, -float(BLK), None, ALU.add))
                ve.tensor_copy(n_rounds[:, 1:2].bitcast(I32), cmax).then_inc(routed, 1)
                v.wait_ge(routed, 1)
                ve.tensor_single_scalar(n_rounds.bitcast(I32), n_rounds.bitcast(I32), 6, ALU.arith_shift_right
                                        ).then_inc(routed, 1)
                v.wait_ge(routed, 2)

        low = Region(moe_at, experts_at)
        gt2_b = low.take(2, D)
        G9 = Region(experts_at, x2_at)
        gath = [G9.take(2, D) for _ in TILES]
        x_blk = [low.take(D) for _ in range(2)]
        x_t = [low.take(KD, 2 * BLK) for _ in range(2)]
        gu = low.take(512)
        act_g = low.take(4, BLK)
        hid = low.take(4, BLK)
        y_blk = [low.take(512) for _ in range(2)]
        gt2_in = sem("gt2_in")
        slots_done = sem("slots_done")
        slot_step = sem("slot_step")
        pool_go = sem("pool_go")
        w_done = sem("w_done")
        scattered = sem("scattered")
        x_in9 = [sem(f"x_in9_{s}") for s in range(2)]
        x_tr9 = sem("x_tr9")
        x_t9 = sem("x_t9")
        gu_mm = sem("gu_mm")
        gu_out = sem("gu_out")
        gu_tr = sem("gu_tr")
        silu_done = sem("silu_done")
        hid_done = sem("hid_done")
        dn_mm = sem("dn_mm")
        y_done = sem("y_done")
        y_out9 = [sem(f"y_out9_{s}") for s in range(2)]
        gathered = [sem(f"gathered{j}") for j, _ in TILES]
        g_first = sem("g_first")
        g_sum = sem("g_sum")
        x3_done = sem("x3_done")
        xs_v = xs_dram[0:NSLOT].rearrange("(e s) d -> e s d", s=2 * BLK)
        ys_v = ys_dram.rearrange("(e s) d -> e s d", s=BLK)
        ROUNDS_MAX = (T + BLK - 1) // BLK

        def experts(eng, before_loop, expert, after_loop):
            n = eng.value_load(n_rounds[0:1, 0:1].bitcast(I32), min_val=1, max_val=ROUNDS_MAX)
            with eng.Fori(0, n) as r:
                before_loop(r)
                with eng.Fori(0, NE // 4) as i:
                    for u in range(4):
                        expert(r, 4 * i + u, u, r * NE + 4 * i + u, 2 * i + u // 2, r * (NE // 4) + i)
                after_loop(r)

        def nothing(r):
            pass

        with nc.Block() as block:
            @block.sync
            def _(sp):
                for s in range(2):
                    sp.dma_start(gt2_b[:, s, :], mod_dram[s, 5 * D:6 * D].partition_broadcast(P)).then_inc(gt2_in, 16)

                def load_rows(pair, b):
                    sp.dma_start(x_blk[b], xs_v[ds(pair, 1)].rearrange("e s d -> (e s) d")).then_inc(x_in9[b], 16)

                def after_expert(r, quad, u):
                    n = r * NE + 4 * quad + u
                    sp.wait_ge(gu_mm, n + 1)
                    load_gate_up(sp, 4 * quad + (u + 2), u % 2)
                    if u % 2 == 0:
                        load_rows(2 * quad + (u // 2 + 1), 1 - u // 2)
                    sp.wait_ge(dn_mm, n + 3)
                    load_down(sp, 4 * quad + (u + 2), u % 2)

                def a_round(r):
                    sp.wait_ge(scattered, r * 160 + 160)
                    load_rows(0, 0)
                    with sp.Fori(0, NE // 4 - 1) as i:
                        for u in range(4):
                            after_expert(r, i, u)
                    for u in range(2):
                        after_expert(r, NE // 4 - 1, u)
                a_round(0)
                more = sp.value_load(n_rounds[0:1, 1:2].bitcast(I32), min_val=0, max_val=ROUNDS_MAX - 1)
                with sp.If(more > 0):
                    with sp.Fori(0, more) as r:
                        sp.wait_ge(x3_done, r * 5 + 6)
                        for u in range(2):
                            sp.wait_ge(dn_mm, r * NE + (NE + 1 + u))
                            load_gate_up(sp, u, u)
                            load_down(sp, u, u)
                        a_round(r + 1)

            @block.gpsimd
            def _(pool):
                def scatter(r):
                    pool.wait_ge(slots_done, r * 6 + 6)
                    pool.sem_inc(pool_go, 1)
                    for j, n in TILES:
                        for k in range(2):
                            pool.indirect_dma_start(
                                xs_dram, bass.IndirectOffsetOnAxis(ap=as_u32(slot_i[k][0:n, j:j + 1]), axis=0),
                                h2[0:n, j, :], None).then_inc(scattered, 16)

                def gather(r):
                    for s in range(2):
                        pool.wait_ge(y_out9[s], r * (NE * 16) + (NE * 16 + 32))
                        pool.sem_inc(pool_go, 1)
                    for j, n in TILES:
                        for k in range(2):
                            pool.indirect_dma_start(
                                gath[j][0:n, k, :], None, ys_dram,
                                bass.IndirectOffsetOnAxis(ap=as_u32(slot_g[k][0:n, j:j + 1]), axis=0)
                                ).then_inc(gathered[j], 16)
                n = pool.value_load(n_rounds[0:1, 0:1].bitcast(I32), min_val=1, max_val=ROUNDS_MAX)
                with pool.Fori(0, n) as r:
                    scatter(r)
                    gather(r)

            @block.tensor
            def _(pe):
                pe.sem_inc(dn_mm, 2)

                def expert(r, e, u, n, pair, pair_use):
                    s = u % 2
                    if s == 0:
                        pe.wait_ge(x_in9[u // 2], 16 * pair_use + 16)
                        for h in range(2):
                            for k in range(4):
                                m = nc.tensor.transpose(psum[h][:, 0, k * P:(k + 1) * P],
                                                        x_blk[u // 2][:, (4 * h + k) * P:(4 * h + k + 1) * P], ident)
                            m.then_inc(x_tr9, 1)
                        pe.wait_ge(x_t9, n + 2)
                    pe.wait_ge(wg_in[s], 32 * (2 * pair_use + u // 2) + 32)
                    for k in range(KD):
                        for b in range(2):
                            m = nc.tensor.matmul(psum[s][64 * b:64 * b + 64, 1, :], x_t[u // 2][:, k, s * BLK:(s + 1) * BLK],
                                                 w_gu[s][:, b, k, :], start=k == 0, stop=k == KD - 1)
                    m.then_inc(gu_mm, 1)
                    pe.wait_ge(gu_out, n + 1)
                    for f in range(4):
                        m = nc.tensor.transpose(psum[2 + s][:, 0, f * P:(f + 1) * P], gu[:, f * P:(f + 1) * P], ident)
                    m.then_inc(gu_tr, 1)
                    pe.wait_ge(hid_done, n + 1)
                    pe.wait_ge(wd_in[s], 16 * (2 * pair_use + u // 2) + 16)
                    pe.wait_ge(y_done, n + 1)
                    for f in range(4):
                        for b in range(2):
                            m = nc.tensor.matmul(psum[2 + s][64 * b:64 * b + 64, 1, :], hid[:, f, :],
                                                 w_dn[s][:, f, b * 512:(b + 1) * 512], start=f == 0, stop=f == 3)
                    m.then_inc(dn_mm, 1)
                experts(pe, nothing, expert, nothing)

            @block.scalar
            def _(act):
                for s in range(2):
                    act.sem_inc(y_out9[s], 32)

                def expert(r, e, u, n, pair, pair_use):
                    s = u % 2
                    if s == 0:
                        for h in range(2):
                            act.wait_ge(x_tr9, n + (h + 1))
                            nc.scalar.activation(x_t[u // 2][:, 4 * h:4 * h + 4, :].rearrange("p k t -> p (k t)"),
                                                 psum[h][:, 0, :], ACT.Copy).then_inc(x_t9, 1)
                    act.wait_ge(gu_tr, n + 1)
                    nc.scalar.activation(act_g, psum[2 + s][:, 0, :].rearrange("p (f t) -> p f t", f=4)[:, :, 0:BLK],
                                         ACT.Silu).then_inc(silu_done, 1)
                    act.wait_ge(y_done, n + 3)
                    for b in range(2):
                        act.dma_start(ys_v[ds(e, 1), :, b * 512:(b + 1) * 512].rearrange("e s d -> (e s) d"),
                                      y_blk[s][64 * b:64 * b + 64, :]).then_inc(y_out9[s], 16)

                def weigh(r):
                    for j, n in TILES:
                        g = gath[j][0:n, 0, :]
                        act.wait_ge(gathered[j], r * 32 + 32)
                        act.wait_ge(w_done, r * 4 + 4)
                        nc.scalar.activation(g, g, ACT.Copy, scale=wgt_r[0][0:n, j:j + 1]).then_inc(g_first, 1)
                experts(act, nothing, expert, weigh)

            @block.vector
            def _(v):
                v.sem_inc(y_done, 2)
                v.sem_inc(x3_done, 1)
                def slots(r):
                    ve = nc.vector
                    for k in range(2):
                        ve.tensor_scalar(tmp_i, pos[k], 0.0, None, ALU.is_ge).then_inc(slot_step, 1)
                        ve.tensor_scalar(in_r[k], pos[k], float(BLK), None, ALU.is_lt).then_inc(slot_step, 1)
                        v.wait_ge(slot_step, r * 14 + (7 * k + 2))
                        ve.tensor_tensor(in_r[k], in_r[k], tmp_i, ALU.mult).then_inc(slot_step, 1)
                        ve.scalar_tensor_tensor(out=wgt_r[k], in0=eid[k], scalar=float(BLK), in1=pos[k],
                                                op0=ALU.mult, op1=ALU.add).then_inc(slot_step, 1)
                        v.wait_ge(slot_step, r * 14 + (7 * k + 4))
                        ve.tensor_tensor(tmp_i, wgt_r[k], in_r[k], ALU.mult).then_inc(slot_step, 1)
                        ve.tensor_tensor(wgt_r[k], wgt_r[k], trash[k], ALU.subtract).then_inc(slot_step, 1)
                        v.wait_ge(slot_step, r * 14 + (7 * k + 6))
                        ve.tensor_copy(as_u32(slot_g[k]), tmp_i).then_inc(slots_done, 1)
                        ve.tensor_tensor(wgt_r[k], wgt_r[k], in_r[k], ALU.mult).then_inc(slot_step, 1)
                        v.wait_ge(slot_step, r * 14 + (7 * k + 7))
                        ve.tensor_tensor(wgt_r[k], wgt_r[k], trash[k], ALU.add).then_inc(slots_done, 1)
                        v.wait_ge(slots_done, r * 6 + (3 * k + 2))
                        ve.tensor_copy(as_u32(slot_i[k]), wgt_r[k]).then_inc(slots_done, 1)
                        v.wait_ge(slots_done, r * 6 + (3 * k + 3))
                        ve.tensor_tensor(wgt_r[k], wgt[k], in_r[k], ALU.mult).then_inc(w_done, 1)
                        ve.tensor_scalar(pos[k], pos[k], -float(BLK), None, ALU.add).then_inc(w_done, 1)

                def expert(r, e, u, n, pair, pair_use):
                    s = u % 2
                    v.wait_ge(gu_mm, n + 1)
                    nc.vector.tensor_copy(gu, psum[s][:, 1, :]).then_inc(gu_out, 1)
                    v.wait_ge(silu_done, n + 1)
                    nc.vector.tensor_tensor(hid, act_g, psum[2 + s][:, 0, :].rearrange("p (f t) -> p f t", f=4
                                                                                       )[:, :, BLK:2 * BLK], ALU.mult
                                            ).then_inc(hid_done, 1)
                    v.wait_ge(dn_mm, n + 3)
                    v.wait_ge(y_out9[s], 32 * (2 * pair_use + u // 2) + 32)
                    nc.vector.tensor_copy(y_blk[s], psum[2 + s][:, 1, :]).then_inc(y_done, 1)

                def add(r):
                    ve = nc.vector
                    for j, n in TILES:
                        g = gath[j]
                        v.wait_ge(gathered[j], r * 32 + 32)
                        if j == 0:
                            v.wait_ge(w_done, r * 4 + 4)
                            v.wait_ge(gt2_in, 32)
                        v.wait_ge(g_first, r * 5 + (j + 1))
                        ve.scalar_tensor_tensor(out=g[0:n, 0, :], in0=g[0:n, 1, :], scalar=wgt_r[1][0:n, j:j + 1],
                                                in1=g[0:n, 0, :], op0=ALU.mult, op1=ALU.add).then_inc(g_sum, 1)
                        v.wait_ge(g_sum, r * 10 + (2 * j + 1))
                        ve.tensor_tensor(g[0:n, 0, :], g[0:n, 0, :], gt2_b[0:n, 1 if j == 4 else 0, :], ALU.mult
                                         ).then_inc(g_sum, 1)
                        v.wait_ge(g_sum, r * 10 + (2 * j + 2))
                        v.wait_ge(x3_done, r * 5 + (j + 1))
                        ve.tensor_tensor(x2[0:n, j, :], x2[0:n, j, :], g[0:n, 0, :], ALU.add).then_inc(x3_done, 1)
                experts(v, slots, expert, add)

        S10 = Region(moe_at)
        fin_g = S10.take(D)
        fin_junk = S10.take(D)
        fg_in = sem("fg_in")
        f_sq = sem("f_sq")
        f_ms = sem("f_ms")
        f_std = sem("f_std")
        f_rs = sem("f_rs")
        f_done = sem("f_done")
        y_final = sem("y_final")
        with nc.Block() as block:
            @block.sync
            def _(sp):
                sp.dma_start(fin_g, I["final_norm_g"].partition_broadcast(P)).then_inc(fg_in, 16)
                for j, n in TILES:
                    sp.wait_ge(f_done, j + 1)
                    dst = O[0][0, j * P:(j + 1) * P, :] if j < 4 else O[1][0]
                    sp.dma_start(dst, x2[0:n, j, :]).then_inc(y_final, 16)
                sp.wait_ge(y_final, 80)

            @block.scalar
            def _(act):
                for j, n in TILES:
                    if j:
                        act.wait_ge(f_sq, j)
                    nc.scalar.activation(fin_junk[0:n], x2[0:n, j, :], ACT.Square, accum_out=sums2[0:n, j:j + 1]
                                         ).then_inc(f_sq, 1)
                act.wait_ge(f_ms, 2)
                for b, c in ((slice(0, P), slice(0, 4)), (slice(0, DEC), slice(4, 5))):
                    nc.scalar.activation(sums2[b, c], sums2[b, c], ACT.Sqrt).then_inc(f_std, 1)

            @block.vector
            def _(v):
                v.wait_ge(f_sq, 5)
                parts2 = ((slice(0, P), slice(0, 4)), (slice(0, DEC), slice(4, 5)))
                for b, c in parts2:
                    nc.vector.tensor_scalar(sums2[b, c], sums2[b, c], 1.0 / D, EPS, ALU.mult, ALU.add
                                            ).then_inc(f_ms, 1)
                v.wait_ge(f_std, 2)
                for b, c in parts2:
                    nc.vector.reciprocal(sums2[b, c], sums2[b, c]).then_inc(f_rs, 1)
                v.wait_ge(f_rs, 2)
                v.wait_ge(fg_in, 16)
                for j, n in TILES:
                    nc.vector.scalar_tensor_tensor(out=x2[0:n, j, :], in0=x2[0:n, j, :], scalar=sums2[0:n, j:j + 1],
                                                   in1=fin_g[0:n], op0=ALU.mult, op1=ALU.mult).then_inc(f_done, 1)


_OUTS = [(1, 512, 1024), (1, 32, 1024), (1, 1, 1, 3328), (1, 1, 16, 64, 64), (1, 1, 4, 128, 256),
         (1, 1, 1, 3328), (1, 1, 16, 64, 64), (1, 1, 4, 128, 256)]


def kernel(**inputs):
    import numpy as np
    import concourse.bacc as bacc
    from concourse.bass_utils import run_bass_kernel_spmd

    nc = bacc.Bacc("TRN2", target_bir_lowering=False, num_devices=1)
    arrays, ins, outs = {}, {}, []
    for name, a in inputs.items():
        a = np.ascontiguousarray(a)
        arrays[f"in_{name}"] = a
        ins[name] = nc.dram_tensor(f"in_{name}", a.shape, mybir.dt.from_np(a.dtype), kind="ExternalInput").ap()
    for i, shape in enumerate(_OUTS):
        outs.append(nc.dram_tensor(f"out_{i}", shape, F32, kind="ExternalOutput").ap())
    build(nc, ins, outs)
    r = run_bass_kernel_spmd(nc, [arrays], core_ids=[0])
    return tuple(r.results[0][f"out_{i}"] for i in range(len(_OUTS)))
```
